# Optimizing a Trainium2 kernel written in Bass

```python
import jax, jax.numpy as jnp
from jax import lax
import numpy as np

D_MODEL = 1024
BATCH = 1
SEQ = 512
DEPTH = 1

N_ATT_HEADS = 8
HEAD_DIM = 64
ATT_WIDTH = N_ATT_HEADS * HEAD_DIM
Q_BLOCK = 128
CONV_WIDTH = 512
CONV_K = 3
N_GROUPS = 4
EXPERTS_PER_GROUP = 4
N_EXPERTS = N_GROUPS * EXPERTS_PER_GROUP
TOP_K_IN_GROUP = 2
D_EXPERT = 256
PLE_DIM = 256
EPS = 1e-6
NEG_INF = -1e30

PROJ_SIZES = (ATT_WIDTH, ATT_WIDTH, ATT_WIDTH, N_ATT_HEADS,
              CONV_WIDTH, CONV_WIDTH, CONV_WIDTH, D_MODEL, D_MODEL)
PROJ_WIDTH = 3 * ATT_WIDTH + N_ATT_HEADS + 3 * CONV_WIDTH + 2 * D_MODEL


def rms_norm(x, g):
    xf = x.astype(jnp.float32)
    y = xf * lax.rsqrt(jnp.mean(xf * xf, axis=-1, keepdims=True) + EPS)
    return (y * g.astype(jnp.float32)).astype(x.dtype)

def split_offsets():
    offs, acc = [], 0
    for s in PROJ_SIZES[:-1]:
        acc += s
        offs.append(acc)
    return offs

def forgetting_attention(q, k, v, log_f):
    b, s, h, d = q.shape
    n_blocks = s // Q_BLOCK
    c = jnp.cumsum(log_f, axis=1).transpose(0, 2, 1)
    qh = q.transpose(0, 2, 1, 3)
    kh = k.transpose(0, 2, 1, 3)
    vh = v.transpose(0, 2, 1, 3)
    q_blocks = jnp.moveaxis(qh.reshape(b, h, n_blocks, Q_BLOCK, d), 2, 0)
    c_blocks = jnp.moveaxis(c.reshape(b, h, n_blocks, Q_BLOCK), 2, 0)
    key_pos = jnp.arange(s)
    scale = HEAD_DIM ** -0.5

    def one_block(args):
        qb, cqb, blk = args
        q_pos = blk * Q_BLOCK + jnp.arange(Q_BLOCK)
        logits = jnp.einsum('bhqd,bhkd->bhqk', qb, kh).astype(jnp.float32) * scale
        logits = logits + (cqb[..., :, None] - c[..., None, :])
        causal = key_pos[None, :] <= q_pos[:, None]
        logits = jnp.where(causal, logits, NEG_INF)
        probs = jax.nn.softmax(logits, axis=-1)
        return jnp.einsum('bhqk,bhkd->bhqd', probs.astype(vh.dtype), vh)

    out = lax.map(one_block, (q_blocks, c_blocks, jnp.arange(n_blocks)))
    out = out.transpose(1, 0, 3, 2, 4).reshape(b, s, h * d)
    return out

def causal_short_conv(u, w):
    s = u.shape[1]
    u_pad = jnp.pad(u, ((0, 0), (CONV_K - 1, 0), (0, 0)))
    y = w[0] * u_pad[:, 0:s]
    for j in range(1, CONV_K):
        y = y + w[j] * u_pad[:, j:j + s]
    return y

def hierarchical_moe(h, w_rg, b_rg, w_re, b_re, w_gate, w_up, w_down):
    b, s, d = h.shape
    ht = h.reshape(b * s, d)
    g_logits = (ht @ w_rg + b_rg).astype(jnp.float32)
    g_prob = jax.nn.softmax(g_logits, axis=-1)
    g_val, g_idx = lax.top_k(g_prob, 1)
    e_logits = (ht @ w_re + b_re).astype(jnp.float32)
    e_logits = e_logits.reshape(-1, N_GROUPS, EXPERTS_PER_GROUP)
    e_in = jnp.take_along_axis(e_logits, g_idx[:, :, None], axis=1)[:, 0]
    e_prob = jax.nn.softmax(e_in, axis=-1)
    e_val, e_idx = lax.top_k(e_prob, TOP_K_IN_GROUP)
    e_val = e_val / jnp.sum(e_val, axis=-1, keepdims=True)
    gate = g_val * e_val
    global_idx = g_idx * EXPERTS_PER_GROUP + e_idx
    combine = jnp.sum(jax.nn.one_hot(global_idx, N_EXPERTS, dtype=jnp.float32)
                      * gate[..., None], axis=1)
    a = jnp.einsum('td,edf->tef', ht, w_gate)
    u = jnp.einsum('td,edf->tef', ht, w_up)
    hid = jax.nn.silu(a) * u * combine[..., None].astype(ht.dtype)
    out = jnp.einsum('tef,efd->td', hid, w_down)
    return out.reshape(b, s, d)

def first_inputs(seed: int = 0) -> dict:
    key = jax.random.key(seed)
    ks = jax.random.split(key, 24)
    L, D = DEPTH, D_MODEL
    f32 = jnp.float32

    def nrm(k, shape, scale):
        return jax.random.normal(k, shape, f32) * scale

    def gain(k, shape):
        return 1.0 + 0.05 * jax.random.normal(k, shape, f32)

    return {
        "x": nrm(ks[0], (BATCH, SEQ, D), 1.0),
        "p": nrm(ks[1], (DEPTH, BATCH, SEQ, PLE_DIM), 1.0),
        "attn_norm_g": gain(ks[2], (L, D)),
        "w_in": nrm(ks[3], (L, D, PROJ_WIDTH), D ** -0.5),
        "b_f": 1.0 + 3.0 * jax.random.uniform(ks[4], (L, N_ATT_HEADS), f32),
        "q_norm_g": gain(ks[5], (L, HEAD_DIM)),
        "k_norm_g": gain(ks[6], (L, HEAD_DIM)),
        "conv_w": nrm(ks[7], (L, CONV_K, CONV_WIDTH), CONV_K ** -0.5),
        "w_out_att": nrm(ks[8], (L, ATT_WIDTH, D), ATT_WIDTH ** -0.5),
        "w_out_conv": nrm(ks[9], (L, CONV_WIDTH, D), CONV_WIDTH ** -0.5),
        "w_o": nrm(ks[10], (L, D, D), D ** -0.5),
        "ffn_norm_g": gain(ks[11], (L, D)),
        "w_rg": nrm(ks[12], (L, D, N_GROUPS), D ** -0.5),
        "b_rg": nrm(ks[13], (L, N_GROUPS), 0.01),
        "w_re": nrm(ks[14], (L, D, N_EXPERTS), D ** -0.5),
        "b_re": nrm(ks[15], (L, N_EXPERTS), 0.01),
        "w_gate": nrm(ks[16], (L, N_EXPERTS, D, D_EXPERT), D ** -0.5),
        "w_up": nrm(ks[17], (L, N_EXPERTS, D, D_EXPERT), D ** -0.5),
        "w_down": nrm(ks[18], (L, N_EXPERTS, D_EXPERT, D), D_EXPERT ** -0.5),
        "ple_norm_g": gain(ks[19], (L, D)),
        "w_pg": nrm(ks[20], (L, D, D), D ** -0.5),
        "w_ple": nrm(ks[21], (L, PLE_DIM, D), PLE_DIM ** -0.5),
    }

def first_block(x, p, attn_norm_g, w_in, b_f, q_norm_g, k_norm_g, conv_w, w_out_att,
              w_out_conv, w_o, ffn_norm_g, w_rg, b_rg, w_re, b_re, w_gate, w_up, w_down,
              ple_norm_g, w_pg, w_ple):
    b, s, _ = x.shape
    offs = split_offsets()
    for i in range(DEPTH):
        h = rms_norm(x, attn_norm_g[i])
        proj = h @ w_in[i]
        q, k, v, f_logit, cb, cc, cu, ga, gb = jnp.split(proj, offs, axis=-1)

        q = rms_norm(q.reshape(b, s, N_ATT_HEADS, HEAD_DIM), q_norm_g[i])
        k = rms_norm(k.reshape(b, s, N_ATT_HEADS, HEAD_DIM), k_norm_g[i])
        v = v.reshape(b, s, N_ATT_HEADS, HEAD_DIM)
        log_f = jax.nn.log_sigmoid(f_logit.astype(jnp.float32) + b_f[i].astype(jnp.float32))
        y_att = forgetting_attention(q, k, v, log_f)

        y_conv = cb * causal_short_conv(cc * cu, conv_w[i])

        merged = (jax.nn.sigmoid(ga) * (y_att @ w_out_att[i])
                  + jax.nn.sigmoid(gb) * (y_conv @ w_out_conv[i]))
        x = x + merged @ w_o[i]

        h2 = rms_norm(x, ffn_norm_g[i])
        x = x + hierarchical_moe(h2, w_rg[i], b_rg[i], w_re[i], b_re[i],
                                 w_gate[i], w_up[i], w_down[i])

        h3 = rms_norm(x, ple_norm_g[i])
        x = x + jax.nn.sigmoid(h3 @ w_pg[i]) * (p[i] @ w_ple[i])
    return x


GRID_W = 64
CTX_LEN = 256
RET_HEADS = 8
RET_QK_DIM = 64
RET_V_DIM = 128
RET_QK_WIDTH = RET_HEADS * RET_QK_DIM
RET_V_WIDTH = RET_HEADS * RET_V_DIM
CHUNK = 128
ROPE_BASE = 10000.0
FOURIER_GROUPS = 4
FOURIER_GROUP_DIM = 128
FOURIER_WIDTH = FOURIER_GROUPS * FOURIER_GROUP_DIM
Q_OFF = 0
K_OFF = Q_OFF + RET_QK_WIDTH
V_OFF = K_OFF + RET_QK_WIDTH
G_OFF = V_OFF + RET_V_WIDTH
F_OFF = G_OFF + RET_V_WIDTH
IN_COLS = F_OFF + FOURIER_WIDTH
N_BRANCHES = 2
FFN_DIM = 2816
CONV_W = 3
N_MOD = 6


def rms_norm_2(x, w):
    x32 = x.astype(jnp.float32)
    y = x32 * lax.rsqrt(jnp.mean(x32 * x32, axis=-1, keepdims=True) + EPS)
    return (y * w.astype(jnp.float32)).astype(x.dtype)

def modulate(h, shift, scale):
    return h * (1 + scale) + shift

def split_heads(t, n_heads):
    b, l, w = t.shape
    return t.reshape(b, l, n_heads, w // n_heads).transpose(0, 2, 1, 3)

def rope_2d(t, row, col):
    n_freq = RET_QK_DIM // 4
    inv = ROPE_BASE ** (-jnp.arange(n_freq, dtype=jnp.float32) / n_freq)
    ang = jnp.concatenate([row[:, None] * inv, col[:, None] * inv], axis=-1)
    cos, sin = jnp.cos(ang), jnp.sin(ang)
    half = RET_QK_DIM // 2
    t1, t2 = t[..., :half], t[..., half:]
    return jnp.concatenate([t1 * cos - t2 * sin, t1 * sin + t2 * cos], axis=-1).astype(t.dtype)

def log_gamma(a):
    return -jnp.exp(a.astype(jnp.float32))

def chunk_retention(q, k, v, a, s0):
    b, h, l, dk = q.shape
    dv = v.shape[-1]
    n = l // CHUNK
    lg = log_gamma(a)
    qc = q.reshape(b, h, n, CHUNK, dk)
    kc = k.reshape(b, h, n, CHUNK, dk)
    vc = v.reshape(b, h, n, CHUNK, dv)
    pos = jnp.arange(CHUNK, dtype=jnp.float32)
    diff = pos[:, None] - pos[None, :]
    intra_decay = jnp.where(diff >= 0, jnp.exp(lg[:, None, None] * jnp.maximum(diff, 0.0)), 0.0)
    scores = jnp.einsum('bhncd,bhnsd->bhncs', qc, kc) * intra_decay[None, :, None]
    intra = jnp.einsum('bhncs,bhnse->bhnce', scores, vc)
    k_dec = kc * jnp.exp(lg[:, None] * (CHUNK - 1 - pos))[None, :, None, :, None]
    kv = jnp.einsum('bhnsd,bhnse->nbhde', k_dec, vc)
    chunk_decay = jnp.exp(lg * CHUNK)[None, :, None, None]

    def step(s, kv_n):
        return chunk_decay * s + kv_n, s

    s_final, s_prev = lax.scan(step, s0.astype(jnp.float32), kv)
    q_dec = qc * jnp.exp(lg[:, None] * (pos + 1))[None, :, None, :, None]
    inter = jnp.einsum('bhncd,nbhde->bhnce', q_dec, s_prev)
    return (intra + inter).reshape(b, h, l, dv), s_final

def retention_state(k, v, a):
    l = k.shape[2]
    lg = log_gamma(a)
    w = jnp.exp(lg[:, None] * (l - 1 - jnp.arange(l, dtype=jnp.float32)))
    return jnp.einsum('bhld,bhle,hl->bhde', k, v, w)

def bidir_retention(q, k, v, a_f, a_b, s_f0, s_b0):
    o_f, s_f = chunk_retention(q, k, v, a_f, s_f0)
    o_b, s_b = chunk_retention(jnp.flip(q, 2), jnp.flip(k, 2), jnp.flip(v, 2), a_b, s_b0)
    return o_f + jnp.flip(o_b, 2), s_f, s_b

def ret_readout(o, g, w_o):
    mu = jnp.mean(o, axis=-1, keepdims=True)
    var = jnp.mean(jnp.square(o - mu), axis=-1, keepdims=True)
    o = (o - mu) * lax.rsqrt(var + EPS)
    b, h, l, dv = o.shape
    o = o.transpose(0, 2, 1, 3).reshape(b, l, h * dv).astype(g.dtype)
    return (o * jax.nn.silu(g)) @ w_o

def fourier_mix(f, w_f):
    b, l, _ = f.shape
    fg = f.reshape(b, l, FOURIER_GROUPS, FOURIER_GROUP_DIM).astype(jnp.float32)
    z = jnp.fft.fft2(fg, axes=(1, 3), norm='ortho').real
    return z.reshape(b, l, FOURIER_WIDTH).astype(f.dtype) @ w_f

def merge_branches(h, ret_d, four_d, w_bg, b_bg, w_out):
    gates = jax.nn.sigmoid(h @ w_bg + b_bg)
    g_r, g_f = jnp.split(gates, N_BRANCHES, axis=-1)
    return (g_r * ret_d + g_f * four_d) @ w_out

def depthwise_conv3(u, w, b):
    up = jnp.pad(u, ((0, 0), (1, 1), (0, 0)))
    return up[:, :-2] * w[0] + up[:, 1:-1] * w[1] + up[:, 2:] * w[2] + b

def conv_ffn(h, w_up, conv_w, conv_b, w_down):
    u = depthwise_conv3(h @ w_up, conv_w, conv_b)
    a, val = jnp.split(u, 2, axis=-1)
    return (jax.nn.gelu(a) * val) @ w_down

def split_proj(p):
    return (p[..., Q_OFF:K_OFF], p[..., K_OFF:V_OFF], p[..., V_OFF:G_OFF],
            p[..., G_OFF:F_OFF], p[..., F_OFF:IN_COLS])

def second_inputs(seed: int = 0) -> dict:
    key = jax.random.key(seed)
    ks = jax.random.split(key, 24)

    def nrm(k, shape, scale):
        return jax.random.normal(k, shape, jnp.float32) * scale

    d = D_MODEL
    base_decay = jnp.log(-jnp.log1p(-(2.0 ** (-5.0 - jnp.arange(RET_HEADS, dtype=jnp.float32)))))
    return {
        "x": nrm(ks[0], (BATCH, SEQ, d), 1.0),
        "c": nrm(ks[1], (BATCH, d), 1.0),
        "ctx": nrm(ks[2], (BATCH, CTX_LEN, d), 1.0),
        "c_ctx": nrm(ks[3], (d,), 1.0),
        "w_mod": nrm(ks[4], (DEPTH, d, N_MOD * d), 0.5 * d ** -0.5),
        "b_mod": nrm(ks[5], (DEPTH, N_MOD * d), 0.01),
        "norm1_w": 1.0 + nrm(ks[6], (DEPTH, d), 0.05),
        "w_in": nrm(ks[7], (DEPTH, d, IN_COLS), d ** -0.5),
        "ret_decay_f": base_decay[None] + nrm(ks[8], (DEPTH, RET_HEADS), 0.1),
        "ret_decay_b": base_decay[None] + nrm(ks[9], (DEPTH, RET_HEADS), 0.1),
        "w_ret_out": nrm(ks[10], (DEPTH, RET_V_WIDTH, d), RET_V_WIDTH ** -0.5),
        "w_four_out": nrm(ks[11], (DEPTH, FOURIER_WIDTH, d), FOURIER_WIDTH ** -0.5),
        "w_branch_gate": nrm(ks[12], (DEPTH, d, N_BRANCHES * d), d ** -0.5),
        "b_branch_gate": nrm(ks[13], (DEPTH, N_BRANCHES * d), 0.01),
        "w_out": nrm(ks[14], (DEPTH, d, d), d ** -0.5),
        "norm2_w": 1.0 + nrm(ks[15], (DEPTH, d), 0.05),
        "w_up": nrm(ks[16], (DEPTH, d, 2 * FFN_DIM), d ** -0.5),
        "conv_w": nrm(ks[17], (DEPTH, CONV_W, 2 * FFN_DIM), CONV_W ** -0.5),
        "conv_b": nrm(ks[18], (DEPTH, 2 * FFN_DIM), 0.01),
        "w_down": nrm(ks[19], (DEPTH, FFN_DIM, d), FFN_DIM ** -0.5),
        "final_norm_w": 1.0 + nrm(ks[20], (d,), 0.05),
    }

def second_block(x, c, ctx, c_ctx, w_mod, b_mod, norm1_w, w_in, ret_decay_f, ret_decay_b,
              w_ret_out, w_four_out, w_branch_gate, b_branch_gate, w_out, norm2_w,
              w_up, conv_w, conv_b, w_down, final_norm_w):
    b, l, _ = x.shape
    rows = l // GRID_W
    row = jnp.repeat(jnp.arange(rows, dtype=jnp.float32), GRID_W)
    col = jnp.tile(jnp.arange(GRID_W, dtype=jnp.float32), rows)
    q_scale = RET_QK_DIM ** -0.5
    silu_c = jax.nn.silu(c)
    silu_cc = jax.nn.silu(c_ctx)
    xc = ctx
    for layer in range(DEPTH):
        last = layer == DEPTH - 1
        wi = w_in[layer]
        a_f, a_b = ret_decay_f[layer], ret_decay_b[layer]
        mod = silu_c @ w_mod[layer] + b_mod[layer]
        sh1, sc1, g1, sh2, sc2, g2 = [m[:, None, :] for m in jnp.split(mod, N_MOD, axis=-1)]
        mc = jnp.split(silu_cc @ w_mod[layer] + b_mod[layer], N_MOD)

        h = modulate(rms_norm_2(x, norm1_w[layer]), sh1, sc1)
        hc = modulate(rms_norm_2(xc, norm1_w[layer]), mc[0], mc[1])

        if last:
            kc = split_heads(hc @ wi[:, K_OFF:V_OFF], RET_HEADS)
            vc = split_heads(hc @ wi[:, V_OFF:G_OFF], RET_HEADS)
            s_f = retention_state(kc, vc, a_f)
            s_b = retention_state(jnp.flip(kc, 2), jnp.flip(vc, 2), a_b)
        else:
            qc, kc, vc, gc, fc = split_proj(hc @ wi)
            qc = split_heads(qc, RET_HEADS) * q_scale
            kc = split_heads(kc, RET_HEADS)
            vc = split_heads(vc, RET_HEADS)
            zeros = jnp.zeros((b, RET_HEADS, RET_QK_DIM, RET_V_DIM), jnp.float32)
            oc, s_f, s_b = bidir_retention(qc, kc, vc, a_f, a_b, zeros, zeros)
            yc = merge_branches(hc, ret_readout(oc, gc, w_ret_out[layer]),
                                fourier_mix(fc, w_four_out[layer]),
                                w_branch_gate[layer], b_branch_gate[layer], w_out[layer])
            xc = xc + mc[2] * yc
            hc2 = modulate(rms_norm_2(xc, norm2_w[layer]), mc[3], mc[4])
            xc = xc + mc[5] * conv_ffn(hc2, w_up[layer], conv_w[layer], conv_b[layer], w_down[layer])

        q, k, v, g, f = split_proj(h @ wi)
        q = rope_2d(split_heads(q, RET_HEADS), row, col) * q_scale
        k = rope_2d(split_heads(k, RET_HEADS), row, col)
        v = split_heads(v, RET_HEADS)
        o, _, _ = bidir_retention(q, k, v, a_f, a_b, s_f, s_b)
        y = merge_branches(h, ret_readout(o, g, w_ret_out[layer]),
                           fourier_mix(f, w_four_out[layer]),
                           w_branch_gate[layer], b_branch_gate[layer], w_out[layer])
        x = x + g1 * y
        h2 = modulate(rms_norm_2(x, norm2_w[layer]), sh2, sc2)
        x = x + g2 * conv_ffn(h2, w_up[layer], conv_w[layer], conv_b[layer], w_down[layer])
    return rms_norm_2(x, final_norm_w)


def setup_inputs(seed=0):
    out = dict(first_inputs(seed))
    for name, value in second_inputs(seed + 1).items():
        if name != "x":
            out[name + "_2"] = value
    return out


def reference(
    x, p, attn_norm_g, w_in, b_f, q_norm_g, k_norm_g, conv_w, w_out_att, w_out_conv, w_o,
    ffn_norm_g, w_rg, b_rg, w_re, b_re, w_gate, w_up, w_down, ple_norm_g, w_pg, w_ple, c_2,
    ctx_2, c_ctx_2, w_mod_2, b_mod_2, norm1_w_2, w_in_2, ret_decay_f_2, ret_decay_b_2,
    w_ret_out_2, w_four_out_2, w_branch_gate_2, b_branch_gate_2, w_out_2, norm2_w_2, w_up_2,
    conv_w_2, conv_b_2, w_down_2, final_norm_w_2,
):
    x = first_block(
        x, p, attn_norm_g, w_in, b_f, q_norm_g, k_norm_g, conv_w, w_out_att, w_out_conv, w_o,
        ffn_norm_g, w_rg, b_rg, w_re, b_re, w_gate, w_up, w_down, ple_norm_g, w_pg, w_ple,
    )
    return second_block(
        x, c_2, ctx_2, c_ctx_2, w_mod_2, b_mod_2, norm1_w_2, w_in_2, ret_decay_f_2,
        ret_decay_b_2, w_ret_out_2, w_four_out_2, w_branch_gate_2, b_branch_gate_2, w_out_2,
        norm2_w_2, w_up_2, conv_w_2, conv_b_2, w_down_2, final_norm_w_2,
    )


_drawn_inputs = setup_inputs


def setup_inputs(seed=0):
    import zlib

    import numpy as np

    out = dict(_drawn_inputs(seed))
    spreads = {}
    factors = {'q_norm_g': 4.123,
     'k_norm_g': 5.447,
     'b_rg': 6.3,
     'b_re': 7.76,
     'ple_norm_g': 6.836,
     'b_mod_2': 6.312,
     'norm1_w_2': 6.115,
     'b_branch_gate_2': 39.984,
     'norm2_w_2': 4.328,
     'conv_b_2': 8.0}
    for name, (base, spread) in spreads.items():
        noise = np.random.default_rng([zlib.crc32(name.encode()), seed]).standard_normal(out[name].shape)
        drawn = base * np.exp(spread * noise) if base else spread * noise
        out[name] = __import__('jax').numpy.asarray(drawn.astype(out[name].dtype))
    for name, factor in factors.items():
        out[name] = (out[name] * factor).astype(out[name].dtype)
    return out
```

```python
from contextlib import ExitStack

import numpy as np

import concourse.bass as bass
from concourse import mybir

F32 = mybir.dt.float32
F32R = mybir.dt.float32r
ALU = mybir.AluOpType
ACT = mybir.ActivationFunctionType
AX = mybir.AxisListType

P = 128
T = 512
D = 1024
KC = D // P
NT = T // P
EPS = 1e-6
NEG_INF = -1e30

HEADS, HEAD_DIM = 8, 64
ATT = HEADS * HEAD_DIM
CONV = 512
CB0 = 3 * ATT + HEADS
CC0, CU0 = CB0 + CONV, CB0 + 2 * CONV
GA0 = CB0 + 3 * CONV
GB0 = GA0 + D
GROUPS, PER_GROUP = 4, 4
EXPERTS = GROUPS * PER_GROUP
ROUTE = GROUPS + EXPERTS
D_EXPERT = 256
PLE = 256

CTX = 256
RET_HEADS, RET_V = 8, 128
RK0, RV0 = 512, 1024
RG0, RF0 = RV0 + RET_HEADS * RET_V, RV0 + 2 * RET_HEADS * RET_V
FFN = 2816
FC = FFN // P
FFN_ROUNDS = (8, 8, 6)
SPAN = 1408
REACH, REACH_C = SPAN - T, T + P

G_FORGET = 0
G_MIX = 1
G_MERGE = G_MIX + 16
G_WO = G_MERGE + 8
G_PLE = G_WO + 4
G_MOE = G_PLE + 1
G_PG = G_MOE + 48
G_RET = G_PG + 4
G_FOUR = G_RET + 16
G_GF = G_FOUR + 2
G_RO = G_GF + 4
G_FO = G_RO + 4
G_WOUT = G_FO + 2
G_FFN = G_WOUT + 4
G_END = G_FFN + sum(FFN_ROUNDS) + 4 * len(FFN_ROUNDS)

R_START, R_WO, R_MOE, R_PG, R_WOUT, R_FFN = 0, 1, 2, 6, 7, 8
N_ATT, N_MOE, N_PLE, N_RET, N_FFN, N_OUT = range(6)
ROUND_OF = (R_START, R_WO, R_MOE + 3, R_PG, R_WOUT, R_FFN + 2)

V_ATT_G, V_CONV, V_FFN_G, V_PLE_G, V_N1, V_N2, V_FIN = 0, 8, 20, 28, 36, 44, 52
V_C, V_CC, V_BG, V_QG, V_KG = 60, 68, 76, 92, 93
V_CONV2, V_CONVB, V_BMOD = 128, 128 + 3 * 2 * FC, 128 + 4 * 2 * FC
V_ROWS = (94, 128, 4 * 2 * FC + 48 - 128)
V_COLS = 256 + V_ROWS[2]


def shape_constants():
    ident = np.eye(P, dtype=np.float32)
    blocks = np.kron(np.eye(2, dtype=np.float32), np.ones((64, 64), np.float32))
    turn = np.zeros((P, P), np.float32)
    for h in range(2):
        for d in range(32):
            turn[64 * h + 32 + d, 64 * h + d] = -1.0
            turn[64 * h + d, 64 * h + 32 + d] = 1.0
    t = np.arange(T)
    inv = (np.float32(10000.0) ** (-np.arange(16, dtype=np.float32) / np.float32(16))).astype(np.float32)
    row, col = (t // 64).astype(np.float32), (t % 64).astype(np.float32)
    ang = np.concatenate([row[:, None] * inv, col[:, None] * inv], axis=-1)
    cos, sin = (np.tile(f(ang).astype(np.float32).T, (4, 1)) for f in (np.cos, np.sin))
    j = np.arange(P)
    a = 2 * np.pi * np.outer(j, j) / P
    dft_d = np.concatenate([np.cos(a), -np.sin(a)], axis=1).astype(np.float32) / np.float32(256)
    a = 2 * np.pi * (np.outer(t, t) % T) / T
    dft_l = np.stack([np.cos(a), np.sin(a)]).astype(np.float32)
    dist = (np.arange(SPAN)[None, :] - 640 - np.arange(P)[:, None]).astype(np.float32)
    return {
        "small": np.concatenate([ident, blocks, turn], axis=1),
        "rope": np.stack([cos, sin], axis=1).reshape(P, 2 * T),
        "dft_d": dft_d,
        "dft_l": dft_l,
        "dist": dist,
    }


def nothing():
    pass


def build(nc, a, const, out):
    scratch_c = nc.dram_tensor("scratch_c", [HEADS, T], F32, kind="Internal").ap()
    scratch_comb = nc.dram_tensor("scratch_comb", [EXPERTS, T], F32, kind="Internal").ap()
    scratch_x = nc.dram_tensor("scratch_x", [P, KC * T], F32, kind="Internal").ap()

    root = ExitStack()
    with root:
        def buffers(stack):
            def sb(name, shape, dt=F32):
                return stack.enter_context(nc.sbuf_tensor(name, shape, dt))
            return sb

        def semaphores(*names):
            return {n: root.enter_context(nc.semaphore(n)) for n in names}

        sb = buffers(root)
        raw = [sb(f"raw{j}", [P, 16, P]) for j in range(2)]
        w_hi = [sb(f"w_hi{j}", [P, 16, P], F32R) for j in range(2)]
        w_lo = [sb(f"w_lo{j}", [P, 16, P], F32R) for j in range(2)]
        h_hi = sb("h_hi", [P, KC, T], F32R)
        h_lo = sb("h_lo", [P, KC, T], F32R)
        small = sb("small", [P, 3, P])
        ident, head_blocks, turn = small[:, 0, :], small[:, 1, :], small[:, 2, :]
        ones = sb("ones", [P, P])
        vec = sb("vec", [P, V_COLS])
        mod = sb("mod", [P, 48, 2])
        silu_c = sb("silu_c", [P, KC, 2])
        gain = sb("gain", [P, 3, KC])
        sq = sb("sq", [P, 2, T])
        ss = sb("ss", [P, T])
        rstd = sb("rstd", [P, T])
        pre = sb("pre", [P, 2, T])
        bias_f = sb("bias_f", [HEADS, 1])
        eps = sb("eps", [P, 1])
        warm = sb("warm", [P, 6])

        with ExitStack() as s:
            sb = buffers(s)
            reach = sb("reach", [P, 2, REACH])
            reach_c = sb("reach_c", [P, 2, REACH_C])
            back = sb("back", [P, REACH])
        with ExitStack() as s:
            fd = buffers(s)("fd", [P, 4, NT, 2 * P])
        x = buffers(root)("x", [P, KC, T])

        first = ExitStack()
        sb = buffers(first)
        d_hi = sb("d_hi", [P, KC, T], F32R)
        d_lo = sb("d_lo", [P, KC, T], F32R)
        with ExitStack() as s:
            sb = buffers(s)
            x_in = sb("x_in", [P, NT, D])
            v_in = sb("v_in", [P, 3, P])
        with ExitStack() as gates:
            ga = buffers(gates)("ga", [P, KC, T])
            with ExitStack() as s:
                sb = buffers(s)
                c_all = sb("c_all", [P, HEADS, T])
                c_row = sb("c_row", [HEADS, T])
                c_col = sb("c_col", [P, NT, HEADS])
                neg_max = sb("neg_max", [P, NT, 2])
                row_sum = sb("row_sum", [P, NT, 2])
                row_inv = sb("row_inv", [P, NT, 2])
                y_tok = sb("y_tok", [P, P])
                bias_qk = sb("bias_qk", [P, 2, T])
                prob = sb("prob", [P, 2, T])
                prob_t = sb("prob_t", [P, 2, T])
                q_raw = sb("q_raw", [P, T])
                k_raw = sb("k_raw", [P, T])
                v_raw = sb("v_raw", [P, T])
                q_t = sb("q_t", [P, T])
                k_t = sb("k_t", [P, T])
                v_tok = sb("v_tok", [P, NT, P])
                u_pad = sb("u_pad", [P, 2 + T])
                u_zero = u_pad[:, 0:2]
            with ExitStack() as s:
                sb = buffers(s)
                m_hi = sb("m_hi", [P, KC, T], F32R)
                m_lo = sb("m_lo", [P, KC, T], F32R)
                gb = sb("gb", [P, 2, T])
        with ExitStack() as s:
            sb = buffers(s)
            p_in = sb("p_in", [P, NT, PLE])
            p_hi = sb("p_hi", [P, 2, T], F32R)
            p_lo = sb("p_lo", [P, 2, T], F32R)
            wr_raw = sb("wr_raw", [P, KC, P])
        with ExitStack() as s:
            sb = buffers(s)
            ctx_x = sb("ctx_x", [P, KC, CTX])
            ctx_sq = sb("ctx_sq", [P, KC, CTX])
            sig = sb("sig", [P, 2, T])
            ctx_pre = sb("ctx_pre", [P, 2, CTX])
            ctx_r = sb("ctx_r", [P, CTX])
        sb = buffers(first)
        comb_all = sb("comb_all", [P, PER_GROUP, T])
        wm_raw = sb("wm_raw", [P, 2, KC, 2 * P])
        pl = sb("pl", [P, KC, T])
        act_u = sb("act_u", [P, 2, T])
        wm_sum = sb("wm_sum", [P, 2, 2, 2 * P])
        rt_row = sb("rt_row", [ROUTE, T])
        b_route = sb("b_route", [P, ROUTE])
        rt = sb("rt", [P, NT, ROUTE])
        r4 = sb("r4", [P, 8, NT, 4])
        comb = sb("comb", [P, NT, EXPERTS])
        comb_row = sb("comb_row", [EXPERTS, T])
        iota4 = sb("iota4", [P, 4])
        r1 = sb("r1", [P, 8, NT])
        with ExitStack() as s:
            sb = buffers(s)
            wr_hi = sb("wr_hi", [P, KC, P], F32R)
            wr_lo = sb("wr_lo", [P, KC, P], F32R)
        ctx_in = buffers(first)("ctx_in", [P, 2, D])
        first.close()

        second = ExitStack()
        with ExitStack() as s:
            sb = buffers(s)
            hc_hi = sb("hc_hi", [P, KC, CTX], F32R)
            hc_lo = sb("hc_lo", [P, KC, CTX], F32R)
        gf = buffers(second)("gf", [P, KC, T])
        f_t = gf[:, 4:8, :]
        with ExitStack() as s:
            yr_lo = buffers(s)("yr_lo", [P, KC, T], F32R)
        yr = buffers(second)("yr", [P, KC, T])
        gr = buffers(second)("gr", [P, KC, T])
        with ExitStack() as s:
            sb = buffers(s)
            dist = sb("dist", [P, SPAN])
            rope = sb("rope", [P, 2, T])
            kr_raw = sb("kr_raw", [P, T + CTX])
            qr_raw = sb("qr_raw", [P, T])
            vr_raw = sb("vr_raw", [P, T + CTX])
            back_c = sb("back_c", [P, REACH_C])
            qr_t = sb("qr_t", [P, T])
            kr_t = sb("kr_t", [P, T + CTX])
            vr_tok = sb("vr_tok", [P, 2, T + CTX])
            sg = sb("sg", [P, 2, T])
            weighted = sb("weighted", [P, 2, T])
            o_buf = sb("o_buf", [P, T])
            cen = sb("cen", [P, T])
            decay = sb("decay", [P, 2, RET_HEADS])
        with ExitStack() as s:
            with ExitStack() as r:
                yr_hi = buffers(r)("yr_hi", [P, KC, T], F32R)
            sb = buffers(s)
            dft_l = sb("dft_l", [P, 2, NT, T])
            dft_d = sb("dft_d", [P, 2 * P])
            z_gap = sb("z_gap", [P, 768])
            z_hi = sb("z_hi", [P, 4, T], F32R)
            z_lo = sb("z_lo", [P, 4, T], F32R)
        second.close()

        with ExitStack() as s:
            sb = buffers(s)
            d2_hi = sb("d2_hi", [P, KC, T], F32R)
            d2_lo = sb("d2_lo", [P, KC, T], F32R)
            cv = sb("cv", [P, 2, 2, T])

        psum = root.enter_context(nc.psum_tensor("psum", [P, 8, T], F32))

        G = semaphores(
            "raw_in0", "raw_in1",
            "hi_ready", "lo_ready",
            "chunk_done",
            "x_ready",
            "sq_ready", "ss_added",
            "ms_ready",
            "ln_ready", "rstd_ready",
            "pre_ready", "h_hi_ready", "h_lo_ready",
        )
        raw_in = (G["raw_in0"], G["raw_in1"])

        def load_slot(sp, g, j, pieces):
            if not isinstance(g, int) or g >= 2:
                sp.wait_ge(G["lo_ready"], g - 1)
            for t0, n, width, src in pieces:
                dst = raw[j][:, t0:t0 + n, :]
                if width > P:
                    dst = dst.rearrange("p (k a) n -> p k (a n)", a=width // P)
                sp.dma_start(dst, src).then_inc(raw_in[j], 32 // len(pieces))

        def split_hi(act, g, j, tiles=16):
            act.wait_ge(raw_in[j], 16 * (g - j) + 32)
            if not isinstance(g, int) or g >= 2:
                act.wait_ge(G["chunk_done"], 2 * g - 2)
            act.activation(w_hi[j][:, 0:tiles, :], raw[j][:, 0:tiles, :], ACT.Copy).then_inc(G["hi_ready"], 1)

        def split_lo(dve, g, j, tiles=16):
            dve.wait_ge(G["hi_ready"], g + 1)
            dve.tensor_tensor(w_lo[j][:, 0:tiles, :], raw[j][:, 0:tiles, :],
                              w_hi[j][:, 0:tiles, :].bitcast(F32), ALU.subtract).then_inc(G["lo_ready"], 1)

        def halves(w, c0, c1=None):
            cols = [c0] if c1 is None else [c0, c1]
            return [(8 * i, 8, P, w[:, bass.ds(c, P)].rearrange("(k p) n -> p k n", p=P))
                    for i, c in enumerate(cols)]

        def pairs(w, c, t0=0):
            k = w.shape[0] // P
            return [(t0, 2 * k, 2 * P, w[:, bass.ds(c, 2 * P)].rearrange("(k p) n -> p k n", p=P))]

        def of_halves(half, k):
            return 8 * half + k

        def of_pairs(half, k):
            return 2 * k + half

        def product(pe, to, j, tile, hi, lo, k, last, n=T):
            hi_k, lo_k = hi[:, k, 0:n], lo[:, k, 0:n]
            pe.matmul(to, w_hi[j][:, tile, :], hi_k, start=(k == 0), stop=False)
            pe.matmul(to, w_hi[j][:, tile, :], lo_k, start=False, stop=False)
            return pe.matmul(to, w_lo[j][:, tile, :], hi_k, start=False, stop=last)

        def half_slot(pe, j, half, tile_of, bank, chunks=KC):
            for k in range(chunks):
                done = product(pe, psum[:, bank, :], j, tile_of(half, k), h_hi, h_lo, k, k == chunks - 1)
            done.then_inc(G["chunk_done"], 1)

        def whole_slot(pe, g, j, tile_of, hi, lo, chunks=KC, ready=None, count=0):
            pe.wait_ge(G["lo_ready"], g + 1)
            for k in range(chunks):
                if ready is not None:
                    pe.wait_ge(ready, count + k + 1)
                for half in range(2):
                    done = product(pe, psum[:, 2 * j + half, :], j, tile_of(half, k), hi, lo, k,
                                   k == chunks - 1)
                    if k == chunks - 1:
                        done.then_inc(G["chunk_done"], 1)

        def square(act, r, c):
            act.wait_ge(G["x_ready"], 8 * r + c + 1)
            if not isinstance(r, int) or 8 * r + c >= 2:
                act.wait_ge(G["ss_added"], 8 * r + c - 1)
            act.activation(sq[:, c % 2, :], x[:, c, :], ACT.Square).then_inc(G["sq_ready"], 1)

        def add_square(dve, r, c, norms=None):
            dve.wait_ge(G["sq_ready"], 8 * r + c + 1)
            if c == 0:
                if norms:
                    dve.wait_ge(G["ms_ready"], norms)
                dve.tensor_copy(ss[:, :], sq[:, 0, :]).then_inc(G["ss_added"], 1)
            else:
                dve.wait_ge(G["ss_added"], 8 * r + c)
                dve.tensor_tensor(ss[:, :], ss[:, :], sq[:, c % 2, :], ALU.add).then_inc(G["ss_added"], 1)

        def norm_mean(pe, n):
            pe.wait_ge(G["ss_added"], 8 * ROUND_OF[n] + 8)
            if n == 0:
                pe.wait_ge(S["set_up"], 1)
            pe.matmul(psum[:, 7, :], ones[:, :], ss[:, :], start=True, stop=True).then_inc(G["ms_ready"], 1)

        def norm_rstd(act, n):
            act.activation(warm[:, n:n + 1], ones[:, 0:1], ACT.Ln)
            act.wait_ge(G["ms_ready"], n + 1)
            act.activation(rstd[:, :], psum[:, 7, :], ACT.Ln, bias=eps[:, 0:1], scale=1.0 / D)\
               .then_inc(G["ln_ready"], 1)
            act.wait_ge(G["ln_ready"], n + 1)
            act.activation(rstd[:, :], rstd[:, :], ACT.Exp, scale=-0.5).then_inc(G["rstd_ready"], 1)

        def norm_hi(act, n, shift=None, between=None):
            for c in range(KC):
                act.wait_ge(G["pre_ready"], 8 * n + c + 1)
                if shift is None:
                    ins = act.activation(h_hi[:, c, :], pre[:, c % 2, :], ACT.Copy)
                else:
                    ins = act.activation(h_hi[:, c, :], pre[:, c % 2, :], ACT.Identity, bias=shift(c))
                ins.then_inc(G["h_hi_ready"], 1)
                if between:
                    between(c)

        def norm_pre(dve, n, c, g):
            if c >= 2:
                dve.wait_ge(G["h_lo_ready"], 8 * n + c - 1)
            dve.scalar_tensor_tensor(out=pre[:, c % 2, :], in0=x[:, c, :], scalar=g(c), in1=rstd[:, :],
                                     op0=ALU.mult, op1=ALU.mult).then_inc(G["pre_ready"], 1)

        def norm_lo(dve, n, c, shift=None):
            dve.wait_ge(G["h_hi_ready"], 8 * n + c + 1)
            hi = h_hi[:, c, :].bitcast(F32)
            if shift is None:
                ins = dve.tensor_tensor(h_lo[:, c, :], pre[:, c % 2, :], hi, ALU.subtract)
            else:
                ins = dve.scalar_tensor_tensor(out=h_lo[:, c, :], in0=pre[:, c % 2, :], scalar=shift(c),
                                               in1=hi, op0=ALU.add, op1=ALU.subtract)
            ins.then_inc(G["h_lo_ready"], 1)

        def norm_dve(dve, n, g, shift=None):
            dve.wait_ge(G["rstd_ready"], n + 1)
            norm_pre(dve, n, 0, g)
            for c in range(KC):
                if c + 1 < KC:
                    norm_pre(dve, n, c + 1, g)
                norm_lo(dve, n, c, shift)

        S = semaphores("x_in", "v_in", "small_in", "x_turned", "v_copied", "set_up")

        VECTORS = (
            ("attn_norm_g", 0, V_ATT_G, 8), ("conv_w", 0, V_CONV, 12), ("ffn_norm_g", 0, V_FFN_G, 8),
            ("ple_norm_g", 0, V_PLE_G, 8), ("norm1_w_2", 0, V_N1, 8), ("norm2_w_2", 0, V_N2, 8),
            ("final_norm_w_2", 0, V_FIN, 8), ("c_2", 0, V_C, 8), ("c_ctx_2", 0, V_CC, 8),
            ("b_branch_gate_2", 0, V_BG, 16),
        )
        V_DMAS = 16 * (len(VECTORS) + 9)

        def start_sync(sp):
            sp.dma_start(small[:, :, :], const["small"].rearrange("p (a n) -> p a n", a=3))\
              .then_inc(S["small_in"], 16)
            for i in range(NT):
                sp.dma_start(x_in[:, i, :], a["x"][i * P:(i + 1) * P, :]).then_inc(S["x_in"], 16)
            load_slot(sp, G_FORGET, 0, halves(a["w_in"], 3 * ATT))
            load_slot(sp, G_MIX, 1, mix_pieces(0, 0))

        def start_scalar(act):
            n = 0
            for name, at, row, rows in VECTORS:
                act.dma_start(v_in[row:row + rows, 0, :], a[name].rearrange("(r n) -> r n", n=P))\
                   .then_inc(S["v_in"], 16)
                n += 1
            for row, name in ((V_QG, "q_norm_g"), (V_KG, "k_norm_g")):
                for h in range(2):
                    act.dma_start(v_in[row:row + 1, 0, 64 * h:64 * h + 64], a[name].rearrange("(r n) -> r n", r=1))\
                       .then_inc(S["v_in"], 16)
                    n += 1
            w2 = a["conv_w_2"].rearrange("(r n) -> r n", n=P)
            act.dma_start(v_in[:, 1, :], w2[0:P, :]).then_inc(S["v_in"], 16)
            act.dma_start(v_in[0:4, 2, :], w2[P:P + 4, :]).then_inc(S["v_in"], 16)
            act.dma_start(v_in[4:48, 2, :], a["conv_b_2"].rearrange("(r n) -> r n", n=P)).then_inc(S["v_in"], 16)
            act.dma_start(v_in[48:96, 2, :], a["b_mod_2"].rearrange("(r n) -> r n", n=P)).then_inc(S["v_in"], 16)
            act.dma_start(bias_f[:, :], a["b_f"].rearrange("(r n) -> r n", n=1)).then_inc(S["v_in"], 16)
            assert 16 * (n + 5) == V_DMAS
            split_hi(act, G_FORGET, 0, 8)
            for c in range(KC):
                square(act, R_START, c)
            norm_rstd(act, N_ATT)
            norm_hi(act, N_ATT)
            split_hi(act, G_MIX, 1)

        def start_tensor(pe):
            pe.wait_ge(S["small_in"], 16)
            pe.wait_ge(S["x_in"], 16 * NT)
            for c in range(KC):
                for i in range(NT):
                    done = pe.transpose(psum[:, c, i * P:(i + 1) * P], x_in[:, i, c * P:(c + 1) * P], ident)
                done.then_inc(S["x_turned"], 1)
            pe.wait_ge(S["v_in"], V_DMAS)
            pe.wait_ge(G["x_ready"], 1)
            for b, rows in enumerate(V_ROWS):
                done = pe.transpose(psum[:, 0, b * P:b * P + rows], v_in[0:rows, b, :], ident[0:rows, 0:rows])
            done.then_inc(S["x_turned"], 1)
            norm_mean(pe, N_ATT)

        def start_vector(dve):
            dve.memset(eps[:, :], EPS).then_inc(H["t_y"], 1)
            dve.memset(u_zero, 0.0).then_inc(M["m_y_lo"], 1)
            dve.memset(ones[:, :], 1.0).then_inc(S["set_up"], 1)
            for c in range(KC):
                dve.wait_ge(S["x_turned"], c + 1)
                dve.tensor_copy(x[:, c, :], psum[:, c, :]).then_inc(G["x_ready"], 1)
                if c >= 1:
                    add_square(dve, R_START, c - 1)
            dve.wait_ge(S["x_turned"], KC + 1)
            dve.tensor_copy(vec[:, 0:V_ROWS[0]], psum[:, 0, 0:V_ROWS[0]])
            dve.tensor_copy(vec[:, P:V_COLS], psum[:, 0, P:V_COLS]).then_inc(S["v_copied"], 1)
            add_square(dve, R_START, KC - 1)
            split_lo(dve, 0, 0, 8)
            dve.wait_ge(S["v_copied"], 1)
            norm_dve(dve, N_ATT, lambda c: vec[:, V_ATT_G + c:V_ATT_G + c + 1])
            split_lo(dve, G_MIX, 1)

        FG = semaphores("f_bias", "f_chain", "c_row", "c_turned", "c_col", "c_all")

        def forget_sync(sp):
            sp.wait_ge(FG["c_row"], 1)
            sp.dma_start(scratch_c, c_row[:, :]).then_inc(FG["c_all"], 16)
            sp.wait_ge(FG["c_all"], 16)
            sp.dma_start(c_all[:, :, :], scratch_c.rearrange("(o h) t -> o h t", o=1).to_broadcast([P, HEADS, T]))\
              .then_inc(FG["c_all"], 16)

        def forget_tensor(pe):
            pe.wait_ge(G["lo_ready"], 1)
            for k in range(KC):
                pe.wait_ge(G["h_lo_ready"], 8 * N_ATT + k + 1)
                done = product(pe, psum[:, 1, :], 0, k, h_hi, h_lo, k, k == KC - 1)
            done.then_inc(G["chunk_done"], 2)

        def forget_turn(pe):
            pe.wait_ge(FG["c_row"], 1)
            for i in range(NT):
                done = pe.transpose(psum[:, 2, i * HEADS:(i + 1) * HEADS], c_row[:, i * P:(i + 1) * P],
                                    ident[0:HEADS, 0:HEADS])
            done.then_inc(FG["c_turned"], 1)

        f_z, f_abs, f_one = sq[0:HEADS, 0, :], sq[0:HEADS, 1, :], pre[0:HEADS, 1, :]

        def forget_scalar(act):
            act.wait_ge(G["chunk_done"], 2)
            act.wait_ge(G["h_lo_ready"], 8 * N_ATT + 8)
            act.activation(f_z, psum[0:HEADS, 1, :], ACT.Identity, bias=bias_f[:, 0:1]).then_inc(FG["f_bias"], 1)
            act.wait_ge(FG["f_bias"], 1)
            act.activation(f_abs, f_z, ACT.Abs).then_inc(FG["f_bias"], 1)
            act.wait_ge(FG["f_bias"], 2)
            act.activation(f_abs, f_abs, ACT.Exp, scale=-1.0).then_inc(FG["f_bias"], 1)
            act.wait_ge(FG["f_bias"], 3)
            act.activation(f_abs, f_abs, ACT.Ln, bias=1.0).then_inc(FG["f_bias"], 1)

        def forget_vector(dve):
            dve.wait_ge(G["h_lo_ready"], 8)
            dve.memset(f_one, 1.0).then_inc(FG["f_chain"], 1)
            dve.wait_ge(FG["f_bias"], 4)
            dve.scalar_tensor_tensor(out=f_z, in0=f_z, scalar=0.0, in1=f_abs, op0=ALU.min,
                                     op1=ALU.subtract).then_inc(FG["f_chain"], 1)
            dve.wait_ge(FG["f_chain"], 2)
            dve.tensor_tensor_scan(c_row[:, :], f_one, f_z, 0.0, ALU.mult, ALU.add).then_inc(FG["c_row"], 1)
            dve.wait_ge(FG["c_turned"], 1)
            dve.tensor_copy(c_col[:, :, :], psum[:, 2, 0:NT * HEADS].rearrange("p (i h) -> p i h", h=HEADS))\
               .then_inc(FG["c_col"], 1)

        M = semaphores("m_v_raw", "m_q_raw", "m_k_raw", "m_cc_raw", "m_ga", "m_u", "m_yc", "m_yc_hi", "m_yc_lo",
                       "m_sq", "m_mean", "m_ln", "m_r", "m_qk", "m_v_turned", "m_v_tok", "m_bias",
                       "m_scores", "m_logits", "m_max", "m_prob", "m_prob_t", "m_prob_copied", "m_inv",
                       "m_y", "m_y_tok", "m_y_turned", "m_y_hi", "m_y_lo", "m_conv")
        S0, S1, PT0, PT1, Y, YT = 2, 3, 4, 5, 6, 7

        def mix_pieces(m, s):
            w = a["w_in"]
            col = lambda c: m * P + c
            if s == 3:
                return pairs(w, m * 2 * P + GA0)
            return halves(w, *((col(2 * ATT), col(0)), (col(ATT), col(CC0)), (col(CU0), col(CB0)))[s])

        def mix_sync(sp):
            forget = [True]

            def pair(m):
                for s in range(4):
                    if isinstance(m, int) and (m, s) == (0, 0):
                        continue
                    load_slot(sp, G_MIX + 4 * m + s, (G_MIX + s) % 2, mix_pieces(m, s))
                    if forget:
                        forget.pop()
                        forget_sync(sp)
            pair(0)
            with sp.Fori(1, 4) as m:
                pair(m)

        def scores(pe, m, u):
            n = (u + 1) * P
            if u == 0:
                pe.wait_ge(M["m_qk"], 2 * m + 2)
            if not (isinstance(m, int) and m == 0 and u == 0):
                pe.wait_ge(M["m_logits"], 4 * m + u)
            for h in range(2):
                r = slice(64 * h, 64 * h + 64)
                done = pe.matmul(psum[:, S0 + h, 0:n], q_t[r, u * P:(u + 1) * P], k_t[r, 0:n],
                                 start=True, stop=True)
            done.then_inc(M["m_scores"], 1)

        def turn_prob(pe, m, u):
            pe.wait_ge(M["m_prob"], 4 * m + u + 1)
            if not (isinstance(m, int) and m == 0 and u == 0):
                pe.wait_ge(M["m_prob_copied"], 4 * m + u)
            for h in range(2):
                for b in range(u + 1):
                    done = pe.transpose(psum[:, PT0 + h, b * P:(b + 1) * P], prob[:, h, b * P:(b + 1) * P], ident)
            done.then_inc(M["m_prob_t"], 1)

        def prob_v(pe, m, u):
            pe.wait_ge(M["m_prob_copied"], 4 * m + u + 1)
            if u == 0:
                pe.wait_ge(M["m_v_tok"], m + 1)
            if not (isinstance(m, int) and m == 0 and u == 0):
                pe.wait_ge(M["m_y_tok"], 4 * m + u)
            for h in range(2):
                for b in range(u + 1):
                    done = pe.matmul(psum[:, Y, 64 * h:64 * h + 64], prob_t[:, h, b * P:(b + 1) * P],
                                     v_tok[:, b, 64 * h:64 * h + 64], start=(b == 0), stop=(b == u))
            done.then_inc(M["m_y"], 1)

        def turn_y(pe, m, u):
            pe.wait_ge(M["m_y_tok"], 4 * m + u + 1)
            pe.wait_ge(M["m_y_lo"], 4 * m + u + 1)
            pe.transpose(psum[:, YT, 0:P], y_tok[:, :], ident).then_inc(M["m_y_turned"], 1)

        def mix_tensor(pe):
            forget_tensor(pe)

            def after(p):
                def t0():
                    turn_y(pe, p, 0)
                    prob_v(pe, p, 1)
                    turn_prob(pe, p, 2)
                    scores(pe, p, 3)

                def t1():
                    turn_y(pe, p, 1)
                    prob_v(pe, p, 2)
                    turn_prob(pe, p, 3)

                def t2():
                    turn_y(pe, p, 2)
                    prob_v(pe, p, 3)

                def t3():
                    turn_y(pe, p, 3)
                return t0, t1, t2, t3

            def pair(m, rest):
                g, j = G_MIX + 4 * m, G_MIX % 2
                rest[0]()
                pe.wait_ge(G["lo_ready"], g + 1)
                if rest[0] is not nothing:
                    pe.wait_ge(M["m_ga"], 2 * m - 1)
                half_slot(pe, j, 0, of_halves, 0)
                rest[1]()
                if rest[0] is nothing:
                    forget_turn(pe)
                else:
                    pe.wait_ge(M["m_ga"], 2 * m)
                half_slot(pe, j, 1, of_halves, 1)
                rest[2]()
                pe.wait_ge(M["m_v_raw"], m + 1)
                if rest[0] is nothing:
                    pe.wait_ge(FG["c_col"], 1)
                for i in range(NT):
                    done = pe.transpose(psum[:, S0, i * P:(i + 1) * P], v_raw[:, i * P:(i + 1) * P], ident)
                done.then_inc(M["m_v_turned"], 1)
                pe.wait_ge(G["lo_ready"], g + 2)
                half_slot(pe, 1 - j, 0, of_halves, 0)
                rest[3]()
                pe.wait_ge(M["m_sq"], 2 * m + 1)
                pe.wait_ge(M["m_v_tok"], m + 1)
                pe.matmul(psum[:, S0, :], head_blocks, sq[:, 0, :], start=True, stop=True).then_inc(M["m_mean"], 1)
                pe.wait_ge(M["m_q_raw"], m + 1)
                half_slot(pe, 1 - j, 1, of_halves, 1)
                pe.wait_ge(M["m_sq"], 2 * m + 2)
                pe.matmul(psum[:, S1, :], head_blocks, sq[:, 1, :], start=True, stop=True).then_inc(M["m_mean"], 1)
                pe.wait_ge(G["lo_ready"], g + 3)
                pe.wait_ge(M["m_k_raw"], m + 1)
                half_slot(pe, j, 0, of_halves, 0)
                scores(pe, m, 0)
                pe.wait_ge(M["m_cc_raw"], m + 1)
                half_slot(pe, j, 1, of_halves, 1)
                turn_prob(pe, m, 0)
                scores(pe, m, 1)
                pe.wait_ge(G["lo_ready"], g + 4)
                pe.wait_ge(M["m_u"], m + 1)
                half_slot(pe, 1 - j, 0, of_pairs, 0)
                prob_v(pe, m, 0)
                turn_prob(pe, m, 1)
                scores(pe, m, 2)
                pe.wait_ge(M["m_yc"], m + 1)
                half_slot(pe, 1 - j, 1, of_pairs, 1)

            pair(0, (nothing,) * 4)
            with pe.Fori(1, 4) as m:
                pair(m, after(m - 1))
            for rest in after(3):
                rest()

        def mix_scalar(act):
            def exps(m, u):
                n = (u + 1) * P
                act.wait_ge(M["m_max"], 4 * m + u + 1)
                for h in range(2):
                    done = act.activation(prob[:, h, 0:n], prob[:, h, 0:n], ACT.Exp, bias=neg_max[:, u, h:h + 1],
                                          accum_out=row_sum[:, u, h:h + 1])
                done.then_inc(M["m_prob"], 1)

            def copy_prob(m, u):
                n = (u + 1) * P
                act.wait_ge(M["m_prob_t"], 4 * m + u + 1)
                if not (isinstance(m, int) and m == 0 and u == 0):
                    act.wait_ge(M["m_y"], 4 * m + u)
                act.activation(prob_t[:, :, 0:n], psum[:, PT0:PT0 + 2, 0:n], ACT.Copy).then_inc(M["m_prob_copied"], 1)

            def y_hi(m, u):
                act.wait_ge(M["m_y_turned"], 4 * m + u + 1)
                act.activation(d_hi[:, bass.ds(m, 1), u * P:(u + 1) * P], psum[:, YT:YT + 1, 0:P], ACT.Copy)\
                   .then_inc(M["m_y_hi"], 1)

            def sig_ga(m, i):
                act.wait_ge(G["chunk_done"], 2 * (G_MIX + 4 * m + 3) + i + 1)
                act.activation(ga[:, bass.ds(2 * m + i, 1), :], psum[:, i:i + 1, :], ACT.Sigmoid).then_inc(M["m_ga"], 1)

            def r_qk(m, i, bank):
                r = (rstd, ss)[i]
                act.wait_ge(M["m_mean"], 2 * m + i + 1)
                act.activation(r[:, :], psum[:, bank, :], ACT.Ln, bias=eps[:, 0:1], scale=1.0 / HEAD_DIM)\
                   .then_inc(M["m_ln"], 1)
                act.wait_ge(M["m_ln"], 2 * m + i + 1)
                act.activation(r[:, :], r[:, :], ACT.Exp, scale=-0.5).then_inc(M["m_r"], 1)

            def after(p):
                def t0():
                    y_hi(p, 0)
                    copy_prob(p, 2)
                    exps(p, 3)

                def t1():
                    y_hi(p, 1)
                    copy_prob(p, 3)

                def t2():
                    y_hi(p, 2)

                def t3():
                    y_hi(p, 3)
                return t0, t1, t2, t3

            def pair(m, rest):
                g, j = G_MIX + 4 * m, G_MIX % 2
                if rest[0] is not nothing:
                    sig_ga(m - 1, 1)
                split_hi(act, g + 1, 1 - j)
                rest[0]()
                act.wait_ge(G["chunk_done"], 2 * g + 1)
                if rest[0] is nothing:
                    act.wait_ge(G["x_ready"], 1)
                act.activation(v_raw[:, :], psum[:, 0, :], ACT.Copy).then_inc(M["m_v_raw"], 1)
                rest[1]()
                act.wait_ge(G["chunk_done"], 2 * g + 2)
                act.activation(q_raw[:, :], psum[:, 1, :], ACT.Copy).then_inc(M["m_q_raw"], 1)
                split_hi(act, g + 2, j)
                if rest[0] is nothing:
                    act.wait_ge(FG["c_row"], 1)
                act.wait_ge(M["m_q_raw"], m + 1)
                act.activation(sq[:, 0, :], q_raw[:, :], ACT.Square).then_inc(M["m_sq"], 1)
                rest[2]()
                act.wait_ge(G["chunk_done"], 2 * g + 3)
                act.activation(k_raw[:, :], psum[:, 0, :], ACT.Copy).then_inc(M["m_k_raw"], 1)
                act.wait_ge(M["m_k_raw"], m + 1)
                act.activation(sq[:, 1, :], k_raw[:, :], ACT.Square).then_inc(M["m_sq"], 1)
                rest[3]()
                r_qk(m, 0, S0)
                act.wait_ge(G["chunk_done"], 2 * g + 4)
                act.wait_ge(M["m_v_turned"], m + 1)
                act.activation(v_raw[:, :], psum[:, 1, :], ACT.Copy).then_inc(M["m_cc_raw"], 1)
                split_hi(act, g + 3, 1 - j)
                r_qk(m, 1, S1)
                exps(m, 0)
                copy_prob(m, 0)
                exps(m, 1)
                split_hi(act, g + 4, j)
                act.wait_ge(M["m_yc"], m + 1)
                act.activation(d_hi[:, bass.ds(4 + m, 1), :], pre[:, 0:1, :], ACT.Copy).then_inc(M["m_yc_hi"], 1)
                copy_prob(m, 1)
                exps(m, 2)
                sig_ga(m, 0)

            pair(0, (nothing,) * 4)
            with act.Fori(1, 4) as m:
                pair(m, after(m - 1))
            sig_ga(3, 1)
            for rest in after(3):
                rest()

        def mix_vector(dve):
            forget_vector(dve)

            def soften(m, u):
                n = (u + 1) * P
                dve.wait_ge(M["m_scores"], 4 * m + u + 1)
                dve.wait_ge(M["m_bias"], 8 * m + 2 * u + 2)
                if not (isinstance(m, int) and m == 0 and u == 0):
                    dve.wait_ge(M["m_prob_t"], 4 * m + u)
                dve.scalar_tensor_tensor(out=prob[:, :, 0:n], in0=psum[:, S0:S0 + 2, 0:n], scalar=HEAD_DIM ** -0.5,
                                         in1=bias_qk[:, :, 0:n], op0=ALU.mult, op1=ALU.add).then_inc(M["m_logits"], 1)
                dve.wait_ge(M["m_logits"], 4 * m + u + 1)
                dve.tensor_reduce(neg_max[:, u, :], prob[:, :, 0:n], AX.X, ALU.max, negate=True).then_inc(M["m_max"], 1)

            def invert(m, u):
                dve.wait_ge(M["m_prob"], 4 * m + u + 1)
                dve.reciprocal(row_inv[:, u, :], row_sum[:, u, :]).then_inc(M["m_inv"], 1)

            def y_norm(m, u):
                dve.wait_ge(M["m_y"], 4 * m + u + 1)
                dve.wait_ge(M["m_inv"], 4 * m + u + 1)
                if not (isinstance(m, int) and m == 0 and u == 0):
                    dve.wait_ge(M["m_y_turned"], 4 * m + u)
                for h in range(2):
                    done = dve.tensor_scalar(y_tok[:, 64 * h:64 * h + 64], psum[:, Y, 64 * h:64 * h + 64],
                                             row_inv[:, u, h:h + 1], None, ALU.mult)
                done.then_inc(M["m_y_tok"], 1)

            def y_lo(m, u):
                dve.wait_ge(M["m_y_hi"], 4 * m + u + 1)
                block = d_hi[:, bass.ds(m, 1), u * P:(u + 1) * P].bitcast(F32)
                dve.tensor_tensor(d_lo[:, bass.ds(m, 1), u * P:(u + 1) * P], psum[:, YT:YT + 1, 0:P], block,
                                  ALU.subtract).then_inc(M["m_y_lo"], 1)

            def after(p):
                def t0():
                    y_lo(p, 0)
                    y_norm(p, 1)
                    soften(p, 3)
                    invert(p, 2)

                def t1():
                    y_lo(p, 1)
                    y_norm(p, 2)
                    invert(p, 3)

                def t2():
                    y_lo(p, 2)
                    y_norm(p, 3)

                def t3():
                    y_lo(p, 3)
                return t0, t1, t2, t3

            def normed(m, i):
                src, dst, r, col = ((q_raw, q_t, rstd, V_QG), (k_raw, k_t, ss, V_KG))[i]
                dve.wait_ge(M["m_r"], 2 * m + i + 1)
                dve.scalar_tensor_tensor(out=dst[:, :], in0=src[:, :], scalar=vec[:, col:col + 1], in1=r[:, :],
                                         op0=ALU.mult, op1=ALU.mult).then_inc(M["m_qk"], 1)

            def pair(m, rest):
                g, j = G_MIX + 4 * m, G_MIX % 2
                split_lo(dve, g + 1, 1 - j)
                rest[0]()
                rest[1]()
                split_lo(dve, g + 2, j)
                rest[2]()
                dve.wait_ge(M["m_v_turned"], m + 1)
                dve.tensor_copy(v_tok[:, :, :], psum[:, S0, :].rearrange("p (i n) -> p i n", n=P))\
                   .then_inc(M["m_v_tok"], 1)
                rest[3]()
                normed(m, 0)
                split_lo(dve, g + 3, 1 - j)
                normed(m, 1)
                dve.wait_ge(G["chunk_done"], 2 * g + 5)
                dve.wait_ge(M["m_cc_raw"], m + 1)
                dve.tensor_tensor(u_pad[:, 2:2 + T], v_raw[:, :], psum[:, 0, :], ALU.mult).then_inc(M["m_u"], 1)
                soften(m, 0)
                dve.wait_ge(M["m_u"], m + 1)
                taps = conv_taps
                dve.tensor_scalar(pre[:, 1, :], u_pad[:, 0:T], taps(m, 0), None, ALU.mult).then_inc(M["m_conv"], 1)
                for i in (1, 2):
                    dve.wait_ge(M["m_conv"], 3 * m + i)
                    dve.scalar_tensor_tensor(out=pre[:, 1, :], in0=u_pad[:, i:i + T], scalar=taps(m, i),
                                             in1=pre[:, 1, :], op0=ALU.mult, op1=ALU.add).then_inc(M["m_conv"], 1)
                soften(m, 1)
                dve.wait_ge(G["chunk_done"], 2 * g + 6)
                dve.wait_ge(M["m_conv"], 3 * m + 3)
                dve.tensor_tensor(pre[:, 0, :], pre[:, 1, :], psum[:, 1, :], ALU.mult).then_inc(M["m_yc"], 1)
                split_lo(dve, g + 4, j)
                invert(m, 0)
                dve.wait_ge(M["m_yc_hi"], m + 1)
                dve.tensor_tensor(d_lo[:, bass.ds(4 + m, 1), :], pre[:, 0:1, :],
                                  d_hi[:, bass.ds(4 + m, 1), :].bitcast(F32), ALU.subtract).then_inc(M["m_yc_lo"], 1)
                y_norm(m, 0)
                soften(m, 2)
                invert(m, 1)

            pair(0, (nothing,) * 4)
            with dve.Fori(1, 4) as m:
                pair(m, after(m - 1))
            for rest in after(3):
                rest()

        def conv_taps(m, i):
            return vec[:, bass.ds(V_CONV + 4 * i + m, 1)]

        def mix_gpsimd(pool):
            pool.wait_ge(FG["c_col"], 1)
            pool.wait_ge(FG["c_all"], 32)

            def pair(m):
                for u in range(NT):
                    n = (u + 1) * P
                    if not (isinstance(m, int) and m == 0 and u == 0):
                        pool.wait_ge(M["m_logits"], 4 * m + u)
                    pool.tensor_tensor(bias_qk[:, :, 0:n],
                                       c_col[:, u, bass.ds(2 * m, 2)].rearrange("p (h o) -> p h o", o=1)
                                       .to_broadcast([P, 2, n]),
                                       c_all[:, bass.ds(2 * m, 2), 0:n], ALU.subtract).then_inc(M["m_bias"], 1)
                    pool.wait_ge(M["m_bias"], 8 * m + 2 * u + 1)
                    pool.affine_select(out=bias_qk[:, :, u * P:n], in_=bias_qk[:, :, u * P:n], compare_op=ALU.is_ge,
                                       fill=NEG_INF, base=0, pattern=[[0, 2], [-1, P]], channel_multiplier=1)\
                        .then_inc(M["m_bias"], 1)

            for m in range(4):
                pair(m)

        MG = semaphores("g_gb", "g_terms", "g_sum", "g_hi", "g_lo")

        def merge_sync(sp):
            with sp.Fori(0, 4) as m:
                load_slot(sp, G_MERGE + 2 * m, G_MERGE % 2, pairs(a["w_in"], m * 2 * P + GB0))
                load_slot(sp, G_MERGE + 2 * m + 1, 1 - G_MERGE % 2,
                          pairs(a["w_out_att"], m * P * 2) + pairs(a["w_out_conv"], m * P * 2, 8))

        def merge_tensor(pe):
            j = G_MERGE % 2

            def step(m, later):
                g = G_MERGE + 2 * m
                pe.wait_ge(G["lo_ready"], g + 1)
                if later:
                    pe.wait_ge(MG["g_gb"], 2 * m)
                else:
                    pe.wait_ge(M["m_ga"], 8)
                for half in range(2):
                    half_slot(pe, j, half, of_pairs, half)
                if later:
                    pe.wait_ge(MG["g_sum"], 2 * m)
                else:
                    pe.wait_ge(M["m_y_lo"], 17)
                    pe.wait_ge(M["m_yc_lo"], 4)
                pe.wait_ge(G["lo_ready"], g + 2)
                for half in range(2):
                    for part in range(2):
                        for k in range(4):
                            t, c = of_pairs(half, 4 * part + k), 4 * part + k
                            to = psum[:, 2 + 2 * part + half, :]
                            pe.matmul(to, w_hi[1 - j][:, t, :], d_hi[:, c, :], start=(k == 0), stop=False)
                            pe.matmul(to, w_hi[1 - j][:, t, :], d_lo[:, c, :], start=False, stop=False)
                            done = pe.matmul(to, w_lo[1 - j][:, t, :], d_hi[:, c, :], start=False, stop=(k == 3))
                    done.then_inc(G["chunk_done"], 1)

            step(0, False)
            with pe.Fori(1, 4) as m:
                step(m, True)

        def merge_scalar(act):
            j = G_MERGE % 2

            def step(m, later):
                g = G_MERGE + 2 * m
                split_hi(act, g + 1, 1 - j)
                for i in range(2):
                    act.wait_ge(G["chunk_done"], 2 * g + i + 1)
                    if later:
                        act.wait_ge(MG["g_lo"], 2 * m + i - 1)
                    act.activation(gb[:, i, :], psum[:, i, :], ACT.Sigmoid).then_inc(MG["g_gb"], 1)
                split_hi(act, g + 2, j)
                for i in range(2):
                    act.wait_ge(MG["g_sum"], 2 * m + i + 1)
                    act.activation(m_hi[:, bass.ds(2 * m + i, 1), :], gb[:, i:i + 1, :], ACT.Copy)\
                       .then_inc(MG["g_hi"], 1)

            step(0, False)
            with act.Fori(1, 4) as m:
                step(m, True)

        def merge_vector(dve):
            j = G_MERGE % 2
            with dve.Fori(0, 4) as m:
                g = G_MERGE + 2 * m
                split_lo(dve, g + 1, 1 - j)
                split_lo(dve, g + 2, j)
                for i in range(2):
                    dve.wait_ge(G["chunk_done"], 2 * g + i + 3)
                    dve.wait_ge(MG["g_gb"], 2 * m + i + 1)
                    dve.tensor_tensor(gb[:, i, :], gb[:, i, :], psum[:, 4 + i, :], ALU.mult).then_inc(MG["g_terms"], 1)
                    dve.tensor_tensor(sq[:, i:i + 1, :], ga[:, bass.ds(2 * m + i, 1), :], psum[:, 2 + i:3 + i, :],
                                      ALU.mult).then_inc(MG["g_terms"], 1)
                    dve.wait_ge(MG["g_terms"], 4 * m + 2 * i + 2)
                    dve.tensor_tensor(gb[:, i, :], gb[:, i, :], sq[:, i, :], ALU.add).then_inc(MG["g_sum"], 1)
                    dve.wait_ge(MG["g_hi"], 2 * m + i + 1)
                    dve.tensor_tensor(m_lo[:, bass.ds(2 * m + i, 1), :], gb[:, i:i + 1, :],
                                      m_hi[:, bass.ds(2 * m + i, 1), :].bitcast(F32), ALU.subtract)\
                       .then_inc(MG["g_lo"], 1)

        def add_tensor(pe, g0, j0, r, hi, lo, chunks, ready, count, free):
            for s in range(4):
                if s >= 2:
                    pe.wait_ge(G["x_ready"], 8 * r + 2 * s - 2)
                else:
                    free(s)
                if s < 3:
                    whole_slot(pe, g0 + s, (j0 + s) % 2, of_pairs, hi, lo, chunks,
                               ready if s == 0 else None, count)
                else:
                    last_slot(pe, g0 + s, (j0 + s) % 2, hi, lo, chunks)

        def last_slot(pe, g, j, hi, lo, chunks=KC):
            pe.wait_ge(G["lo_ready"], g + 1)
            for half in range(2):
                for k in range(chunks):
                    done = product(pe, psum[:, 2 * j + half, :], j, of_pairs(half, k), hi, lo, k, k == chunks - 1)
                done.then_inc(G["chunk_done"], 1)

        def add_scalar(act, g0, j0, r, tiles=(16,) * 4, between={}):
            for s in range(4):
                if tiles[s]:
                    split_hi(act, g0 + s + 1, (j0 + s + 1) % 2, tiles[s])
                if s in between:
                    between[s]()
                for i in range(2):
                    square(act, r, 2 * s + i)

        def add_vector(dve, g0, j0, r, norms, by=None, tiles=(16,) * 4, between={}):
            for s in range(4):
                if tiles[s]:
                    split_lo(dve, g0 + s + 1, (j0 + s + 1) % 2, tiles[s])
                if s in between:
                    between[s]()
                for i in range(2):
                    c = 2 * s + i
                    bank = psum[:, 2 * ((j0 + s) % 2) + i, :]
                    if c == 7:
                        add_square(dve, r, 6, norms)
                    dve.wait_ge(G["chunk_done"], 2 * (g0 + s) + i + 1)
                    if by is None:
                        ins = dve.tensor_tensor(x[:, c, :], x[:, c, :], bank, ALU.add)
                    else:
                        ins = dve.scalar_tensor_tensor(out=x[:, c, :], in0=bank, scalar=by(c), in1=x[:, c, :],
                                                       op0=ALU.mult, op1=ALU.add)
                    ins.then_inc(G["x_ready"], 1)
                for i in range(s // 3, 2):
                    add_square(dve, r, 2 * s + i, norms)

        L = semaphores("p_in", "p_turned", "p_hi", "p_lo", "p_done", "pg_sig", "pg_gated",
                       "p_bank", "ctx_in", "ctx_turned", "ctx_copied", "ctx_sq", "ctx_mean", "ctx_rstd",
                       "ctx_pre", "ctx_hi", "ctx_lo", "gains")

        def wo_sync(sp):
            for s in range(4):
                load_slot(sp, G_WO + s, (G_WO + s) % 2, pairs(a["w_o"], s * 2 * P))
                if s == 0:
                    sp.wait_ge(MG["g_lo"], 8)
                    sp.dma_start(p_in[:, :, :], a["p"].rearrange("(i p) n -> p i n", p=P)).then_inc(L["p_in"], 16)
                    route_load(sp)

        def wo_tensor(pe):
            def free(s):
                if s == 0:
                    pe.wait_ge(MG["g_sum"], 8)
                    return
                pe.wait_ge(L["p_in"], 16)
                for k in range(2):
                    for i in range(NT):
                        done = pe.transpose(psum[:, 4 + k, i * P:(i + 1) * P], p_in[:, i, k * P:(k + 1) * P], ident)
                done.then_inc(L["p_turned"], 1)
            add_tensor(pe, G_WO, G_WO % 2, R_WO, m_hi, m_lo, KC, MG["g_lo"], 0, free)

        def wo_scalar(act):
            def split_p():
                act.wait_ge(L["p_turned"], 1)
                act.activation(p_hi[:, :, :], psum[:, 4:6, :], ACT.Copy).then_inc(L["p_hi"], 1)

            def split_route():
                act.wait_ge(E["e_wr"], 64)
                act.wait_ge(E["e_iota"], 1)
                act.activation(wr_hi[:, :, :], wr_raw[:, :, :], ACT.Copy).then_inc(E["e_wr_hi"], 1)
            add_scalar(act, G_WO, G_WO % 2, R_WO, between={2: split_p, 3: split_route})

        def wo_vector(dve):
            def split_p():
                dve.wait_ge(L["p_hi"], 1)
                dve.tensor_tensor(p_lo[:, :, :], psum[:, 4:6, :], p_hi[:, :, :].bitcast(F32), ALU.subtract)\
                   .then_inc(L["p_lo"], 1)

            def split_route():
                dve.wait_ge(E["e_wr_hi"], 1)
                dve.tensor_tensor(wr_lo[:, :, :], wr_raw[:, :, :], wr_hi[:, :, :].bitcast(F32), ALU.subtract)\
                   .then_inc(E["e_wr_lo"], 1)
            add_vector(dve, G_WO, G_WO % 2, R_WO, N_ATT + 1, between={2: split_p, 3: split_route})

        EMBED_BANKS = (4, 5, 6, 0, 1, 2, 3, 4)

        def embed_sync(sp):
            load_slot(sp, G_PLE, G_PLE % 2, [(0, 16, D, a["w_ple"].rearrange("(k p) n -> p k n", p=P))])

        def embed_tensor(pe):
            for c in range(KC):
                if c == 0:
                    pe.wait_ge(L["p_lo"], 1)
                    pe.wait_ge(G["lo_ready"], G_PLE + 1)
                if c == 3:
                    norm_mean(pe, N_MOE)
                    pe.wait_ge(G["x_ready"], 8 * R_WO + 8)
                if c == 7:
                    pe.wait_ge(L["p_done"], 1)
                for k in range(2):
                    done = product(pe, psum[:, EMBED_BANKS[c], :], G_PLE % 2, 8 * k + c, p_hi, p_lo, k, k == 1)
                done.then_inc(G["chunk_done"], 1) if c in (3, 7) else done.then_inc(L["p_bank"], 1)

        def copy_embedded(act, c):
            act.wait_ge(*((G["chunk_done"], 2 * G_PLE + 1 + c // 4) if c in (3, 7) else (L["p_bank"], c + 1 - c // 4)))
            act.activation(pl[:, c, :], psum[:, EMBED_BANKS[c], :], ACT.Copy).then_inc(L["p_done"], 1)

        def embed_scalar(act):
            split_hi(act, G_MOE, G_MOE % 2)
            norm_rstd(act, N_MOE)
            norm_hi(act, N_MOE, between=lambda c: copy_embedded(act, c))

        def embed_vector(dve):
            split_lo(dve, G_MOE, G_MOE % 2)
            norm_dve(dve, N_MOE, lambda c: vec[:, V_FFN_G + c:V_FFN_G + c + 1])

        E = semaphores("e_wr", "e_wr_hi", "e_wr_lo", "e_iota", "e_logits", "e_rows", "e_turned", "e_chain", "e_shift",
                       "e_exp", "e_comb", "e_comb_in", "e_silu", "e_up", "e_hid", "e_hi", "e_lo", "m2_in", "m2_sum",
                       "m2_ctx", "m2_used", "e_silu_c")
        w_gate = a["w_gate"].rearrange("e d f -> (e d) f")
        w_up = a["w_up"].rearrange("e d f -> (e d) f")
        w_down = a["w_down"].rearrange("e f d -> (e f) d")
        CTX_BLOCKS = 8

        def block_at(q, s):
            if isinstance(q, int):
                return s - 2 if 2 <= s <= 10 else None
            return 5 * q + 4 + s // 2 if s in (1, 3, 5, 7, 9) else None

        def buffer_of(n):
            return n % 2 if isinstance(n, int) else 0

        def has_ctx(n):
            return isinstance(n, int) and n < CTX_BLOCKS

        def route_load(eng):
            for src, c0, n in (("w_rg", 0, GROUPS), ("w_re", GROUPS, EXPERTS)):
                with nc.allow_non_contiguous_dma(reason="a few columns of weights"):
                    eng.dma_start(wr_raw[:, :, c0:c0 + n], a[src].rearrange("(k p) n -> p k n", p=P))\
                       .then_inc(E["e_wr"], 16)
            for src, c0, n in (("b_rg", 0, GROUPS), ("b_re", GROUPS, EXPERTS)):
                eng.dma_start(b_route[:, c0:c0 + n], a[src].rearrange("(o n) -> o n", o=1).to_broadcast([P, n]))\
                   .then_inc(E["e_wr"], 16)

        def moe_sync(sp):
            j0 = G_MOE % 2

            def group(q):
                g = G_MOE + 12 * q
                for s in range(12):
                    if s < 8:
                        rows = bass.ds(q * 4096 + (s // 2) * D, D)
                        cols = slice((s % 2) * P, (s % 2) * P + P)
                        load_slot(sp, g + s, (j0 + s) % 2,
                                  [(8 * i, 8, P, w[rows, cols].rearrange("(k p) n -> p k n", p=P))
                                   for i, w in enumerate((w_gate, w_up))])
                    else:
                        load_slot(sp, g + s, (j0 + s) % 2,
                                  pairs(w_down[bass.ds(q * D, D), :], (s - 8) * 2 * P))
                    if s == (2 if isinstance(q, int) else 0):
                        if isinstance(q, int):
                            sp.wait_ge(E["e_rows"], 2)
                            sp.dma_start(scratch_comb, comb_row[:, :]).then_inc(E["e_comb_in"], 16)
                            sp.wait_ge(E["e_comb_in"], 16)
                        else:
                            sp.wait_ge(E["e_up"], 8 * q)
                        sp.dma_start(comb_all[:, :, :],
                                     scratch_comb[bass.ds(4 * q, 4), :].rearrange("(o e) t -> o e t", o=1)
                                     .to_broadcast([P, 4, T])).then_inc(E["e_comb_in"], 16)
                    n = block_at(q, s)
                    if n is not None:
                        if isinstance(n, int) and n == 0:
                            sp.wait_ge(G["chunk_done"], 2 * G_PLE + 2)
                        elif not isinstance(n, int) or n >= 2:
                            sp.wait_ge(E["m2_sum"], 8 * n - 8 if isinstance(n, int) else 8 * n)
                        sp.dma_start(wm_raw[:, buffer_of(n), :, :], a["w_mod_2"][:, bass.ds(n * 2 * P, 2 * P)]
                                     .rearrange("(k p) n -> p k n", p=P)).then_inc(E["m2_in"], 16)
            group(0)
            sp.dma_start(ctx_in[:, :, :], a["ctx_2"].rearrange("(i p) n -> p i n", p=P)).then_inc(L["ctx_in"], 16)
            with sp.Fori(1, 4) as q:
                group(q)

        def moe_tensor(pe):
            pe.wait_ge(E["e_wr_lo"], 1)
            pe.wait_ge(L["p_done"], 3)
            for k in range(KC):
                pe.wait_ge(G["h_lo_ready"], 8 * N_MOE + k + 1)
                to = psum[:, 6, :]
                pe.matmul(to, wr_hi[:, k, :], h_hi[:, k, :], start=(k == 0), stop=False)
                pe.matmul(to, wr_hi[:, k, :], h_lo[:, k, :], start=False, stop=False)
                done = pe.matmul(to, wr_lo[:, k, :], h_hi[:, k, :], start=False, stop=(k == KC - 1))
            done.then_inc(E["e_logits"], 1)
            j0 = G_MOE % 2

            def turn_logits():
                pe.wait_ge(E["e_rows"], 1)
                for i in range(NT):
                    done = pe.transpose(psum[:, 5, 32 * i:32 * i + ROUTE], rt_row[:, i * P:(i + 1) * P],
                                        ident[0:ROUTE, 0:ROUTE])
                done.then_inc(E["e_turned"], 1)

            def turn_comb():
                pe.wait_ge(E["e_comb"], 1)
                for i in range(NT):
                    done = pe.transpose(psum[0:EXPERTS, 4, i * P:(i + 1) * P], comb[:, i, :], ident)
                done.then_inc(E["e_turned"], 1)

            def sum_block(q, s):
                n = block_at(q, s)
                if n is None:
                    return
                pe.wait_ge(E["m2_sum"], 8 * n + 8)
                for v in range(2 if has_ctx(n) else 1):
                    for half in range(2):
                        done = pe.matmul(psum[:, 6, bass.ds(48 * v + 2 * n + half, 1)],
                                         wm_sum[:, buffer_of(n), v, half * P:(half + 1) * P], ones[:, 0:1], start=True, stop=True)
                done.then_inc(E["m2_used"], 1)

            def group(q):
                g, r = G_MOE + 12 * q, R_MOE + q
                for s in range(8):
                    if s >= 2:
                        pe.wait_ge(E["e_silu"], 8 * q + s - 1)
                        pe.wait_ge(E["e_up"], 8 * q + s - 1)
                    elif not isinstance(q, int):
                        pe.wait_ge(G["x_ready"], 8 * r - 2 + 2 * s)
                    if isinstance(q, int) and s < 2:
                        pe.wait_ge(L["p_done"], 8)
                        pe.wait_ge(G["lo_ready"], g + s + 1)
                        j = (j0 + s) % 2
                        half_slot(pe, j, 0, of_halves, 2 * j)
                        (turn_logits, turn_comb)[s]()
                        half_slot(pe, j, 1, of_halves, 2 * j + 1)
                    else:
                        whole_slot(pe, g + s, (j0 + s) % 2, of_halves, h_hi, h_lo)
                    sum_block(q, s - 1)
                for s in range(4):
                    if s >= 2:
                        pe.wait_ge(G["x_ready"], 8 * r + 2 * s - 2)
                    else:
                        pe.wait_ge(E["e_silu"], 8 * q + 7 + s)
                        pe.wait_ge(E["e_up"], 8 * q + 7 + s)
                    if s < 3:
                        whole_slot(pe, g + 8 + s, (j0 + s) % 2, of_pairs, d_hi, d_lo, KC,
                                   E["e_lo"] if s == 0 else None, 8 * q)
                    else:
                        last_slot(pe, g + 8 + s, (j0 + s) % 2, d_hi, d_lo)
                    sum_block(q, 7 + s)
            group(0)
            with pe.Fori(1, 4) as q:
                group(q)

        def moe_scalar(act):
            j0 = G_MOE % 2
            split_hi(act, G_MOE + 1, (j0 + 1) % 2)
            for n in range(2):
                act.wait_ge(E["e_shift"], n + 1)
                act.activation(r4[:, n, :, :], r4[:, n, :, :], ACT.Exp).then_inc(E["e_exp"], 1)
            for v in range(2):
                act.activation(silu_c[:, :, v:v + 1], vec[:, V_C + 8 * v:V_C + 8 * v + 8]
                               .rearrange("p (k o) -> p k o", o=1), ACT.Silu).then_inc(E["e_silu_c"], 1)
            split_hi(act, G_MOE + 2, j0)

            def group(q):
                g, r = G_MOE + 12 * q, R_MOE + q
                for s in range(8):
                    if s >= 2 or not isinstance(q, int):
                        split_hi(act, g + s + 1, (j0 + s + 1) % 2)
                    act.wait_ge(G["chunk_done"], 2 * (g + s) + 1)
                    act.activation(act_u[:, s % 2, :], psum[:, 2 * ((j0 + s) % 2), :], ACT.Silu)\
                       .then_inc(E["e_silu"], 1)
                    act.wait_ge(E["e_hid"], 8 * q + s + 1)
                    act.activation(d_hi[:, s, :], pre[:, s % 2, :], ACT.Copy).then_inc(E["e_hi"], 1)
                add_scalar(act, g + 8, j0, r)
            group(0)
            with act.Fori(1, 4) as q:
                group(q)

        def moe_vector(dve):
            j0 = G_MOE % 2
            dve.wait_ge(E["e_logits"], 1)
            dve.tensor_copy(rt_row[:, :], psum[0:ROUTE, 6, :]).then_inc(E["e_rows"], 1)
            split_lo(dve, G_MOE + 1, (j0 + 1) % 2)
            route(dve)
            dve.wait_ge(E["e_turned"], 2)
            dve.tensor_copy(comb_row[:, :], psum[0:EXPERTS, 4, :]).then_inc(E["e_rows"], 1)
            split_lo(dve, G_MOE + 2, j0)

            def accumulate(q, s):
                n = block_at(q, s)
                if n is None:
                    return
                dve.wait_ge(E["m2_in"], 16 * n + 16)
                if isinstance(n, int) and n == 0:
                    dve.wait_ge(E["e_silu_c"], 2)
                elif not isinstance(n, int) or n >= 2:
                    dve.wait_ge(E["m2_used"], n - 1 if isinstance(n, int) else n)
                for v in ((1, 0) if has_ctx(n) else (0,)):
                    count = E[("m2_sum", "m2_ctx")[v]]
                    for k in range(KC):
                        w, sum_v, c = wm_raw[:, buffer_of(n), k, :], wm_sum[:, buffer_of(n), v, :], silu_c[:, k, v:v + 1]
                        if k == 0:
                            ins = dve.tensor_scalar(sum_v, w, c, None, ALU.mult)
                        else:
                            dve.wait_ge(count, 8 * n + k)
                            ins = dve.scalar_tensor_tensor(out=sum_v, in0=w, scalar=c, in1=sum_v, op0=ALU.mult,
                                                           op1=ALU.add)
                        ins.then_inc(count, 1)

            def group(q):
                g, r = G_MOE + 12 * q, R_MOE + q
                for s in range(8):
                    if s >= 2 or not isinstance(q, int):
                        split_lo(dve, g + s + 1, (j0 + s + 1) % 2)
                    accumulate(q, s)
                    if s == 0:
                        dve.wait_ge(E["e_comb_in"], 16 * q + 32)
                    dve.wait_ge(G["chunk_done"], 2 * (g + s) + 2)
                    bank = 2 * ((j0 + s) % 2) + 1
                    dve.tensor_tensor(pre[:, s % 2, :], comb_all[:, s // 2, :], psum[:, bank, :],
                                      ALU.mult).then_inc(E["e_up"], 1)
                    dve.wait_ge(E["e_up"], 8 * q + s + 1)
                    dve.wait_ge(E["e_silu"], 8 * q + s + 1)
                    dve.tensor_tensor(pre[:, s % 2, :], pre[:, s % 2, :], act_u[:, s % 2, :], ALU.mult)\
                       .then_inc(E["e_hid"], 1)
                    dve.wait_ge(E["e_hi"], 8 * q + s + 1)
                    dve.tensor_tensor(d_lo[:, s, :], pre[:, s % 2, :], d_hi[:, s, :].bitcast(F32), ALU.subtract)\
                       .then_inc(E["e_lo"], 1)

                add_vector(dve, g + 8, j0, r, N_MOE + 1,
                           between={s: lambda s=s: accumulate(q, 8 + s) for s in range(4)})
            group(0)
            with dve.Fori(1, 4) as q:
                group(q)

        def route(dve):
            n = [0]

            def step(ins):
                n[0] += 1
                ins.then_inc(E["e_chain"], 1)
                dve.wait_ge(E["e_chain"], n[0])

            def wide(v):
                return v.rearrange("p (i o) -> p i o", o=1).to_broadcast([P, NT, 4])

            iota = iota4[:, :].rearrange("p (o n) -> p o n", o=1).to_broadcast([P, NT, 4])
            dve.wait_ge(E["e_turned"], 1)
            dve.wait_ge(E["e_iota"], 5)
            step(dve.tensor_tensor(rt[:, :, :], psum[:, 5, 0:P].rearrange("p (i n) -> p i n", n=32)[:, :, 0:20],
                                   b_route[:, :].rearrange("p (o n) -> p o n", o=1).to_broadcast([P, NT, 20]), ALU.add))

            def first_of(values, peak, mask, at, tmp):
                step(dve.tensor_reduce(peak, values, AX.X, ALU.max))
                step(dve.tensor_tensor(tmp, values, wide(peak), ALU.is_lt))
                step(dve.scalar_tensor_tensor(out=tmp, in0=tmp, scalar=64.0, in1=iota, op0=ALU.mult, op1=ALU.add))
                step(dve.tensor_reduce(at, tmp, AX.X, ALU.min))
                step(dve.tensor_tensor(mask, iota, wide(at), ALU.is_equal))

            g_exp, e_exp, g_mask, mask1, mask2, tmp, e_in = (r4[:, i, :, :] for i in range(7))
            g_max, at, g_sum, e_max, top, e_sum = (r1[:, i, :] for i in range(6))
            first_of(rt[:, :, 0:GROUPS], g_max, g_mask, at, tmp)
            dve.tensor_tensor(g_exp, rt[:, :, 0:GROUPS], wide(g_max), ALU.subtract).then_inc(E["e_shift"], 1)
            for e in range(PER_GROUP):
                of_e = rt[:, :, GROUPS:20].rearrange("p i (g e) -> p i g e", g=GROUPS)[:, :, :, e]
                step(dve.tensor_tensor(tmp, of_e, g_mask, ALU.mult))
                step(dve.tensor_reduce(e_in[:, :, e], tmp, AX.X, ALU.add))
            step(dve.tensor_reduce(e_max, e_in, AX.X, ALU.max))
            dve.tensor_tensor(e_exp, e_in, wide(e_max), ALU.subtract).then_inc(E["e_shift"], 1)
            dve.wait_ge(E["e_exp"], 2)
            step(dve.tensor_reduce(g_sum, g_exp, AX.X, ALU.add))
            first_of(e_exp, top, mask1, at, tmp)
            step(dve.scalar_tensor_tensor(out=e_in, in0=mask1, scalar=-2.0, in1=e_exp, op0=ALU.mult, op1=ALU.add))
            first_of(e_in, top, mask2, at, tmp)
            step(dve.tensor_tensor(mask1, mask1, mask2, ALU.add))
            step(dve.tensor_tensor(e_exp, e_exp, mask1, ALU.mult))
            step(dve.tensor_reduce(e_sum, e_exp, AX.X, ALU.add))
            step(dve.tensor_tensor(e_sum, e_sum, g_sum, ALU.mult))
            step(dve.reciprocal(e_sum, e_sum))
            step(dve.tensor_tensor(e_exp, e_exp, wide(e_sum), ALU.mult))
            for q in range(GROUPS):
                done = dve.tensor_tensor(comb[:, :, 4 * q:4 * q + 4], e_exp, wide(g_mask[:, :, q]), ALU.mult)
            done.then_inc(E["e_comb"], 1)

        def moe_gpsimd(pool):
            pool.wait_ge(MG["g_sum"], 8)
            pool.memset(wr_raw[:, :, ROUTE:P], 0.0).then_inc(E["e_iota"], 1)
            pool.wait_ge(G["chunk_done"], 2 * (G_WO + 3) + 2)
            for i in range(4):
                pool.memset(iota4[:, i:i + 1], float(i)).then_inc(E["e_iota"], 1)

        def ple_sync(sp):
            for s in range(4):
                load_slot(sp, G_PG + s, (G_PG + s) % 2, pairs(a["w_pg"], s * 2 * P))

        def ple_tensor(pe):
            def turn_context(n):
                for k in range(2):
                    for i in range(2):
                        done = pe.transpose(psum[:, 4 + n % 2, (2 * k + i) * P:(2 * k + i + 1) * P],
                                            ctx_in[:, i, (2 * n + k) * P:(2 * n + k + 1) * P], ident)
                done.then_inc(L["ctx_turned"], 1)
            pe.wait_ge(L["ctx_in"], 16)
            for n in range(2):
                turn_context(n)
            norm_mean(pe, N_PLE)
            pe.wait_ge(L["ctx_copied"], 2)
            for n in range(2, 4):
                turn_context(n)
            for s in range(4):
                if s == 1:
                    pe.wait_ge(L["ctx_sq"], 4)
                    pe.wait_ge(L["gains"], 2)
                    for k in range(KC):
                        done = pe.matmul(psum[:, 6, 0:CTX], ones[:, :], ctx_sq[:, k, :], start=(k == 0),
                                         stop=(k == KC - 1))
                    done.then_inc(L["ctx_mean"], 1)
                if s >= 2:
                    pe.wait_ge(L["pg_sig"], 2 * s - 2)
                else:
                    pe.wait_ge(G["x_ready"], 8 * R_PG)
                if s < 3:
                    whole_slot(pe, G_PG + s, (G_PG + s) % 2, of_pairs, h_hi, h_lo, KC,
                               G["h_lo_ready"] if s == 0 else None, 8 * N_PLE)
                else:
                    last_slot(pe, G_PG + s, (G_PG + s) % 2, h_hi, h_lo)

        def ple_scalar(act):
            def context(c):
                n = 2 * (c // 4) + c % 2
                if c % 4 < 2:
                    act.wait_ge(L["ctx_turned"], n + 1)
                    act.activation(ctx_x[:, 2 * n:2 * n + 2, :],
                                   psum[:, 4 + n % 2, :].rearrange("p (k t) -> p k t", t=CTX), ACT.Copy)\
                       .then_inc(L["ctx_copied"], 1)
                else:
                    act.wait_ge(L["ctx_copied"], n + 1)
                    act.activation(ctx_sq[:, 2 * n:2 * n + 2, :], ctx_x[:, 2 * n:2 * n + 2, :], ACT.Square)\
                       .then_inc(L["ctx_sq"], 1)
            norm_rstd(act, N_PLE)
            norm_hi(act, N_PLE, between=context)
            for s in range(4):
                split_hi(act, G_PG + s + 1, (G_PG + s + 1) % 2)
                if s == 2:
                    context_scalar(act)
                for i in range(2):
                    c = 2 * s + i
                    act.wait_ge(G["chunk_done"], 2 * (G_PG + s) + i + 1)
                    if c >= 2:
                        act.wait_ge(G["x_ready"], 8 * R_PG + c - 1)
                    act.activation(sig[:, i, :], psum[:, 2 * ((G_PG + s) % 2) + i, :], ACT.Sigmoid)\
                       .then_inc(L["pg_sig"], 1)
                    if c == 6:
                        square(act, R_PG, 6)
                for i in range(s // 3, 2):
                    square(act, R_PG, 2 * s + i)

        def ple_vector(dve):
            norm_dve(dve, N_PLE, lambda c: vec[:, V_PLE_G + c:V_PLE_G + c + 1])
            dve.wait_ge(E["m2_used"], 24)
            bias = vec[:, V_BMOD:V_BMOD + 48]
            dve.tensor_tensor(mod[:, :, 0], psum[:, 6, 0:48], bias, ALU.add).then_inc(L["gains"], 1)
            dve.tensor_tensor(mod[:, 0:16, 1], psum[:, 6, 48:64], bias[:, 0:16], ALU.add).then_inc(L["gains"], 1)
            dve.wait_ge(L["gains"], 2)
            for n, (v, scale, col) in enumerate(((0, 8, V_N1), (1, 8, V_N1), (0, 32, V_N2))):
                dve.scalar_tensor_tensor(out=gain[:, n, :], in0=mod[:, scale:scale + 8, v], scalar=1.0,
                                         in1=vec[:, col:col + 8], op0=ALU.add, op1=ALU.mult).then_inc(L["gains"], 1)
            for s in range(4):
                split_lo(dve, G_PG + s + 1, (G_PG + s + 1) % 2)
                if s == 2:
                    dve.wait_ge(L["gains"], 5)
                    context_vector(dve)
                for i in range(2):
                    c = 2 * s + i
                    if c == 7:
                        add_square(dve, R_PG, 6, N_PLE + 1)
                    dve.wait_ge(L["pg_sig"], c + 1)
                    dve.wait_ge(L["p_done"], c + 1)
                    dve.tensor_tensor(sig[:, i, :], sig[:, i, :], pl[:, c, :], ALU.mult).then_inc(L["pg_gated"], 1)
                    dve.wait_ge(L["pg_gated"], c + 1)
                    dve.tensor_tensor(x[:, c, :], x[:, c, :], sig[:, i, :], ALU.add).then_inc(G["x_ready"], 1)
                for i in range(s // 3, 2):
                    add_square(dve, R_PG, 2 * s + i, N_PLE + 1)

        def context_scalar(act):
            act.wait_ge(L["ctx_mean"], 1)
            act.activation(ctx_r[:, :], psum[:, 6, 0:CTX], ACT.Ln, bias=eps[:, 0:1], scale=1.0 / D)\
               .then_inc(L["ctx_rstd"], 1)
            act.wait_ge(L["ctx_rstd"], 1)
            act.activation(ctx_r[:, :], ctx_r[:, :], ACT.Exp, scale=-0.5).then_inc(L["ctx_rstd"], 1)
            for c in range(KC):
                act.wait_ge(L["ctx_pre"], c + 1)
                act.activation(hc_hi[:, c, :], ctx_pre[:, c % 2, :], ACT.Identity, bias=mod[:, c, 1:2])\
                   .then_inc(L["ctx_hi"], 1)

        def context_vector(dve):
            def make(c):
                if c >= 2:
                    dve.wait_ge(L["ctx_lo"], c - 1)
                dve.scalar_tensor_tensor(out=ctx_pre[:, c % 2, :], in0=ctx_x[:, c, :], scalar=gain[:, 1, c:c + 1],
                                         in1=ctx_r[:, :], op0=ALU.mult, op1=ALU.mult).then_inc(L["ctx_pre"], 1)
            dve.wait_ge(L["ctx_rstd"], 2)
            make(0)
            for c in range(KC):
                if c + 1 < KC:
                    make(c + 1)
                dve.wait_ge(L["ctx_hi"], c + 1)
                dve.scalar_tensor_tensor(out=hc_lo[:, c, :], in0=ctx_pre[:, c % 2, :], scalar=mod[:, c, 1:2],
                                         in1=hc_hi[:, c, :].bitcast(F32), op0=ALU.add, op1=ALU.subtract)\
                   .then_inc(L["ctx_lo"], 1)

        H = semaphores("t_const", "t_dec", "t_kraw", "t_qraw", "t_vraw", "t_turn", "t_rot", "t_qk", "t_vturned", "t_vtok",
                       "t_expf", "t_sel", "t_reach", "t_scores", "t_dm", "t_pv", "t_o", "t_mean", "t_cen", "t_sq",
                       "t_var", "t_ln", "t_rstd", "t_yn", "t_y", "t_silu", "t_gate", "x_out")
        C, SA, SB, O, X0, X1 = 2, 3, 4, 5, 6, 7

        def ret_pieces(m, s):
            w = a["w_in_2"]
            if s == 0:
                return halves(w, RK0 + m * P, m * P)
            if s == 3:
                return pairs(a["w_branch_gate_2"], m * P * 2)
            return pairs(w, m * 2 * P + (RV0, RG0)[s - 1])

        def ret_sync(sp):
            def pair(m):
                for s in range(4):
                    load_slot(sp, G_RET + 4 * m + s, (G_RET + s) % 2, ret_pieces(m, s))
                    if isinstance(m, int) and s == 1:
                        sp.wait_ge(G["x_ready"], 8 * R_PG + 8)
                        sp.wait_ge(L["ctx_lo"], 8)
                        sp.dma_start(dist[:, :], const["dist"]).then_inc(H["t_const"], 16)
                        sp.dma_start(rope[:, :, :], const["rope"].rearrange("p (a t) -> p a t", a=2))\
                          .then_inc(H["t_const"], 16)
                        for d, name in enumerate(("ret_decay_f_2", "ret_decay_b_2")):
                            sp.dma_start(decay[:, d, :], a[name].rearrange("(o h) -> o h", o=1)
                                         .to_broadcast([P, RET_HEADS])).then_inc(H["t_const"], 16)
                        sp.dma_start(scratch_x, x[:, :, :].rearrange("p k t -> p (k t)")).then_inc(H["x_out"], 16)
            pair(0)
            with sp.Fori(1, 4) as m:
                pair(m)

        def ret_scores(pe, m, n):
            pe.wait_ge(H["t_dm"], 6 * m + n) if n or not isinstance(m, int) else None
            if n == 0:
                pe.wait_ge(H["t_qk"], 2 * m + 2)
                pe.wait_ge(H["t_vtok"], 2 * m + 1)
            r = slice(64 * (n // 3), 64 * (n // 3) + 64)
            for i in range(2):
                b = 2 * (n % 3) + i
                done = pe.matmul(psum[:, SA + i, :], kr_t[r, b * P:(b + 1) * P], qr_t[r, :], start=True, stop=True)
            done.then_inc(H["t_scores"], 1)

        def ret_pv(pe, m, n):
            h = n // 3
            pe.wait_ge(H["t_dm"], 6 * m + n + 1)
            if n % 3 == 0:
                pe.wait_ge(H["t_vtok"], 2 * m + h + 1)
                if h or not isinstance(m, int):
                    pe.wait_ge(H["t_o"], 2 * m + h)
            for i in range(2):
                b = 2 * (n % 3) + i
                done = pe.matmul(psum[:, O, :], vr_tok[:, h, b * P:(b + 1) * P], weighted[:, i, :],
                                 start=(b == 0), stop=(b == 5))
            done.then_inc(H["t_pv"], 1)

        def ret_mean(pe, m, h):
            pe.wait_ge(H["t_o"], 2 * m + h + 1)
            pe.matmul(psum[:, X0, :], ones[:, :], o_buf[:, :], start=True, stop=True).then_inc(H["t_mean"], 1)

        def ret_var(pe, m, h):
            pe.wait_ge(H["t_sq"], 2 * m + h + 1)
            pe.matmul(psum[:, (X1, C)[h], :], ones[:, :], o_buf[:, :], start=True, stop=True).then_inc(H["t_var"], 1)

        def ret_after_tensor(pe, p):
            def t0():
                ret_pv(pe, p, 2)
                ret_scores(pe, p, 3)

            def t1():
                ret_pv(pe, p, 3)
                ret_scores(pe, p, 4)
                ret_mean(pe, p, 0)

            def t2():
                ret_pv(pe, p, 4)
                ret_scores(pe, p, 5)
                ret_var(pe, p, 0)

            def t3():
                ret_pv(pe, p, 5)

            def t4():
                ret_mean(pe, p, 1)

            def t5():
                ret_var(pe, p, 1)
            return t0, t1, t2, t3, t4, t5

        def ret_tensor(pe):
            def context(j, tile_of, half, first=False):
                for k in range(KC):
                    if first:
                        pe.wait_ge(L["ctx_lo"], k + 1)
                    product(pe, psum[:, C, 0:CTX], j, tile_of(half, k), hc_hi, hc_lo, k, k == KC - 1, CTX)

            def turn_v(m, h, banks):
                for b in range(6):
                    done = pe.transpose(psum[:, banks[b // 4], (b % 4) * P:(b % 4 + 1) * P],
                                        vr_raw[:, b * P:(b + 1) * P], ident)
                done.then_inc(H["t_vturned"], 1)

            def pair(m, rest):
                g, j = G_RET + 4 * m, G_RET % 2
                first = rest[0] is nothing
                rest[0]()
                pe.wait_ge(G["lo_ready"], g + 1)
                if first:
                    pe.wait_ge(L["pg_sig"], 8)
                context(j, of_halves, 0, first)
                if first:
                    norm_mean(pe, N_RET)
                    pe.wait_ge(G["x_ready"], 8 * R_PG + 8)
                    assert j == 0
                    whole_slot(pe, g, j, of_halves, h_hi, h_lo, KC, G["h_lo_ready"], 8 * N_RET)
                else:
                    pe.wait_ge(H["t_gate"], 2 * m - 1)
                    half_slot(pe, j, 0, of_halves, 0)
                rest[1]()
                if not first:
                    pe.wait_ge(H["t_gate"], 2 * m)
                    half_slot(pe, j, 1, of_halves, 1)
                rest[2]()
                pe.wait_ge(G["lo_ready"], g + 2)
                pe.wait_ge(H["t_kraw"], m + 1)
                context(1 - j, of_pairs, 0)
                half_slot(pe, 1 - j, 0, of_pairs, 0)
                rest[3]()
                pe.wait_ge(H["t_qraw"], m + 1)
                if not first:
                    pe.wait_ge(H["t_dm"], 6 * m)
                pe.matmul(psum[:, SA, :], turn, kr_raw[:, 0:T], start=True, stop=True)
                pe.matmul(psum[:, SB, :], turn, qr_raw[:, :], start=True, stop=True).then_inc(H["t_turn"], 1)
                pe.wait_ge(H["t_vraw"], 2 * m + 1)
                context(1 - j, of_pairs, 1)
                half_slot(pe, 1 - j, 1, of_pairs, 1)
                rest[4]()
                pe.wait_ge(H["t_qk"], 2 * m + 2)
                turn_v(m, 0, (SA, SB))
                pe.wait_ge(G["lo_ready"], g + 3)
                half_slot(pe, j, 0, of_pairs, 0)
                pe.wait_ge(H["t_vraw"], 2 * m + 2)
                rest[5]()
                if not first:
                    pe.wait_ge(H["t_cen"], 2 * m)
                turn_v(m, 1, (X0, X1))
                ret_scores(pe, m, 0)
                half_slot(pe, j, 1, of_pairs, 1)
                ret_pv(pe, m, 0)
                ret_scores(pe, m, 1)
                pe.wait_ge(G["lo_ready"], g + 4)
                pe.wait_ge(H["t_silu"], 2 * m + 1)
                half_slot(pe, 1 - j, 0, of_pairs, 0)
                ret_pv(pe, m, 1)
                ret_scores(pe, m, 2)
                pe.wait_ge(H["t_silu"], 2 * m + 2)
                half_slot(pe, 1 - j, 1, of_pairs, 1)

            pair(0, (nothing,) * 6)
            with pe.Fori(1, 4) as m:
                pair(m, ret_after_tensor(pe, m - 1))

        def ret_gate(act, m, i):
            act.wait_ge(G["chunk_done"], 2 * (G_RET + 4 * m + 3) + i + 1)
            act.activation(gr[:, bass.ds(2 * m + i, 1), :], psum[:, i:i + 1, :], ACT.Sigmoid,
                           bias=vec[:, bass.ds(V_BG + 2 * m + i, 1)]).then_inc(H["t_gate"], 1)

        def ret_copy_o(act, m, h):
            act.wait_ge(H["t_pv"], 6 * m + 3 * h + 3)
            act.activation(o_buf[:, :], psum[:, O, :], ACT.Copy).then_inc(H["t_o"], 1)

        def ret_square(act, m, h):
            act.wait_ge(H["t_cen"], 2 * m + h + 1)
            act.activation(o_buf[:, :], cen[:, :], ACT.Square).then_inc(H["t_sq"], 1)

        def ret_rstd(act, m, h):
            act.wait_ge(H["t_var"], 2 * m + h + 1)
            act.activation(rstd[:, :], psum[:, (X1, C)[h], :], ACT.Ln, bias=eps[:, 0:1], scale=1.0 / RET_V)\
               .then_inc(H["t_ln"], 1)
            act.wait_ge(H["t_ln"], 2 * m + h + 1)
            act.activation(rstd[:, :], rstd[:, :], ACT.Exp, scale=-0.5).then_inc(H["t_rstd"], 1)

        def ret_after_scalar(act, p):
            return (lambda: ret_copy_o(act, p, 0), lambda: ret_square(act, p, 0), lambda: ret_rstd(act, p, 0),
                    lambda: ret_copy_o(act, p, 1), lambda: ret_square(act, p, 1), lambda: ret_rstd(act, p, 1))

        def ret_scalar(act):
            norm_rstd(act, N_RET)
            norm_hi(act, N_RET, lambda c: mod[:, c, 0:1])
            act.wait_ge(H["t_const"], 64)
            act.activation(decay[:, :, :], decay[:, :, :], ACT.Exp).then_inc(H["t_dec"], 1)

            def reach_of(m, h):
                f = decay[:, 0, bass.ds(2 * m + h, 1)]
                b = decay[:, 1, bass.ds(2 * m + h, 1)]
                if h == 0 and isinstance(m, int):
                    act.wait_ge(H["t_dec"], 2)
                    act.wait_ge(H["x_out"], 16)
                if h == 0 and not isinstance(m, int):
                    act.wait_ge(H["t_dm"], 6 * m)
                act.activation(reach[:, h, :], dist[:, 256:256 + REACH], ACT.Exp, scale=f).then_inc(H["t_expf"], 1)
                act.activation(reach_c[:, h, :], dist[:, 768:768 + REACH_C], ACT.Exp, scale=f).then_inc(H["t_expf"], 1)
                if h or not isinstance(m, int):
                    act.wait_ge(H["t_reach"], 4 * m + 2 * h)
                act.activation(back[:, :], dist[:, 256:256 + REACH], ACT.Exp, scale=b).then_inc(H["t_expf"], 1)
                act.activation(back_c[:, :], dist[:, 0:REACH_C], ACT.Exp, scale=b).then_inc(H["t_expf"], 1)

            def copy_v(m, h):
                g = G_RET + 4 * m + 1
                act.wait_ge(G["chunk_done"], 2 * g + h + 1)
                if h or not isinstance(m, int):
                    act.wait_ge(H["t_vturned"], 2 * m + h)
                act.activation(vr_raw[:, 0:T], psum[:, h, :], ACT.Copy)
                act.activation(vr_raw[:, T:T + CTX], psum[:, C, 0:CTX], ACT.Copy).then_inc(H["t_vraw"], 1)

            def silu_g(m, i):
                act.wait_ge(G["chunk_done"], 2 * (G_RET + 4 * m + 2) + i + 1)
                if not isinstance(m, int):
                    act.wait_ge(H["t_y"], 2 * m + i)
                act.activation(sg[:, i, :], psum[:, i, :], ACT.Silu).then_inc(H["t_silu"], 1)

            def pair(m, rest):
                g, j = G_RET + 4 * m, G_RET % 2
                if rest[0] is not nothing:
                    ret_gate(act, m - 1, 1)
                split_hi(act, g + 1, 1 - j)
                rest[0]()
                act.wait_ge(G["chunk_done"], 2 * g + 1)
                act.activation(kr_raw[:, 0:T], psum[:, 0, :], ACT.Copy)
                act.activation(kr_raw[:, T:T + CTX], psum[:, C, 0:CTX], ACT.Copy).then_inc(H["t_kraw"], 1)
                rest[1]()
                act.wait_ge(G["chunk_done"], 2 * g + 2)
                act.activation(qr_raw[:, :], psum[:, 1, :], ACT.Copy).then_inc(H["t_qraw"], 1)
                split_hi(act, g + 2, j)
                rest[2]()
                copy_v(m, 0)
                rest[3]()
                reach_of(m, 0)
                copy_v(m, 1)
                split_hi(act, g + 3, 1 - j)
                rest[4]()
                reach_of(m, 1)
                rest[5]()
                silu_g(m, 0)
                split_hi(act, g + 4, j)
                silu_g(m, 1)
                ret_gate(act, m, 0)

            pair(0, (nothing,) * 6)
            with act.Fori(1, 4) as m:
                pair(m, ret_after_scalar(act, m - 1))

        def ret_weigh(dve, m, n):
            h = n // 3
            dve.wait_ge(H["t_scores"], 6 * m + n + 1)
            dve.wait_ge(H["t_reach"], 4 * m + 2 * h + (2 if n % 3 == 2 else 1))
            if n or not isinstance(m, int):
                dve.wait_ge(H["t_pv"], 6 * m + n)
            for i in range(2):
                b = 2 * (n % 3) + i
                w = reach[:, h, 384 - P * b:384 - P * b + T] if b < 4 else \
                    reach_c[:, h, P - P * (b - 4):P - P * (b - 4) + T]
                done = dve.tensor_tensor(weighted[:, i, :], w, psum[:, SA + i, :], ALU.mult)
            done.then_inc(H["t_dm"], 1)

        def ret_center(dve, m, h):
            dve.wait_ge(H["t_mean"], 2 * m + h + 1)
            dve.wait_ge(H["t_y"], 2 * m + h + 1)
            dve.scalar_tensor_tensor(out=cen[:, :], in0=psum[:, X0, :], scalar=-1.0 / RET_V, in1=o_buf[:, :],
                                     op0=ALU.mult, op1=ALU.add).then_inc(H["t_cen"], 1)

        def ret_out(dve, m, h):
            dve.wait_ge(H["t_rstd"], 2 * m + h + 1)
            dve.wait_ge(H["t_silu"], 2 * m + h + 1)
            dve.tensor_tensor(cen[:, :], cen[:, :], rstd[:, :], ALU.mult).then_inc(H["t_yn"], 1)
            dve.wait_ge(H["t_yn"], 2 * m + h + 1)
            dve.tensor_tensor(yr[:, bass.ds(2 * m + h, 1), :], cen[:, :].rearrange("p (o t) -> p o t", o=1),
                              sg[:, h:h + 1, :], ALU.mult).then_inc(H["t_y"], 1)

        def ret_after_vector(dve, p):
            def t1():
                ret_weigh(dve, p, 4)
                ret_center(dve, p, 0)

            def t2():
                ret_weigh(dve, p, 5)
                ret_out(dve, p, 0)
            return (lambda: ret_weigh(dve, p, 3), t1, t2, nothing, lambda: ret_center(dve, p, 1),
                    lambda: ret_out(dve, p, 1))

        def ret_vector(dve):
            norm_dve(dve, N_RET, lambda c: gain[:, 0, c:c + 1], lambda c: mod[:, c, 0:1])
            dve.wait_ge(H["t_dec"], 1)
            dve.tensor_scalar(decay[:, 0, :], decay[:, 0, :], -1.0, None, ALU.mult).then_inc(H["t_dec"], 1)
            cos, sin = rope[:, 0, :], rope[:, 1, :]

            def rotate(m, i):
                raw_t, bank, out, scale = ((kr_raw, SA, kr_t, 1.0), (qr_raw, SB, qr_t, HEAD_DIM ** -0.5))[i]
                tmp = pre[:, i, :]
                dve.scalar_tensor_tensor(out=tmp, in0=psum[:, bank, :], scalar=scale, in1=sin, op0=ALU.mult,
                                         op1=ALU.mult).then_inc(H["t_rot"], 1)
                dve.scalar_tensor_tensor(out=out[:, 0:T], in0=raw_t[:, 0:T], scalar=scale, in1=cos, op0=ALU.mult,
                                         op1=ALU.mult).then_inc(H["t_rot"], 1)
                dve.wait_ge(H["t_rot"], 4 * m + 2 * i + 2)
                dve.tensor_tensor(out[:, 0:T], out[:, 0:T], tmp, ALU.add).then_inc(H["t_qk"], 1)

            def pair(m, rest):
                g, j = G_RET + 4 * m, G_RET % 2
                split_lo(dve, g + 1, 1 - j)
                rest[0]()
                rest[1]()
                split_lo(dve, g + 2, j)
                rest[2]()
                dve.wait_ge(H["t_turn"], m + 1)
                if rest[0] is nothing:
                    dve.wait_ge(H["t_const"], 64)
                dve.tensor_copy(kr_t[:, T:T + CTX], kr_raw[:, T:T + CTX])
                for i in range(2):
                    rotate(m, i)
                split_lo(dve, g + 3, 1 - j)
                for h, banks in enumerate(((SA, SB), (X0, X1))):
                    dve.wait_ge(H["t_vturned"], 2 * m + h + 1)
                    dve.tensor_copy(vr_tok[:, h, 0:T], psum[:, banks[0], :])
                    dve.tensor_copy(vr_tok[:, h, T:T + CTX], psum[:, banks[1], 0:CTX]).then_inc(H["t_vtok"], 1)
                    if h == 0:
                        rest[4]()
                ret_weigh(dve, m, 0)
                rest[5]()
                split_lo(dve, g + 4, j)
                ret_weigh(dve, m, 1)
                ret_weigh(dve, m, 2)

            pair(0, (nothing,) * 6)
            with dve.Fori(1, 4) as m:
                pair(m, ret_after_vector(dve, m - 1))

        def ret_gpsimd(pool):
            def head(m, h):
                for n, (table, sign) in enumerate(((reach[:, h, :], 1), (back[:, :], -1))):
                    pool.wait_ge(H["t_expf"], 8 * m + 4 * h + 1 + 2 * n)
                    pool.affine_select(out=table, in_=table, compare_op=ALU.is_ge, fill=0.0, base=-384 * sign,
                                       pattern=[[sign, REACH]], channel_multiplier=-sign).then_inc(H["t_sel"], 1)
                pool.wait_ge(H["t_sel"], 4 * m + 2 * h + 2)
                pool.tensor_tensor(reach[:, h, :], reach[:, h, :], back[:, :], ALU.add).then_inc(H["t_reach"], 1)
                pool.wait_ge(H["t_expf"], 8 * m + 4 * h + 4)
                pool.tensor_tensor(reach_c[:, h, :], reach_c[:, h, :], back_c[:, :], ALU.add).then_inc(H["t_reach"], 1)

            for m in range(4):
                for h in range(2):
                    head(m, h)

        Z = semaphores("z_const", "z_f", "z_gate", "z_d", "z_copied", "z_l", "z_hi", "z_lo", "z_yhi", "z_ylo", "z_ret",
                       "z_bank", "z_four", "z_sum", "z_mhi", "z_mlo")

        def four_sync(sp):
            for s in range(2):
                load_slot(sp, G_FOUR + s, (G_FOUR + s) % 2, pairs(a["w_in_2"], RF0 + s * 2 * P))
            sp.wait_ge(G["chunk_done"], 2 * G_FOUR)
            sp.wait_ge(H["t_reach"], 16)
            sp.wait_ge(H["t_vtok"], 8)
            sp.dma_start(dft_d[:, :], const["dft_d"]).then_inc(Z["z_const"], 16)
            sp.dma_start(dft_l[:, :, :, :], const["dft_l"].rearrange("a (i p) t -> p a i t", p=P))\
              .then_inc(Z["z_const"], 16)
            for s in range(4):
                load_slot(sp, G_GF + s, (G_GF + s) % 2, pairs(a["w_branch_gate_2"], D + s * 2 * P))
            for s in range(4):
                load_slot(sp, G_RO + s, (G_RO + s) % 2, pairs(a["w_ret_out_2"], s * 2 * P))
            sp.wait_ge(Z["z_l"], 4)
            sp.dma_start(x[:, :, :].rearrange("p k t -> p (k t)"), scratch_x).then_inc(H["x_out"], 16)
            for s in range(2):
                load_slot(sp, G_FO + s, (G_FO + s) % 2,
                          [(0, 16, T, a["w_four_out_2"][:, s * T:(s + 1) * T].rearrange("(k p) n -> p k n", p=P))])

        def four_tensor(pe):
            rest = ret_after_tensor(pe, 3)

            def over_features(g):
                if g == 0:
                    pe.wait_ge(Z["z_const"], 32)
                    pe.wait_ge(Z["z_f"], 4)
                    pe.wait_ge(H["t_dm"], 24)
                else:
                    pe.wait_ge(Z["z_copied"], g)
                for i in range(NT):
                    done = pe.matmul(psum[:, SA + i // 2, (i % 2) * 256:(i % 2) * 256 + 256],
                                     f_t[:, g, i * P:(i + 1) * P], dft_d[:, :], start=True, stop=True)
                done.then_inc(Z["z_d"], 1)

            def over_tokens(g):
                pe.wait_ge(Z["z_copied"], g + 1)
                if g == 0:
                    pe.wait_ge(H["t_y"], 9)
                if g >= 2:
                    pe.wait_ge(Z["z_lo"], g - 1)
                for n in range(8):
                    i, part = n // 2, n % 2
                    done = pe.matmul(psum[:, 5 + g % 2, :], fd[:, g, i, part * P:(part + 1) * P],
                                     dft_l[:, part, i, :], start=(n == 0), stop=(n == 7))
                done.then_inc(Z["z_l"], 1)

            for t in range(12):
                s, half = G_FOUR + t // 2, t % 2
                if t < 6:
                    rest[t]()
                if 5 <= t < 9:
                    over_features(t - 5)
                if 7 <= t < 11:
                    over_tokens(t - 7)
                if half == 0:
                    pe.wait_ge(G["lo_ready"], s + 1)
                if t < 2:
                    pe.wait_ge(H["t_gate"], 7 + t)
                elif t < 6:
                    pe.wait_ge(Z["z_f"], t - 1)
                else:
                    pe.wait_ge(Z["z_gate"], t - 5)
                half_slot(pe, s % 2, half, of_pairs, half)
            for s in range(4):
                if s == 0:
                    pe.wait_ge(Z["z_gate"], 8)
                if s >= 2:
                    pe.wait_ge(Z["z_ret"], 2 * s - 2)
                whole_slot(pe, G_RO + s, (G_RO + s) % 2, of_pairs, yr_hi, yr_lo, KC, Z["z_ylo"] if s == 0 else None, 0)
            pe.wait_ge(Z["z_lo"], 4)
            for c in range(KC):
                s = c // 4
                if c % 4 == 0:
                    pe.wait_ge(G["lo_ready"], G_FO + s + 1)
                if c >= 4:
                    pe.wait_ge(Z["z_four"], c - 3)
                for k in range(4):
                    done = product(pe, psum[:, 4 + c % 4, :], (G_FO + s) % 2, 4 * k + c % 4, z_hi, z_lo, k, k == 3)
                done.then_inc(G["chunk_done"] if c % 2 else Z["z_bank"], 1)

        def four_scalar(act):
            rest = ret_after_scalar(act, 3)
            ret_gate(act, 3, 1)
            for t in range(12):
                if t % 2 == 0:
                    split_hi(act, G_FOUR + t // 2 + 1, (G_FOUR + t // 2 + 1) % 2)
                if 1 <= t <= 4:
                    act.wait_ge(G["chunk_done"], 2 * G_FOUR + t)
                    act.activation(f_t[:, t - 1, :], psum[:, (t - 1) % 2, :], ACT.Copy).then_inc(Z["z_f"], 1)
                if t < 6:
                    rest[t]()
                if 5 <= t < 9:
                    act.wait_ge(Z["z_d"], t - 4)
                    act.activation(fd[:, t - 5, :, :], psum[:, SA:SA + 2, :].rearrange("p b (i n) -> p (b i) n", n=256),
                                   ACT.Copy).then_inc(Z["z_copied"], 1)
                if t >= 5:
                    four_gate(act, t - 5)
                if 7 <= t < 11:
                    g = t - 7
                    act.wait_ge(Z["z_l"], g + 1)
                    act.activation(z_hi[:, g, :], psum[:, 5 + g % 2, :], ACT.Copy).then_inc(Z["z_hi"], 1)
            four_gate(act, 7)
            for c in range(KC):
                act.activation(yr_hi[:, c, :], yr[:, c, :], ACT.Copy).then_inc(Z["z_yhi"], 1)
            for s in range(4):
                split_hi(act, G_RO + s + 1, (G_RO + s + 1) % 2)
            for c in range(KC):
                if c % 4 == 0:
                    split_hi(act, G_FO + c // 4 + 1, (G_FO + c // 4 + 1) % 2)
                act.wait_ge(Z["z_sum"], c + 1)
                act.activation(h_hi[:, c, :], pre[:, c % 2, :], ACT.Copy).then_inc(Z["z_mhi"], 1)

        def four_gate(act, c):
            act.wait_ge(G["chunk_done"], 2 * G_GF + c + 1)
            act.activation(gf[:, c, :], psum[:, c % 2, :], ACT.Sigmoid, bias=vec[:, V_BG + 8 + c:V_BG + 9 + c])\
               .then_inc(Z["z_gate"], 1)

        def four_vector(dve):
            rest = ret_after_vector(dve, 3)
            for t in range(12):
                if t % 2 == 0:
                    split_lo(dve, G_FOUR + t // 2 + 1, (G_FOUR + t // 2 + 1) % 2)
                if t < 6:
                    rest[t]()
                if 7 <= t < 11:
                    g = t - 7
                    dve.wait_ge(Z["z_hi"], g + 1)
                    dve.tensor_tensor(z_lo[:, g, :], psum[:, 5 + g % 2, :], z_hi[:, g, :].bitcast(F32), ALU.subtract)\
                       .then_inc(Z["z_lo"], 1)
            for c in range(KC):
                dve.wait_ge(Z["z_yhi"], c + 1)
                dve.tensor_tensor(yr_lo[:, c, :], yr[:, c, :], yr_hi[:, c, :].bitcast(F32), ALU.subtract)\
                   .then_inc(Z["z_ylo"], 1)
            for c in range(KC):
                s = G_RO + c // 2
                if c % 2 == 0:
                    split_lo(dve, s + 1, (s + 1) % 2)
                dve.wait_ge(G["chunk_done"], 2 * s + c % 2 + 1)
                dve.tensor_tensor(gr[:, c, :], gr[:, c, :], psum[:, 2 * (s % 2) + c % 2, :], ALU.mult)\
                   .then_inc(Z["z_ret"], 1)
            for c in range(KC):
                s = G_FO + c // 4
                if c % 4 == 0:
                    split_lo(dve, s + 1, (s + 1) % 2)
                if c % 2:
                    dve.wait_ge(G["chunk_done"], 2 * s + (c % 4) // 2 + 1)
                else:
                    dve.wait_ge(Z["z_bank"], c // 2 + 1)
                dve.wait_ge(Z["z_ret"], c + 1)
                dve.tensor_tensor(pre[:, c % 2, :], gf[:, c, :], psum[:, 4 + c % 4, :], ALU.mult).then_inc(Z["z_four"], 1)
                dve.wait_ge(Z["z_four"], c + 1)
                dve.tensor_tensor(pre[:, c % 2, :], pre[:, c % 2, :], gr[:, c, :], ALU.add).then_inc(Z["z_sum"], 1)
                dve.wait_ge(Z["z_mhi"], c + 1)
                dve.tensor_tensor(h_lo[:, c, :], pre[:, c % 2, :], h_hi[:, c, :].bitcast(F32), ALU.subtract)\
                   .then_inc(Z["z_mlo"], 1)

        def wout_sync(sp):
            for s in range(4):
                load_slot(sp, G_WOUT + s, (G_WOUT + s) % 2, pairs(a["w_out_2"], s * 2 * P))

        def wout_tensor(pe):
            add_tensor(pe, G_WOUT, G_WOUT % 2, R_WOUT, h_hi, h_lo, KC, Z["z_mlo"], 0, lambda s: None)

        def wout_scalar(act):
            add_scalar(act, G_WOUT, G_WOUT % 2, R_WOUT)

        def wout_vector(dve):
            dve.wait_ge(H["x_out"], 32)
            add_vector(dve, G_WOUT, G_WOUT % 2, R_WOUT, N_RET + 1, lambda c: mod[:, 16 + c, 0:1])

        V = semaphores("v_mid", "v_left", "v_conv", "v_gelu", "v_hid", "v_hi", "v_lo")

        def ffn_rounds(eng, body):
            with eng.Fori(0, 2) as q:
                body(q, 8)
            body(2, 6)

        def ffn_sync(sp):
            def body(q, n):
                g = G_FFN + 12 * q
                for s in range(n):
                    col = q * D + s * P
                    load_slot(sp, g + s, (G_FFN + s) % 2, halves(a["w_up_2"], col, col + FFN))
                for s in range(4):
                    load_slot(sp, g + n + s, (G_FFN + s) % 2,
                              pairs(a["w_down_2"][bass.ds(q * D, n * P), :], s * 2 * P))
            ffn_rounds(sp, body)

        def ffn_tensor(pe):
            norm_mean(pe, N_FFN)

            def body(q, n):
                g, r, j0 = G_FFN + 12 * q, R_FFN + q, G_FFN % 2
                for s in range(n):
                    if s < 2:
                        pe.wait_ge(G["x_ready"], 8 * r - 2 + 2 * s)
                    else:
                        pe.wait_ge(V["v_conv"], 2 * (8 * q + s) - 2)
                    whole_slot(pe, g + s, (j0 + s) % 2, of_halves, h_hi, h_lo, KC,
                               G["h_lo_ready"] if s == 0 else None, 8 * N_FFN)
                add_tensor(pe, g + n, j0, r, d2_hi, d2_lo, n, V["v_lo"], 8 * q,
                           lambda s: pe.wait_ge(V["v_conv"], 2 * (8 * q + n - 1 + s)))
            ffn_rounds(pe, body)

        def ffn_scalar(act):
            norm_rstd(act, N_FFN)
            norm_hi(act, N_FFN, lambda c: mod[:, 24 + c, 0:1])

            def body(q, n):
                g, r, j0 = G_FFN + 12 * q, R_FFN + q, G_FFN % 2
                for s in range(n):
                    at = 8 * q + s
                    split_hi(act, g + s + 1, (j0 + s + 1) % 2, 16 if s + 1 < n else 2 * n)
                    for half in range(2):
                        act.wait_ge(G["chunk_done"], 2 * (g + s) + half + 1)
                        col = at + half * FC
                        act.activation(cv[:, s % 2, half, :], psum[:, 2 * ((j0 + s) % 2) + half, :], ACT.Identity,
                                       bias=vec[:, bass.ds(V_CONVB + col, 1)],
                                       scale=vec[:, bass.ds(V_CONV2 + 2 * FC + col, 1)]).then_inc(V["v_mid"], 1)
                    act.wait_ge(V["v_conv"], 2 * at + 1)
                    act.activation(cv[:, s % 2, 0, :], cv[:, s % 2, 0, :], ACT.Gelu_apprx_tanh).then_inc(V["v_gelu"], 1)
                    act.wait_ge(V["v_hid"], at + 1)
                    act.activation(d2_hi[:, s, :], pre[:, s % 2, :], ACT.Copy).then_inc(V["v_hi"], 1)
                add_scalar(act, g + n, j0, r, (2 * n,) * 3 + (16 if n == 8 else 0,))
            ffn_rounds(act, body)

        def ffn_vector(dve):
            norm_dve(dve, N_FFN, lambda c: gain[:, 2, c:c + 1], lambda c: mod[:, 24 + c, 0:1])

            def body(q, n):
                g, r, j0 = G_FFN + 12 * q, R_FFN + q, G_FFN % 2
                for s in range(n):
                    at = 8 * q + s
                    split_lo(dve, g + s + 1, (j0 + s + 1) % 2, 16 if s + 1 < n else 2 * n)
                    for half in range(2):
                        col = at + half * FC
                        buf, bank = cv[:, s % 2, half, :], psum[:, 2 * ((j0 + s) % 2) + half, :]
                        dve.wait_ge(V["v_mid"], 2 * at + half + 1)
                        dve.scalar_tensor_tensor(out=buf[:, 1:T], in0=bank[:, 0:T - 1],
                                                 scalar=vec[:, bass.ds(V_CONV2 + col, 1)], in1=buf[:, 1:T],
                                                 op0=ALU.mult, op1=ALU.add).then_inc(V["v_left"], 1)
                        dve.wait_ge(V["v_left"], 2 * at + half + 1)
                        dve.scalar_tensor_tensor(out=buf[:, 0:T - 1], in0=bank[:, 1:T],
                                                 scalar=vec[:, bass.ds(V_CONV2 + 4 * FC + col, 1)],
                                                 in1=buf[:, 0:T - 1], op0=ALU.mult, op1=ALU.add)\
                           .then_inc(V["v_conv"], 1)
                    dve.wait_ge(V["v_gelu"], at + 1)
                    dve.wait_ge(V["v_conv"], 2 * at + 2)
                    dve.tensor_tensor(pre[:, s % 2, :], cv[:, s % 2, 0, :], cv[:, s % 2, 1, :], ALU.mult)\
                       .then_inc(V["v_hid"], 1)
                    dve.wait_ge(V["v_hi"], at + 1)
                    dve.tensor_tensor(d2_lo[:, s, :], pre[:, s % 2, :], d2_hi[:, s, :].bitcast(F32), ALU.subtract)\
                       .then_inc(V["v_lo"], 1)
                add_vector(dve, g + n, j0, r, N_FFN + 1, lambda c: mod[:, 40 + c, 0:1],
                           (2 * n,) * 3 + (16 if n == 8 else 0,))
            ffn_rounds(dve, body)

        OUT = semaphores("o_turned", "o_copied", "o_out0", "o_out1")

        def out_tensor(pe):
            norm_mean(pe, N_OUT)
            for c in range(KC):
                pe.wait_ge(G["pre_ready"], 8 * N_OUT + c + 1)
                if c >= 4:
                    pe.wait_ge(OUT["o_copied"], c - 3)
                for i in range(NT):
                    done = pe.transpose(psum[:, c % 4, i * P:(i + 1) * P], pre[:, c % 2, i * P:(i + 1) * P], ident)
                done.then_inc(OUT["o_turned"], 1)

        def out_scalar(act):
            norm_rstd(act, N_OUT)
            for c in range(KC):
                act.wait_ge(OUT["o_turned"], c + 1)
                if c >= 2:
                    act.wait_ge((OUT["o_out0"], OUT["o_out1"])[c % 2], 16 * (c // 2))
                act.activation(cv[:, c % 2, 0, :], psum[:, c % 4, :], ACT.Copy).then_inc(OUT["o_copied"], 1)

        def out_vector(dve):
            dve.wait_ge(G["rstd_ready"], N_OUT + 1)
            for c in range(KC):
                if c >= 2:
                    dve.wait_ge(OUT["o_turned"], c - 1)
                dve.scalar_tensor_tensor(out=pre[:, c % 2, :], in0=x[:, c, :], scalar=vec[:, V_FIN + c:V_FIN + c + 1],
                                         in1=rstd[:, :], op0=ALU.mult, op1=ALU.mult).then_inc(G["pre_ready"], 1)

        def out_sync(sp):
            for c in range(KC):
                sp.wait_ge(OUT["o_copied"], c + 1)
                sp.dma_start(out[:, c * P:(c + 1) * P].rearrange("(i p) n -> p i n", p=P),
                             cv[:, c % 2, 0, :].rearrange("p (i n) -> p i n", n=P))\
                  .then_inc((OUT["o_out0"], OUT["o_out1"])[c % 2], 16)
            for s in (OUT["o_out0"], OUT["o_out1"]):
                sp.wait_ge(s, 16 * KC // 2)

        block = root.enter_context(nc.Block())

        @block.sync
        def _(sp):
            for stage in (start_sync, mix_sync, merge_sync, wo_sync, embed_sync, moe_sync, ple_sync, ret_sync, four_sync,
                          wout_sync, ffn_sync, out_sync):
                stage(sp)

        @block.scalar
        def _(act):
            for stage in (start_scalar, forget_scalar, mix_scalar, merge_scalar, wo_scalar, embed_scalar, moe_scalar, ple_scalar,
                          ret_scalar, four_scalar, wout_scalar, ffn_scalar, out_scalar):
                stage(act)

        @block.tensor
        def _(pe):
            for stage in (start_tensor, mix_tensor, merge_tensor, wo_tensor, embed_tensor, moe_tensor, ple_tensor, ret_tensor,
                          four_tensor, wout_tensor, ffn_tensor, out_tensor):
                stage(pe)

        @block.vector
        def _(dve):
            for stage in (start_vector, mix_vector, merge_vector, wo_vector, embed_vector, moe_vector, ple_vector, ret_vector,
                          four_vector, wout_vector, ffn_vector, out_vector):
                stage(dve)

        @block.gpsimd
        def _(pool):
            for stage in (mix_gpsimd, moe_gpsimd, ret_gpsimd):
                stage(pool)


def kernel(**inputs):
    import concourse.bacc as bacc
    from concourse.bass_utils import run_bass_kernel_spmd

    nc = bacc.Bacc("TRN2", target_bir_lowering=False, num_devices=1)
    arrays, a, const = {}, {}, {}
    for name, value in inputs.items():
        value = np.ascontiguousarray(value)
        while value.ndim > 1 and value.shape[0] == 1:
            value = value[0]
        if name in ("conv_w", "conv_w_2"):
            value = value.reshape(-1)
        arrays[f"in_{name}"] = value
        a[name] = nc.dram_tensor(f"in_{name}", value.shape, F32, kind="ExternalInput").ap()
    for name, value in shape_constants().items():
        arrays[f"const_{name}"] = value
        const[name] = nc.dram_tensor(f"const_{name}", value.shape, F32, kind="ExternalInput").ap()
    out = nc.dram_tensor("out", (T, D), F32, kind="ExternalOutput").ap()
    build(nc, a, const, out)
    result = run_bass_kernel_spmd(nc, [arrays], core_ids=[0])
    return result.results[0]["out"].reshape(1, T, D)
```

```python
from contextlib import ExitStack

import numpy as np

import concourse.bass as bass
from concourse import mybir

F32 = mybir.dt.float32
F32R = mybir.dt.float32r
ALU = mybir.AluOpType
ACT = mybir.ActivationFunctionType
AX = mybir.AxisListType

P = 128
T = 512
D = 1024
KC = D // P
NT = T // P
EPS = 1e-6
NEG_INF = -1e30

HEADS, HEAD_DIM = 8, 64
ATT = HEADS * HEAD_DIM
CONV = 512
CB0 = 3 * ATT + HEADS
CC0, CU0 = CB0 + CONV, CB0 + 2 * CONV
GA0 = CB0 + 3 * CONV
GB0 = GA0 + D
GROUPS, PER_GROUP = 4, 4
EXPERTS = GROUPS * PER_GROUP
ROUTE = GROUPS + EXPERTS
D_EXPERT = 256
PLE = 256

CTX = 256
RET_HEADS, RET_V = 8, 128
RK0, RV0 = 512, 1024
RG0, RF0 = RV0 + RET_HEADS * RET_V, RV0 + 2 * RET_HEADS * RET_V
FFN = 2816
FC = FFN // P
FFN_ROUNDS = (8, 8, 6)
CHUNK = P
DIST = 3 * CHUNK + 5

G_FORGET = 0
G_MIX = 1
G_MERGE = G_MIX + 16
G_WO = G_MERGE + 8
G_PLE = G_WO + 4
G_MOE = G_PLE + 1
G_PG = G_MOE + 48
G_RET = G_PG + 4
G_FOUR = G_RET + 16
G_GF = G_FOUR + 2
G_RO = G_GF + 4
G_FO = G_RO + 4
G_WOUT = G_FO + 2
G_FFN = G_WOUT + 4
G_END = G_FFN + sum(FFN_ROUNDS) + 4 * len(FFN_ROUNDS)

R_START, R_WO, R_MOE, R_PG, R_WOUT, R_FFN = 0, 1, 2, 6, 7, 8
N_ATT, N_MOE, N_PLE, N_RET, N_FFN, N_OUT = range(6)
ROUND_OF = (R_START, R_WO, R_MOE + 3, R_PG, R_WOUT, R_FFN + 2)

V_ATT_G, V_CONV, V_FFN_G, V_PLE_G, V_N1, V_N2, V_FIN = 0, 8, 20, 28, 36, 44, 52
V_C, V_CC, V_BG, V_QG, V_KG = 60, 68, 76, 92, 93
V_CONV2, V_CONVB, V_BMOD = 128, 128 + 3 * 2 * FC, 128 + 4 * 2 * FC
V_ROWS = (94, 128, 4 * 2 * FC + 48 - 128)
V_COLS = 256 + V_ROWS[2]


def shape_constants():
    ident = np.eye(P, dtype=np.float32)
    blocks = np.kron(np.eye(2, dtype=np.float32), np.ones((64, 64), np.float32))
    turn = np.zeros((P, P), np.float32)
    for h in range(2):
        for d in range(32):
            turn[64 * h + 32 + d, 64 * h + d] = -1.0
            turn[64 * h + d, 64 * h + 32 + d] = 1.0
    t = np.arange(T)
    inv = (np.float32(10000.0) ** (-np.arange(16, dtype=np.float32) / np.float32(16))).astype(np.float32)
    row, col = (t // 64).astype(np.float32), (t % 64).astype(np.float32)
    ang = np.concatenate([row[:, None] * inv, col[:, None] * inv], axis=-1)
    cos, sin = (np.tile(f(ang).astype(np.float32).T, (4, 1)) for f in (np.cos, np.sin))
    j = np.arange(P)
    a = 2 * np.pi * np.outer(j, j) / P
    dft_d = np.concatenate([np.cos(a), -np.sin(a)], axis=1).astype(np.float32) / np.float32(256)
    a = 2 * np.pi * (np.outer(t, t) % T) / T
    dft_l = np.stack([np.cos(a), np.sin(a)]).astype(np.float32)
    col, part = np.arange(P)[None, :], np.arange(P)[:, None]
    at = np.arange(1)[None, :]
    dist = np.concatenate([col - part, col + 1 + 0 * part, CHUNK - col + 0 * part, CHUNK - 1 - part, part + at,
                           2 * CHUNK - 1 - part, CHUNK + part, CHUNK + 0 * part], axis=1).astype(np.float32)
    return {
        "small": np.concatenate([ident, blocks, turn], axis=1),
        "rope": np.stack([cos, sin], axis=1).reshape(P, 2 * T),
        "dft_d": dft_d,
        "dft_l": dft_l,
        "dist": dist,
    }


def nothing():
    pass


def build(nc, a, const, out):
    scratch_c = nc.dram_tensor("scratch_c", [HEADS, T], F32, kind="Internal").ap()
    scratch_comb = nc.dram_tensor("scratch_comb", [EXPERTS, T], F32, kind="Internal").ap()
    scratch_x = nc.dram_tensor("scratch_x", [P, KC * T], F32, kind="Internal").ap()

    root = ExitStack()
    with root:
        def buffers(stack):
            def sb(name, shape, dt=F32):
                return stack.enter_context(nc.sbuf_tensor(name, shape, dt))
            return sb

        def semaphores(*names):
            return {n: root.enter_context(nc.semaphore(n)) for n in names}

        sb = buffers(root)
        raw = [sb(f"raw{j}", [P, 16, P]) for j in range(2)]
        w_hi = [sb(f"w_hi{j}", [P, 16, P], F32R) for j in range(2)]
        w_lo = [sb(f"w_lo{j}", [P, 16, P], F32R) for j in range(2)]
        h_hi = sb("h_hi", [P, KC, T], F32R)
        h_lo = sb("h_lo", [P, KC, T], F32R)
        small = sb("small", [P, 3, P])
        ident, head_blocks, turn = small[:, 0, :], small[:, 1, :], small[:, 2, :]
        ones = sb("ones", [P, P])
        vec = sb("vec", [P, V_COLS])
        mod = sb("mod", [P, 48, 2])
        silu_c = sb("silu_c", [P, KC, 2])
        gain = sb("gain", [P, 3, KC])
        sq = sb("sq", [P, 2, T])
        ss = sb("ss", [P, T])
        rstd = sb("rstd", [P, T])
        pre = sb("pre", [P, 2, T])
        bias_f = sb("bias_f", [HEADS, 1])
        eps = sb("eps", [P, 1])
        warm = sb("warm", [P, 6])

        with ExitStack() as s:
            sb = buffers(s)
            near = sb("near", [P, RET_HEADS, CHUNK])
            near_b = sb("near_b", [P, RET_HEADS, CHUNK])
            q_reach = sb("q_reach", [P, 2, 4, CHUNK])
            state = sb("state", [P, 2, NT, RET_V])
        with ExitStack() as s:
            fd = buffers(s)("fd", [P, 4, NT, 2 * P])
        x = buffers(root)("x", [P, KC, T])

        first = ExitStack()
        sb = buffers(first)
        d_hi = sb("d_hi", [P, KC, T], F32R)
        d_lo = sb("d_lo", [P, KC, T], F32R)
        with ExitStack() as s:
            sb = buffers(s)
            x_in = sb("x_in", [P, NT, D])
            v_in = sb("v_in", [P, 3, P])
            x_ss = sb("x_ss", [P, NT])
            x_diag = sb("x_diag", [P, NT, P])
        with ExitStack() as gates:
            ga = buffers(gates)("ga", [P, KC, T])
            with ExitStack() as s:
                sb = buffers(s)
                c_all = sb("c_all", [P, HEADS, T])
                c_row = sb("c_row", [HEADS, T])
                c_col = sb("c_col", [P, NT, HEADS])
                neg_max = sb("neg_max", [P, NT, 2])
                row_sum = sb("row_sum", [P, NT, 2])
                row_inv = sb("row_inv", [P, NT, 2])
                y_tok = sb("y_tok", [P, P])
                bias_qk = sb("bias_qk", [P, 2, T])
                prob = sb("prob", [P, 2, T])
                prob_t = sb("prob_t", [P, 2, T])
                q_raw = sb("q_raw", [P, T])
                k_raw = sb("k_raw", [P, T])
                v_raw = sb("v_raw", [P, T])
                q_t = sb("q_t", [P, T])
                k_t = sb("k_t", [P, T])
                v_tok = sb("v_tok", [P, NT, P])
                u_pad = sb("u_pad", [P, 2 + T])
                u_zero = u_pad[:, 0:2]
            with ExitStack() as s:
                sb = buffers(s)
                m_hi = sb("m_hi", [P, KC, T], F32R)
                m_lo = sb("m_lo", [P, KC, T], F32R)
                gb = sb("gb", [P, 2, T])
        with ExitStack() as s:
            sb = buffers(s)
            p_in = sb("p_in", [P, NT, PLE])
            p_hi = sb("p_hi", [P, 2, T], F32R)
            p_lo = sb("p_lo", [P, 2, T], F32R)
            wr_raw = sb("wr_raw", [P, KC, P])
        with ExitStack() as s:
            sb = buffers(s)
            ctx_x = sb("ctx_x", [P, KC, CTX])
            ctx_sq = sb("ctx_sq", [P, KC, CTX])
            sig = sb("sig", [P, 2, T])
            ctx_pre = sb("ctx_pre", [P, 2, CTX])
            ctx_r = sb("ctx_r", [P, CTX])
        sb = buffers(first)
        comb_all = sb("comb_all", [P, PER_GROUP, T])
        wm_raw = sb("wm_raw", [P, 2, KC, 2 * P])
        pl = sb("pl", [P, KC, T])
        act_u = sb("act_u", [P, 2, T])
        wm_sum = sb("wm_sum", [P, 2, 2, 2 * P])
        rt_row = sb("rt_row", [ROUTE, T])
        b_route = sb("b_route", [P, ROUTE])
        rt = sb("rt", [P, NT, ROUTE])
        r4 = sb("r4", [P, 8, NT, 4])
        comb = sb("comb", [P, NT, EXPERTS])
        comb_row = sb("comb_row", [EXPERTS, T])
        iota4 = sb("iota4", [P, 4])
        r1 = sb("r1", [P, 8, NT])
        with ExitStack() as s:
            sb = buffers(s)
            wr_hi = sb("wr_hi", [P, KC, P], F32R)
            wr_lo = sb("wr_lo", [P, KC, P], F32R)
        ctx_in = buffers(first)("ctx_in", [P, 2, D])
        first.close()

        second = ExitStack()
        with ExitStack() as s:
            sb = buffers(s)
            hc_hi = sb("hc_hi", [P, KC, CTX], F32R)
            hc_lo = sb("hc_lo", [P, KC, CTX], F32R)
        gf = buffers(second)("gf", [P, KC, T])
        f_t = gf[:, 4:8, :]
        with ExitStack() as s:
            yr_lo = buffers(s)("yr_lo", [P, KC, T], F32R)
        yr = buffers(second)("yr", [P, KC, T])
        gr = buffers(second)("gr", [P, KC, T])
        with ExitStack() as s:
            sb = buffers(s)
            dist = sb("dist", [P, DIST])
            rope = sb("rope", [P, 2, T])
            kr_raw = sb("kr_raw", [P, T + CTX])
            qr_raw = sb("qr_raw", [P, T])
            vr_raw = sb("vr_raw", [P, T + CTX])
            k_dec = sb("k_dec", [P, 2, 6, 2, HEAD_DIM])
            qr_t = sb("qr_t", [P, T])
            kr_t = sb("kr_t", [P, T + CTX])
            vr_tok = sb("vr_tok", [P, 2, T + CTX])
            weighted = sb("weighted", [P, 2, T])
            q_dec = sb("q_dec", [P, 2, T])
            sg = sb("sg", [P, 2, T])
            o_buf = sb("o_buf", [P, T])
            cen = sb("cen", [P, T])
            decay = sb("decay", [P, 2, RET_HEADS])
            decay_b = sb("decay_b", [P, RET_HEADS])
            decay_row = sb("decay_row", [P, 2, 4])
            k_reach = sb("k_reach", [P, 2, 3, RET_HEADS])
            step = sb("step", [P, 2, 4])
        with ExitStack() as s:
            with ExitStack() as r:
                yr_hi = buffers(r)("yr_hi", [P, KC, T], F32R)
            sb = buffers(s)
            dft_l = sb("dft_l", [P, 2, NT, T])
            dft_d = sb("dft_d", [P, 2 * P])
            z_gap = sb("z_gap", [P, 1536])
            z_hi = sb("z_hi", [P, 4, T], F32R)
            z_lo = sb("z_lo", [P, 4, T], F32R)
        second.close()

        with ExitStack() as s:
            sb = buffers(s)
            d2_hi = sb("d2_hi", [P, KC, T], F32R)
            d2_lo = sb("d2_lo", [P, KC, T], F32R)
            cv = sb("cv", [P, 2, 2, T])

        psum = root.enter_context(nc.psum_tensor("psum", [P, 8, T], F32))

        G = semaphores(
            "raw_in0", "raw_in1",
            "hi_ready", "lo_ready",
            "chunk_done",
            "x_ready",
            "sq_ready", "ss_added",
            "ms_ready",
            "ln_ready", "rstd_ready",
            "pre_ready", "h_hi_ready", "h_lo_ready",
        )
        raw_in = (G["raw_in0"], G["raw_in1"])

        def load_slot(sp, g, j, pieces):
            if not isinstance(g, int) or g >= 2:
                sp.wait_ge(G["lo_ready"], g - 1)
            for t0, n, width, src in pieces:
                dst = raw[j][:, t0:t0 + n, :]
                if width > P:
                    dst = dst.rearrange("p (k a) n -> p k (a n)", a=width // P)
                sp.dma_start(dst, src).then_inc(raw_in[j], 32 // len(pieces))

        def split_hi(act, g, j, tiles=16):
            act.wait_ge(raw_in[j], 16 * (g - j) + 32)
            if not isinstance(g, int) or g >= 2:
                act.wait_ge(G["chunk_done"], 2 * g - 2)
            act.activation(w_hi[j][:, 0:tiles, :], raw[j][:, 0:tiles, :], ACT.Copy).then_inc(G["hi_ready"], 1)

        def split_lo(dve, g, j, tiles=16):
            dve.wait_ge(G["hi_ready"], g + 1)
            dve.tensor_tensor(w_lo[j][:, 0:tiles, :], raw[j][:, 0:tiles, :],
                              w_hi[j][:, 0:tiles, :].bitcast(F32), ALU.subtract).then_inc(G["lo_ready"], 1)

        def halves(w, c0, c1=None):
            cols = [c0] if c1 is None else [c0, c1]
            return [(8 * i, 8, P, w[:, bass.ds(c, P)].rearrange("(k p) n -> p k n", p=P))
                    for i, c in enumerate(cols)]

        def pairs(w, c, t0=0):
            k = w.shape[0] // P
            return [(t0, 2 * k, 2 * P, w[:, bass.ds(c, 2 * P)].rearrange("(k p) n -> p k n", p=P))]

        def of_halves(half, k):
            return 8 * half + k

        def of_pairs(half, k):
            return 2 * k + half

        def product(pe, to, j, tile, hi, lo, k, last, n=T):
            hi_k, lo_k = hi[:, k, 0:n], lo[:, k, 0:n]
            pe.matmul(to, w_hi[j][:, tile, :], hi_k, start=(k == 0), stop=False)
            pe.matmul(to, w_hi[j][:, tile, :], lo_k, start=False, stop=False)
            return pe.matmul(to, w_lo[j][:, tile, :], hi_k, start=False, stop=last)

        def half_slot(pe, j, half, tile_of, bank, chunks=KC, between=None):
            for k in range(chunks):
                if between is not None and k == chunks // 2:
                    between()
                done = product(pe, psum[:, bank, :], j, tile_of(half, k), h_hi, h_lo, k, k == chunks - 1)
            done.then_inc(G["chunk_done"], 1)

        def whole_slot(pe, g, j, tile_of, hi, lo, chunks=KC, ready=None, count=0):
            pe.wait_ge(G["lo_ready"], g + 1)
            for k in range(chunks):
                if ready is not None:
                    pe.wait_ge(ready, count + k + 1)
                for half in range(2):
                    done = product(pe, psum[:, 2 * j + half, :], j, tile_of(half, k), hi, lo, k,
                                   k == chunks - 1)
                    if k == chunks - 1:
                        done.then_inc(G["chunk_done"], 1)

        def square(act, r, c):
            act.wait_ge(G["x_ready"], 8 * r + c + 1)
            if not isinstance(r, int) or r > R_WO or c >= 2:
                act.wait_ge(G["ss_added"], 8 * (r - 1) + c - 1)
            act.activation(sq[:, c % 2, :], x[:, c, :], ACT.Square).then_inc(G["sq_ready"], 1)

        def add_square(dve, r, c, norms=None):
            dve.wait_ge(G["sq_ready"], 8 * (r - 1) + c + 1)
            if c == 0:
                if norms:
                    dve.wait_ge(G["ms_ready"], norms)
                dve.tensor_copy(ss[:, :], sq[:, 0, :]).then_inc(G["ss_added"], 1)
            else:
                dve.wait_ge(G["ss_added"], 8 * (r - 1) + c)
                dve.tensor_tensor(ss[:, :], ss[:, :], sq[:, c % 2, :], ALU.add).then_inc(G["ss_added"], 1)

        def keep_warm(pe, bank, times):
            for _ in range(times):
                pe.matmul(psum[:, bank, 0:3 * P], ones[:, :], small[:, :, :].rearrange("p a n -> p (a n)"),
                          start=True, stop=True)

        def norm_mean(pe, n):
            pe.wait_ge(G["ss_added"], 8 * ROUND_OF[n])
            pe.matmul(psum[:, 7, :], ones[:, :], ss[:, :], start=True, stop=True).then_inc(G["ms_ready"], 1)

        def norm_rstd(act, n, bank=7):
            act.activation(warm[:, n:n + 1], ones[:, 0:1], ACT.Ln)
            act.wait_ge(G["ms_ready"], n + 1)
            act.activation(rstd[:, :], psum[:, bank, :], ACT.Ln, bias=eps[:, 0:1], scale=1.0 / D)\
               .then_inc(G["ln_ready"], 1)
            act.wait_ge(G["ln_ready"], n + 1)
            act.activation(rstd[:, :], rstd[:, :], ACT.Exp, scale=-0.5).then_inc(G["rstd_ready"], 1)

        def norm_hi(act, n, shift=None, between=None):
            for c in range(KC):
                act.wait_ge(G["pre_ready"], 8 * n + c + 1)
                if shift is None:
                    ins = act.activation(h_hi[:, c, :], pre[:, c % 2, :], ACT.Copy)
                else:
                    ins = act.activation(h_hi[:, c, :], pre[:, c % 2, :], ACT.Identity, bias=shift(c))
                ins.then_inc(G["h_hi_ready"], 1)
                if between:
                    between(c)

        def norm_pre(dve, n, c, g):
            if c >= 2:
                dve.wait_ge(G["h_lo_ready"], 8 * n + c - 1)
            dve.scalar_tensor_tensor(out=pre[:, c % 2, :], in0=x[:, c, :], scalar=g(c), in1=rstd[:, :],
                                     op0=ALU.mult, op1=ALU.mult).then_inc(G["pre_ready"], 1)

        def norm_lo(dve, n, c, shift=None):
            dve.wait_ge(G["h_hi_ready"], 8 * n + c + 1)
            hi = h_hi[:, c, :].bitcast(F32)
            if shift is None:
                ins = dve.tensor_tensor(h_lo[:, c, :], pre[:, c % 2, :], hi, ALU.subtract)
            else:
                ins = dve.scalar_tensor_tensor(out=h_lo[:, c, :], in0=pre[:, c % 2, :], scalar=shift(c),
                                               in1=hi, op0=ALU.add, op1=ALU.subtract)
            ins.then_inc(G["h_lo_ready"], 1)

        def norm_dve(dve, n, g, shift=None):
            dve.wait_ge(G["rstd_ready"], n + 1)
            norm_pre(dve, n, 0, g)
            for c in range(KC):
                if c + 1 < KC:
                    norm_pre(dve, n, c + 1, g)
                norm_lo(dve, n, c, shift)

        S = semaphores("x_in0", "x_in1", "v_in", "small_in", "x_turned", "v_copied", "x_sq", "x_diag")

        VECTORS = (
            ("attn_norm_g", 0, V_ATT_G, 8), ("conv_w", 0, V_CONV, 12), ("ffn_norm_g", 0, V_FFN_G, 8),
            ("ple_norm_g", 0, V_PLE_G, 8), ("norm1_w_2", 0, V_N1, 8), ("norm2_w_2", 0, V_N2, 8),
            ("final_norm_w_2", 0, V_FIN, 8), ("c_2", 0, V_C, 8), ("c_ctx_2", 0, V_CC, 8),
            ("b_branch_gate_2", 0, V_BG, 16),
        )
        x_half_in = (S["x_in0"], S["x_in1"])
        V_DMAS = 16 * (len(VECTORS) + 9)

        def start_sync(sp):
            sp.dma_start(small[:, :, :], const["small"].rearrange("p (a n) -> p a n", a=3))\
              .then_inc(S["small_in"], 16)
            for i in range(NT):
                sp.dma_start(x_in[:, i, :], a["x"][i * P:(i + 1) * P, :]).then_inc(x_half_in[i // 2], 16)
            load_slot(sp, G_FORGET, 0, halves(a["w_in"], 3 * ATT))
            load_slot(sp, G_MIX, 1, mix_pieces(0, 0))
            n = 0
            for name, at, row, rows in VECTORS:
                sp.dma_start(v_in[row:row + rows, 0, :], a[name].rearrange("(r n) -> r n", n=P))\
                   .then_inc(S["v_in"], 16)
                n += 1
            for row, name in ((V_QG, "q_norm_g"), (V_KG, "k_norm_g")):
                for h in range(2):
                    sp.dma_start(v_in[row:row + 1, 0, 64 * h:64 * h + 64], a[name].rearrange("(r n) -> r n", r=1))\
                       .then_inc(S["v_in"], 16)
                    n += 1
            w2 = a["conv_w_2"].rearrange("(r n) -> r n", n=P)
            sp.dma_start(v_in[:, 1, :], w2[0:P, :]).then_inc(S["v_in"], 16)
            sp.dma_start(v_in[0:4, 2, :], w2[P:P + 4, :]).then_inc(S["v_in"], 16)
            sp.dma_start(v_in[4:48, 2, :], a["conv_b_2"].rearrange("(r n) -> r n", n=P)).then_inc(S["v_in"], 16)
            sp.dma_start(v_in[48:96, 2, :], a["b_mod_2"].rearrange("(r n) -> r n", n=P)).then_inc(S["v_in"], 16)
            sp.dma_start(bias_f[:, :], a["b_f"].rearrange("(r n) -> r n", n=1)).then_inc(S["v_in"], 16)
            assert 16 * (n + 5) == V_DMAS

        def start_scalar(act):
            for i in range(NT):
                if i % 2 == 0:
                    act.wait_ge(x_half_in[i // 2], 32)
                if i >= 2:
                    act.wait_ge(S["x_sq"], i - 1)
                act.activation((sq, pre)[i % 2][:, :, :].rearrange("p a t -> p (a t)"), x_in[:, i, :], ACT.Square,
                               accum_out=x_ss[:, i:i + 1]).then_inc(S["x_sq"], 1)
            split_hi(act, G_FORGET, 0, 8)
            act.wait_ge(G["x_ready"], 1)
            norm_rstd(act, N_ATT, 0)
            split_hi(act, G_MIX, 1)
            norm_hi(act, N_ATT)

        def start_tensor(pe):
            pe.wait_ge(S["small_in"], 16)
            for half in range(2):
                pe.wait_ge(x_half_in[half], 32)
                for c in range(KC):
                    for i in (2 * half, 2 * half + 1):
                        done = pe.transpose(psum[:, c, i * P:(i + 1) * P], x_in[:, i, c * P:(c + 1) * P], ident)
                    if half:
                        done.then_inc(S["x_turned"], 1)
            pe.wait_ge(S["x_diag"], NT)
            pe.wait_ge(G["x_ready"], 1)
            for i in range(NT):
                done = pe.matmul(psum[:, 0, i * P:(i + 1) * P], ones[:, :], x_diag[:, i, :], start=True, stop=True)
            done.then_inc(G["ms_ready"], 1)
            pe.wait_ge(S["v_in"], V_DMAS)
            pe.wait_ge(G["x_ready"], 2)
            for b, rows in enumerate(V_ROWS):
                done = pe.transpose(psum[:, 1, b * P:b * P + rows], v_in[0:rows, b, :], ident[0:rows, 0:rows])
            done.then_inc(S["x_turned"], 1)
            pe.wait_ge(G["x_ready"], 3)
            keep_warm(pe, 2, 4)

        def start_vector(dve):
            dve.memset(eps[:, :], EPS).then_inc(H["t_y"], 1)
            dve.memset(u_zero, 0.0).then_inc(M["m_y_lo"], 1)
            dve.memset(ones[:, :], 1.0)
            for c in range(KC):
                dve.wait_ge(S["x_turned"], c + 1)
                dve.tensor_copy(x[:, c, :], psum[:, c, :]).then_inc(G["x_ready"], 1)
                if c == 3:
                    dve.wait_ge(S["x_sq"], NT)
                    for i in range(NT):
                        dve.tensor_scalar(x_diag[:, i, :], ident, x_ss[:, i:i + 1], None, ALU.mult)\
                           .then_inc(S["x_diag"], 1)
            split_lo(dve, 0, 0, 8)
            dve.wait_ge(S["x_turned"], KC + 1)
            dve.tensor_copy(vec[:, 0:V_ROWS[0]], psum[:, 1, 0:V_ROWS[0]])
            dve.tensor_copy(vec[:, P:V_COLS], psum[:, 1, P:V_COLS]).then_inc(S["v_copied"], 1)
            dve.wait_ge(S["v_copied"], 1)
            norm_dve(dve, N_ATT, lambda c: vec[:, V_ATT_G + c:V_ATT_G + c + 1])

        def start_gpsimd(pool):
            pool.wait_ge(G["lo_ready"], 1)
            split_lo(pool, G_MIX, 1)

        FG = semaphores("f_bias", "f_chain", "c_row", "c_turned", "c_col", "c_all")

        def forget_sync(sp):
            sp.wait_ge(FG["c_row"], 1)
            sp.dma_start(scratch_c, c_row[:, :]).then_inc(FG["c_all"], 16)
            sp.wait_ge(FG["c_all"], 16)
            sp.dma_start(c_all[:, :, :], scratch_c.rearrange("(o h) t -> o h t", o=1).to_broadcast([P, HEADS, T]))\
              .then_inc(FG["c_all"], 16)

        def forget_tensor(pe):
            pe.wait_ge(G["lo_ready"], 1)
            pe.wait_ge(S["v_copied"], 1)
            for k in range(KC):
                pe.wait_ge(G["h_lo_ready"], 8 * N_ATT + k + 1)
                done = product(pe, psum[:, 4, :], 0, k, h_hi, h_lo, k, k == KC - 1)
                if k == KC - 1:
                    done.then_inc(G["chunk_done"], 2)
                if k == 0:
                    pe.wait_ge(G["lo_ready"], 2)
                done = product(pe, psum[:, 0, :], 1, of_halves(0, k), h_hi, h_lo, k, k == KC - 1)
            done.then_inc(G["chunk_done"], 1)

        def forget_turn(pe):
            pe.wait_ge(FG["c_row"], 1)
            for i in range(NT):
                done = pe.transpose(psum[:, 3, i * HEADS:(i + 1) * HEADS], c_row[:, i * P:(i + 1) * P],
                                    ident[0:HEADS, 0:HEADS])
            done.then_inc(FG["c_turned"], 1)

        f_z, f_abs, f_one = sq[0:HEADS, 0, :], sq[0:HEADS, 1, :], pre[0:HEADS, 1, :]

        def forget_scalar(act):
            split_hi(act, G_MIX + 1, 1 - G_MIX % 2)
            act.wait_ge(G["chunk_done"], 2)
            act.wait_ge(G["h_lo_ready"], 8 * N_ATT + 8)
            act.activation(f_z, psum[0:HEADS, 4, :], ACT.Identity, bias=bias_f[:, 0:1]).then_inc(FG["f_bias"], 1)
            act.wait_ge(FG["f_bias"], 1)
            act.activation(f_abs, f_z, ACT.Abs).then_inc(FG["f_bias"], 1)
            act.wait_ge(FG["f_bias"], 2)
            act.activation(f_abs, f_abs, ACT.Exp, scale=-1.0).then_inc(FG["f_bias"], 1)
            act.wait_ge(FG["f_bias"], 3)
            act.activation(f_abs, f_abs, ACT.Ln, bias=1.0).then_inc(FG["f_bias"], 1)

        def forget_vector(dve):
            dve.wait_ge(G["h_lo_ready"], 8)
            dve.memset(f_one, 1.0).then_inc(FG["f_chain"], 1)
            split_lo(dve, G_MIX + 1, 1 - G_MIX % 2)
            dve.wait_ge(FG["f_bias"], 4)
            dve.scalar_tensor_tensor(out=f_z, in0=f_z, scalar=0.0, in1=f_abs, op0=ALU.min,
                                     op1=ALU.subtract).then_inc(FG["f_chain"], 1)
            dve.wait_ge(FG["f_chain"], 2)
            dve.tensor_tensor_scan(c_row[:, :], f_one, f_z, 0.0, ALU.mult, ALU.add).then_inc(FG["c_row"], 1)
            dve.wait_ge(FG["c_turned"], 1)
            dve.tensor_copy(c_col[:, :, :], psum[:, 3, 0:NT * HEADS].rearrange("p (i h) -> p i h", h=HEADS))\
               .then_inc(FG["c_col"], 1)

        M = semaphores("m_v_raw", "m_q_raw", "m_k_raw", "m_cc_raw", "m_ga", "m_u", "m_yc", "m_yc_hi", "m_yc_lo",
                       "m_sq", "m_mean", "m_ln", "m_r", "m_qk", "m_v_turned", "m_v_tok", "m_bias",
                       "m_scores", "m_logits", "m_max", "m_prob", "m_prob_t", "m_prob_copied", "m_inv",
                       "m_y", "m_y_tok", "m_y_turned", "m_y_hi", "m_y_lo", "m_conv")
        S0, S1, PT0, PT1, Y, YT = 2, 3, 4, 5, 6, 7

        def mix_pieces(m, s):
            w = a["w_in"]
            col = lambda c: m * P + c
            if s == 3:
                return pairs(w, m * 2 * P + GA0)
            return halves(w, *((col(2 * ATT), col(0)), (col(ATT), col(CC0)), (col(CU0), col(CB0)))[s])

        def mix_sync(sp):
            def pair(m):
                for s in range(4):
                    if isinstance(m, int) and (m, s) == (0, 0):
                        continue
                    load_slot(sp, G_MIX + 4 * m + s, (G_MIX + s) % 2, mix_pieces(m, s))
                    if isinstance(m, int) and s == 2:
                        forget_sync(sp)
            pair(0)
            with sp.Fori(1, 4) as m:
                pair(m)

        def scores(pe, m, u):
            n = (u + 1) * P
            if u == 0:
                pe.wait_ge(M["m_qk"], 2 * m + 2)
            if not (isinstance(m, int) and m == 0 and u == 0):
                pe.wait_ge(M["m_logits"], 4 * m + u)
            for h in range(2):
                r = slice(64 * h, 64 * h + 64)
                done = pe.matmul(psum[:, S0 + h, 0:n], q_t[r, u * P:(u + 1) * P], k_t[r, 0:n],
                                 start=True, stop=True)
            done.then_inc(M["m_scores"], 1)

        def turn_prob(pe, m, u):
            pe.wait_ge(M["m_prob"], 4 * m + u + 1)
            if not (isinstance(m, int) and m == 0 and u == 0):
                pe.wait_ge(M["m_prob_copied"], 4 * m + u)
            for h in range(2):
                for b in range(u + 1):
                    done = pe.transpose(psum[:, PT0 + h, b * P:(b + 1) * P], prob[:, h, b * P:(b + 1) * P], ident)
            done.then_inc(M["m_prob_t"], 1)

        def prob_v(pe, m, u):
            pe.wait_ge(M["m_prob_copied"], 4 * m + u + 1)
            if u == 0:
                pe.wait_ge(M["m_v_tok"], m + 1)
            if not (isinstance(m, int) and m == 0 and u == 0):
                pe.wait_ge(M["m_y_tok"], 4 * m + u)
            for h in range(2):
                for b in range(u + 1):
                    done = pe.matmul(psum[:, Y, 64 * h:64 * h + 64], prob_t[:, h, b * P:(b + 1) * P],
                                     v_tok[:, b, 64 * h:64 * h + 64], start=(b == 0), stop=(b == u))
            done.then_inc(M["m_y"], 1)

        def turn_y(pe, m, u):
            pe.wait_ge(M["m_y_tok"], 4 * m + u + 1)
            pe.wait_ge(M["m_y_lo"], 4 * m + u + 1)
            pe.transpose(psum[:, YT, 0:P], y_tok[:, :], ident).then_inc(M["m_y_turned"], 1)

        def mix_tensor(pe):
            forget_tensor(pe)

            def after(p):
                def t0():
                    turn_y(pe, p, 0)
                    prob_v(pe, p, 1)
                    turn_prob(pe, p, 2)
                    scores(pe, p, 3)

                def t1():
                    turn_y(pe, p, 1)
                    prob_v(pe, p, 2)
                    turn_prob(pe, p, 3)

                def t2():
                    turn_y(pe, p, 2)
                    prob_v(pe, p, 3)

                def t3():
                    turn_y(pe, p, 3)
                return t0, t1, t2, t3

            def pair(m, rest):
                g, j = G_MIX + 4 * m, G_MIX % 2
                rest[0]()
                if rest[0] is not nothing:
                    pe.wait_ge(G["lo_ready"], g + 1)
                    pe.wait_ge(M["m_ga"], 2 * m - 1)
                    half_slot(pe, j, 0, of_halves, 0)
                rest[1]()
                if rest[0] is not nothing:
                    pe.wait_ge(M["m_ga"], 2 * m)
                half_slot(pe, j, 1, of_halves, 1)
                rest[2]()
                pe.wait_ge(M["m_v_raw"], m + 1)
                for i in range(NT):
                    done = pe.transpose(psum[:, S0, i * P:(i + 1) * P], v_raw[:, i * P:(i + 1) * P], ident)
                done.then_inc(M["m_v_turned"], 1)
                if rest[0] is nothing:
                    forget_turn(pe)
                pe.wait_ge(G["lo_ready"], g + 2)
                half_slot(pe, 1 - j, 0, of_halves, 0)
                rest[3]()
                pe.wait_ge(M["m_sq"], 2 * m + 1)
                pe.wait_ge(M["m_v_tok"], m + 1)
                pe.matmul(psum[:, S0, :], head_blocks, sq[:, 0, :], start=True, stop=True).then_inc(M["m_mean"], 1)
                pe.wait_ge(M["m_q_raw"], m + 1)
                half_slot(pe, 1 - j, 1, of_halves, 1)
                if rest[0] is nothing:
                    pe.wait_ge(FG["c_col"], 1)
                pe.wait_ge(M["m_sq"], 2 * m + 2)
                pe.matmul(psum[:, S1, :], head_blocks, sq[:, 1, :], start=True, stop=True).then_inc(M["m_mean"], 1)
                pe.wait_ge(G["lo_ready"], g + 3)
                pe.wait_ge(M["m_k_raw"], m + 1)
                half_slot(pe, j, 0, of_halves, 0)
                scores(pe, m, 0)
                pe.wait_ge(M["m_cc_raw"], m + 1)
                half_slot(pe, j, 1, of_halves, 1)
                turn_prob(pe, m, 0)
                scores(pe, m, 1)
                pe.wait_ge(G["lo_ready"], g + 4)
                pe.wait_ge(M["m_u"], m + 1)
                half_slot(pe, 1 - j, 0, of_pairs, 0)
                prob_v(pe, m, 0)
                turn_prob(pe, m, 1)
                scores(pe, m, 2)
                pe.wait_ge(M["m_yc"], m + 1)
                half_slot(pe, 1 - j, 1, of_pairs, 1)

            pair(0, (nothing,) * 4)
            with pe.Fori(1, 4) as m:
                pair(m, after(m - 1))
            return after(3)

        def mix_scalar(act):
            def exps(m, u):
                n = (u + 1) * P
                act.wait_ge(M["m_max"], 4 * m + u + 1)
                for h in range(2):
                    done = act.activation(prob[:, h, 0:n], prob[:, h, 0:n], ACT.Exp, bias=neg_max[:, u, h:h + 1],
                                          accum_out=row_sum[:, u, h:h + 1])
                done.then_inc(M["m_prob"], 1)

            def copy_prob(m, u):
                n = (u + 1) * P
                act.wait_ge(M["m_prob_t"], 4 * m + u + 1)
                if not (isinstance(m, int) and m == 0 and u == 0):
                    act.wait_ge(M["m_y"], 4 * m + u)
                act.activation(prob_t[:, :, 0:n], psum[:, PT0:PT0 + 2, 0:n], ACT.Copy).then_inc(M["m_prob_copied"], 1)

            def y_hi(m, u):
                act.wait_ge(M["m_y_turned"], 4 * m + u + 1)
                act.activation(d_hi[:, bass.ds(m, 1), u * P:(u + 1) * P], psum[:, YT:YT + 1, 0:P], ACT.Copy)\
                   .then_inc(M["m_y_hi"], 1)

            def sig_ga(m, i):
                act.wait_ge(G["chunk_done"], 2 * (G_MIX + 4 * m + 3) + i + 1)
                act.activation(ga[:, bass.ds(2 * m + i, 1), :], psum[:, i:i + 1, :], ACT.Sigmoid).then_inc(M["m_ga"], 1)

            def r_qk(m, i, bank):
                r = (rstd, ss)[i]
                act.wait_ge(M["m_mean"], 2 * m + i + 1)
                act.activation(r[:, :], psum[:, bank, :], ACT.Ln, bias=eps[:, 0:1], scale=1.0 / HEAD_DIM)\
                   .then_inc(M["m_ln"], 1)
                act.wait_ge(M["m_ln"], 2 * m + i + 1)
                act.activation(r[:, :], r[:, :], ACT.Exp, scale=-0.5).then_inc(M["m_r"], 1)

            def after(p):
                def t0():
                    y_hi(p, 0)
                    copy_prob(p, 2)
                    exps(p, 3)

                def t1():
                    y_hi(p, 1)
                    copy_prob(p, 3)

                def t2():
                    y_hi(p, 2)

                def t3():
                    y_hi(p, 3)
                return t0, t1, t2, t3

            def pair(m, rest):
                g, j = G_MIX + 4 * m, G_MIX % 2
                if rest[0] is not nothing:
                    sig_ga(m - 1, 1)
                    split_hi(act, g + 1, 1 - j)
                rest[0]()
                act.wait_ge(G["chunk_done"], 2 * g + 1)
                if rest[0] is nothing:
                    act.wait_ge(G["x_ready"], 1)
                act.activation(v_raw[:, :], psum[:, 0, :], ACT.Copy).then_inc(M["m_v_raw"], 1)
                rest[1]()
                act.wait_ge(G["chunk_done"], 2 * g + 2)
                act.activation(q_raw[:, :], psum[:, 1, :], ACT.Copy).then_inc(M["m_q_raw"], 1)
                split_hi(act, g + 2, j)
                if rest[0] is nothing:
                    act.wait_ge(FG["c_row"], 1)
                act.wait_ge(M["m_q_raw"], m + 1)
                act.activation(sq[:, 0, :], q_raw[:, :], ACT.Square).then_inc(M["m_sq"], 1)
                rest[2]()
                act.wait_ge(G["chunk_done"], 2 * g + 3)
                act.activation(k_raw[:, :], psum[:, 0, :], ACT.Copy).then_inc(M["m_k_raw"], 1)
                act.wait_ge(M["m_k_raw"], m + 1)
                act.activation(sq[:, 1, :], k_raw[:, :], ACT.Square).then_inc(M["m_sq"], 1)
                rest[3]()
                r_qk(m, 0, S0)
                act.wait_ge(G["chunk_done"], 2 * g + 4)
                act.wait_ge(M["m_v_turned"], m + 1)
                act.activation(v_raw[:, :], psum[:, 1, :], ACT.Copy).then_inc(M["m_cc_raw"], 1)
                split_hi(act, g + 3, 1 - j)
                r_qk(m, 1, S1)
                exps(m, 0)
                copy_prob(m, 0)
                exps(m, 1)
                split_hi(act, g + 4, j)
                act.wait_ge(M["m_yc"], m + 1)
                act.activation(d_hi[:, bass.ds(4 + m, 1), :], pre[:, 0:1, :], ACT.Copy).then_inc(M["m_yc_hi"], 1)
                copy_prob(m, 1)
                exps(m, 2)
                sig_ga(m, 0)

            pair(0, (nothing,) * 4)
            with act.Fori(1, 4) as m:
                pair(m, after(m - 1))
            sig_ga(3, 1)
            return after(3)

        def mix_vector(dve):
            forget_vector(dve)

            def soften(m, u):
                n = (u + 1) * P
                dve.wait_ge(M["m_scores"], 4 * m + u + 1)
                dve.wait_ge(M["m_bias"], 8 * m + 2 * u + 2)
                if not (isinstance(m, int) and m == 0 and u == 0):
                    dve.wait_ge(M["m_prob_t"], 4 * m + u)
                dve.scalar_tensor_tensor(out=prob[:, :, 0:n], in0=psum[:, S0:S0 + 2, 0:n], scalar=HEAD_DIM ** -0.5,
                                         in1=bias_qk[:, :, 0:n], op0=ALU.mult, op1=ALU.add).then_inc(M["m_logits"], 1)
                dve.wait_ge(M["m_logits"], 4 * m + u + 1)
                dve.tensor_reduce(neg_max[:, u, :], prob[:, :, 0:n], AX.X, ALU.max, negate=True).then_inc(M["m_max"], 1)

            def invert(m, u):
                dve.wait_ge(M["m_prob"], 4 * m + u + 1)
                dve.reciprocal(row_inv[:, u, :], row_sum[:, u, :]).then_inc(M["m_inv"], 1)

            def y_norm(m, u):
                dve.wait_ge(M["m_y"], 4 * m + u + 1)
                dve.wait_ge(M["m_inv"], 4 * m + u + 1)
                if not (isinstance(m, int) and m == 0 and u == 0):
                    dve.wait_ge(M["m_y_turned"], 4 * m + u)
                for h in range(2):
                    done = dve.tensor_scalar(y_tok[:, 64 * h:64 * h + 64], psum[:, Y, 64 * h:64 * h + 64],
                                             row_inv[:, u, h:h + 1], None, ALU.mult)
                done.then_inc(M["m_y_tok"], 1)

            def y_lo(m, u):
                dve.wait_ge(M["m_y_hi"], 4 * m + u + 1)
                block = d_hi[:, bass.ds(m, 1), u * P:(u + 1) * P].bitcast(F32)
                dve.tensor_tensor(d_lo[:, bass.ds(m, 1), u * P:(u + 1) * P], psum[:, YT:YT + 1, 0:P], block,
                                  ALU.subtract).then_inc(M["m_y_lo"], 1)

            def after(p):
                def t0():
                    y_lo(p, 0)
                    y_norm(p, 1)
                    soften(p, 3)
                    invert(p, 2)

                def t1():
                    y_lo(p, 1)
                    y_norm(p, 2)
                    invert(p, 3)

                def t2():
                    y_lo(p, 2)
                    y_norm(p, 3)

                def t3():
                    y_lo(p, 3)
                return t0, t1, t2, t3

            def normed(m, i):
                src, dst, r, col = ((q_raw, q_t, rstd, V_QG), (k_raw, k_t, ss, V_KG))[i]
                dve.wait_ge(M["m_r"], 2 * m + i + 1)
                dve.scalar_tensor_tensor(out=dst[:, :], in0=src[:, :], scalar=vec[:, col:col + 1], in1=r[:, :],
                                         op0=ALU.mult, op1=ALU.mult).then_inc(M["m_qk"], 1)

            def pair(m, rest):
                g, j = G_MIX + 4 * m, G_MIX % 2
                if rest[0] is not nothing:
                    split_lo(dve, g + 1, 1 - j)
                rest[0]()
                rest[1]()
                split_lo(dve, g + 2, j)
                rest[2]()
                dve.wait_ge(M["m_v_turned"], m + 1)
                dve.tensor_copy(v_tok[:, :, :], psum[:, S0, :].rearrange("p (i n) -> p i n", n=P))\
                   .then_inc(M["m_v_tok"], 1)
                rest[3]()
                normed(m, 0)
                split_lo(dve, g + 3, 1 - j)
                normed(m, 1)
                dve.wait_ge(G["chunk_done"], 2 * g + 5)
                dve.wait_ge(M["m_cc_raw"], m + 1)
                dve.tensor_tensor(u_pad[:, 2:2 + T], v_raw[:, :], psum[:, 0, :], ALU.mult).then_inc(M["m_u"], 1)
                soften(m, 0)
                dve.wait_ge(M["m_u"], m + 1)
                taps = conv_taps
                dve.tensor_scalar(pre[:, 1, :], u_pad[:, 0:T], taps(m, 0), None, ALU.mult).then_inc(M["m_conv"], 1)
                for i in (1, 2):
                    dve.wait_ge(M["m_conv"], 3 * m + i)
                    dve.scalar_tensor_tensor(out=pre[:, 1, :], in0=u_pad[:, i:i + T], scalar=taps(m, i),
                                             in1=pre[:, 1, :], op0=ALU.mult, op1=ALU.add).then_inc(M["m_conv"], 1)
                soften(m, 1)
                dve.wait_ge(G["chunk_done"], 2 * g + 6)
                dve.wait_ge(M["m_conv"], 3 * m + 3)
                dve.tensor_tensor(pre[:, 0, :], pre[:, 1, :], psum[:, 1, :], ALU.mult).then_inc(M["m_yc"], 1)
                split_lo(dve, g + 4, j)
                invert(m, 0)
                dve.wait_ge(M["m_yc_hi"], m + 1)
                dve.tensor_tensor(d_lo[:, bass.ds(4 + m, 1), :], pre[:, 0:1, :],
                                  d_hi[:, bass.ds(4 + m, 1), :].bitcast(F32), ALU.subtract).then_inc(M["m_yc_lo"], 1)
                y_norm(m, 0)
                soften(m, 2)
                invert(m, 1)

            pair(0, (nothing,) * 4)
            with dve.Fori(1, 4) as m:
                pair(m, after(m - 1))
            return after(3)

        def conv_taps(m, i):
            return vec[:, bass.ds(V_CONV + 4 * i + m, 1)]

        def mix_gpsimd(pool):
            pool.wait_ge(FG["c_col"], 1)
            pool.wait_ge(FG["c_all"], 32)

            def pair(m):
                for u in range(NT):
                    n = (u + 1) * P
                    if not (isinstance(m, int) and m == 0 and u == 0):
                        pool.wait_ge(M["m_logits"], 4 * m + u)
                    pool.tensor_tensor(bias_qk[:, :, 0:n],
                                       c_col[:, u, bass.ds(2 * m, 2)].rearrange("p (h o) -> p h o", o=1)
                                       .to_broadcast([P, 2, n]),
                                       c_all[:, bass.ds(2 * m, 2), 0:n], ALU.subtract).then_inc(M["m_bias"], 1)
                    pool.wait_ge(M["m_bias"], 8 * m + 2 * u + 1)
                    pool.affine_select(out=bias_qk[:, :, u * P:n], in_=bias_qk[:, :, u * P:n], compare_op=ALU.is_ge,
                                       fill=NEG_INF, base=0, pattern=[[0, 2], [-1, P]], channel_multiplier=1)\
                        .then_inc(M["m_bias"], 1)

            for m in range(4):
                pair(m)

        MG = semaphores("g_gb", "g_terms", "g_sum", "g_hi", "g_lo")

        def merge_sync(sp):
            with sp.Fori(0, 4) as m:
                load_slot(sp, G_MERGE + 2 * m, G_MERGE % 2, pairs(a["w_in"], m * 2 * P + GB0))
                load_slot(sp, G_MERGE + 2 * m + 1, 1 - G_MERGE % 2,
                          pairs(a["w_out_att"], m * P * 2) + pairs(a["w_out_conv"], m * P * 2, 8))

        def merge_tensor(pe, rest):
            j = G_MERGE % 2

            def step(m, later):
                g = G_MERGE + 2 * m
                if not later:
                    rest[0]()
                pe.wait_ge(G["lo_ready"], g + 1)
                if later:
                    pe.wait_ge(MG["g_gb"], 2 * m)
                else:
                    pe.wait_ge(M["m_ga"], 8)
                for half in range(2):
                    half_slot(pe, j, half, of_pairs, half)
                    if not later:
                        rest[1 + half]()
                if later:
                    pe.wait_ge(MG["g_sum"], 2 * m)
                else:
                    rest[3]()
                    pe.wait_ge(M["m_y_lo"], 17)
                    pe.wait_ge(M["m_yc_lo"], 4)
                pe.wait_ge(G["lo_ready"], g + 2)
                for half in range(2):
                    for part in range(2):
                        for k in range(4):
                            t, c = of_pairs(half, 4 * part + k), 4 * part + k
                            to = psum[:, 4 + 2 * part + half, :]
                            pe.matmul(to, w_hi[1 - j][:, t, :], d_hi[:, c, :], start=(k == 0), stop=False)
                            pe.matmul(to, w_hi[1 - j][:, t, :], d_lo[:, c, :], start=False, stop=False)
                            done = pe.matmul(to, w_lo[1 - j][:, t, :], d_hi[:, c, :], start=False, stop=(k == 3))
                    done.then_inc(G["chunk_done"], 1)

            step(0, False)
            with pe.Fori(1, 4) as m:
                step(m, True)

        def merge_scalar(act, rest):
            j = G_MERGE % 2

            def step(m, later):
                g = G_MERGE + 2 * m
                if not later:
                    rest[0]()
                split_hi(act, g + 1, 1 - j)
                for i in range(2):
                    if not later:
                        rest[1 + i]()
                    act.wait_ge(G["chunk_done"], 2 * g + i + 1)
                    if later:
                        act.wait_ge(MG["g_lo"], 2 * m + i - 1)
                    act.activation(gb[:, i, :], psum[:, i, :], ACT.Sigmoid).then_inc(MG["g_gb"], 1)
                if not later:
                    rest[3]()
                split_hi(act, g + 2, j)
                for i in range(2):
                    act.wait_ge(MG["g_sum"], 2 * m + i + 1)
                    act.activation(m_hi[:, bass.ds(2 * m + i, 1), :], gb[:, i:i + 1, :], ACT.Copy)\
                       .then_inc(MG["g_hi"], 1)

            step(0, False)
            with act.Fori(1, 4) as m:
                step(m, True)

        def merge_vector(dve, rest):
            j = G_MERGE % 2

            def step(m, later):
                g = G_MERGE + 2 * m
                if not later:
                    rest[0]()
                split_lo(dve, g + 1, 1 - j)
                if not later:
                    for left in rest[1:]:
                        left()
                split_lo(dve, g + 2, j)
                for i in range(2):
                    dve.wait_ge(G["chunk_done"], 2 * g + i + 3)
                    dve.wait_ge(MG["g_gb"], 2 * m + i + 1)
                    dve.tensor_tensor(gb[:, i, :], gb[:, i, :], psum[:, 6 + i, :], ALU.mult).then_inc(MG["g_terms"], 1)
                    dve.tensor_tensor(sq[:, i:i + 1, :], ga[:, bass.ds(2 * m + i, 1), :], psum[:, 4 + i:5 + i, :],
                                      ALU.mult).then_inc(MG["g_terms"], 1)
                    dve.wait_ge(MG["g_terms"], 4 * m + 2 * i + 2)
                    dve.tensor_tensor(gb[:, i, :], gb[:, i, :], sq[:, i, :], ALU.add).then_inc(MG["g_sum"], 1)
                    dve.wait_ge(MG["g_hi"], 2 * m + i + 1)
                    dve.tensor_tensor(m_lo[:, bass.ds(2 * m + i, 1), :], gb[:, i:i + 1, :],
                                      m_hi[:, bass.ds(2 * m + i, 1), :].bitcast(F32), ALU.subtract)\
                       .then_inc(MG["g_lo"], 1)

            step(0, False)
            with dve.Fori(1, 4) as m:
                step(m, True)

        def add_tensor(pe, g0, j0, r, hi, lo, chunks, ready, count, free):
            for s in range(4):
                if s >= 2:
                    pe.wait_ge(G["x_ready"], 8 * r + 2 * s - 2)
                else:
                    free(s)
                if s < 3:
                    whole_slot(pe, g0 + s, (j0 + s) % 2, of_pairs, hi, lo, chunks,
                               ready if s == 0 else None, count)
                else:
                    last_slot(pe, g0 + s, (j0 + s) % 2, hi, lo, chunks)

        def last_slot(pe, g, j, hi, lo, chunks=KC):
            pe.wait_ge(G["lo_ready"], g + 1)
            for half in range(2):
                for k in range(chunks):
                    done = product(pe, psum[:, 2 * j + half, :], j, of_pairs(half, k), hi, lo, k, k == chunks - 1)
                done.then_inc(G["chunk_done"], 1)

        def add_scalar(act, g0, j0, r, tiles=(16,) * 4, between={}):
            for s in range(4):
                if tiles[s]:
                    split_hi(act, g0 + s + 1, (j0 + s + 1) % 2, tiles[s])
                if s in between:
                    between[s]()
                for i in range(2):
                    square(act, r, 2 * s + i)

        def add_vector(dve, g0, j0, r, norms, by=None, tiles=(16,) * 4, between={}):
            for s in range(4):
                if tiles[s]:
                    split_lo(dve, g0 + s + 1, (j0 + s + 1) % 2, tiles[s])
                if s in between:
                    between[s]()
                for i in range(2):
                    c = 2 * s + i
                    bank = psum[:, 2 * ((j0 + s) % 2) + i, :]
                    if c == 7:
                        add_square(dve, r, 6, norms)
                    dve.wait_ge(G["chunk_done"], 2 * (g0 + s) + i + 1)
                    if by is None:
                        ins = dve.tensor_tensor(x[:, c, :], x[:, c, :], bank, ALU.add)
                    else:
                        ins = dve.scalar_tensor_tensor(out=x[:, c, :], in0=bank, scalar=by(c), in1=x[:, c, :],
                                                       op0=ALU.mult, op1=ALU.add)
                    ins.then_inc(G["x_ready"], 1)
                for i in range(s // 3, 2):
                    add_square(dve, r, 2 * s + i, norms)

        L = semaphores("p_in", "turned", "p_hi", "p_lo", "p_done", "pg_sig", "pg_gated",
                       "p_bank", "ctx_in", "ctx_copied", "ctx_sq", "ctx_mean", "ctx_rstd",
                       "ctx_pre", "ctx_hi", "ctx_lo", "gains")

        def wo_sync(sp):
            for s in range(4):
                load_slot(sp, G_WO + s, (G_WO + s) % 2, pairs(a["w_o"], s * 2 * P))
                if s == 1:
                    sp.wait_ge(MG["g_lo"], 8)
                    sp.dma_start(p_in[:, :, :], a["p"].rearrange("(i p) n -> p i n", p=P)).then_inc(L["p_in"], 16)
                    route_load(sp)

        def wo_tensor(pe):
            def free(s):
                if s == 0:
                    return
                pe.wait_ge(MG["g_sum"], 8)
                pe.wait_ge(L["p_in"], 16)
                for k in range(2):
                    for i in range(NT):
                        done = pe.transpose(psum[:, 4 + k, i * P:(i + 1) * P], p_in[:, i, k * P:(k + 1) * P], ident)
                done.then_inc(L["turned"], 1)
            add_tensor(pe, G_WO, G_WO % 2, R_WO, m_hi, m_lo, KC, MG["g_lo"], 0, free)

        def wo_scalar(act):
            def split_p():
                act.wait_ge(L["turned"], 1)
                act.activation(p_hi[:, :, :], psum[:, 4:6, :], ACT.Copy).then_inc(L["p_hi"], 1)

            def split_route():
                act.wait_ge(E["e_wr"], 64)
                act.wait_ge(E["e_iota"], 1)
                act.activation(wr_hi[:, :, :], wr_raw[:, :, :], ACT.Copy).then_inc(E["e_wr_hi"], 1)
            add_scalar(act, G_WO, G_WO % 2, R_WO, between={2: split_p, 3: split_route})

        def wo_vector(dve):
            def split_p():
                dve.wait_ge(L["p_hi"], 1)
                dve.tensor_tensor(p_lo[:, :, :], psum[:, 4:6, :], p_hi[:, :, :].bitcast(F32), ALU.subtract)\
                   .then_inc(L["p_lo"], 1)

            def split_route():
                dve.wait_ge(E["e_wr_hi"], 1)
                dve.tensor_tensor(wr_lo[:, :, :], wr_raw[:, :, :], wr_hi[:, :, :].bitcast(F32), ALU.subtract)\
                   .then_inc(E["e_wr_lo"], 1)
            add_vector(dve, G_WO, G_WO % 2, R_WO, N_ATT + 1, between={2: split_p, 3: split_route})

        EMBED_BANKS = (4, 5, 6, 0, 1, 2, 3, 4)

        def embed_sync(sp):
            load_slot(sp, G_PLE, G_PLE % 2, [(0, 16, D, a["w_ple"].rearrange("(k p) n -> p k n", p=P))])

        def embed_tensor(pe):
            for c in range(KC):
                if c == 0:
                    pe.wait_ge(L["p_lo"], 1)
                    pe.wait_ge(G["lo_ready"], G_PLE + 1)
                if c == 3:
                    norm_mean(pe, N_MOE)
                    pe.wait_ge(G["x_ready"], 8 * R_WO + 8)
                if c == 7:
                    pe.wait_ge(L["p_done"], 1)
                for k in range(2):
                    done = product(pe, psum[:, EMBED_BANKS[c], :], G_PLE % 2, 8 * k + c, p_hi, p_lo, k, k == 1)
                done.then_inc(G["chunk_done"], 1) if c in (3, 7) else done.then_inc(L["p_bank"], 1)

        def copy_embedded(act, c):
            act.wait_ge(*((G["chunk_done"], 2 * G_PLE + 1 + c // 4) if c in (3, 7) else (L["p_bank"], c + 1 - c // 4)))
            act.activation(pl[:, c, :], psum[:, EMBED_BANKS[c], :], ACT.Copy).then_inc(L["p_done"], 1)

        def embed_scalar(act):
            split_hi(act, G_MOE, G_MOE % 2)
            norm_rstd(act, N_MOE)
            norm_hi(act, N_MOE, between=lambda c: copy_embedded(act, c))

        def embed_vector(dve):
            split_lo(dve, G_MOE, G_MOE % 2)
            norm_dve(dve, N_MOE, lambda c: vec[:, V_FFN_G + c:V_FFN_G + c + 1])

        E = semaphores("e_wr", "e_wr_hi", "e_wr_lo", "e_iota", "e_logits", "e_rows", "e_turned", "e_chain", "e_shift",
                       "e_exp", "e_comb", "e_comb_in", "e_silu", "e_up", "e_hid", "e_hi", "e_lo", "m2_in0",
                       "m2_in1", "m2_sum", "m2_ctx", "m2_used", "e_silu_c")
        w_gate = a["w_gate"].rearrange("e d f -> (e d) f")
        w_up = a["w_up"].rearrange("e d f -> (e d) f")
        w_down = a["w_down"].rearrange("e f d -> (e f) d")
        CTX_BLOCKS = 8

        def block_at(q, s):
            if isinstance(q, int):
                return s - 2 if 2 <= s <= 10 else None
            return 5 * q + 4 + s // 2 if s in (1, 3, 5, 7, 9) else None

        def buffer_of(n):
            return n % 2 if isinstance(n, int) else 0

        def block_in(n):
            if isinstance(n, int):
                return E[("m2_in0", "m2_in1")[n % 2]], 16 * (n // 2) + 16
            return E["m2_in0"], 16 * (n - 8) + 80

        def has_ctx(n):
            return isinstance(n, int) and n < CTX_BLOCKS

        def route_load(eng):
            for src, c0, n in (("w_rg", 0, GROUPS), ("w_re", GROUPS, EXPERTS)):
                with nc.allow_non_contiguous_dma(reason="a few columns of weights"):
                    eng.dma_start(wr_raw[:, :, c0:c0 + n], a[src].rearrange("(k p) n -> p k n", p=P))\
                       .then_inc(E["e_wr"], 16)
            for src, c0, n in (("b_rg", 0, GROUPS), ("b_re", GROUPS, EXPERTS)):
                eng.dma_start(b_route[:, c0:c0 + n], a[src].rearrange("(o n) -> o n", o=1).to_broadcast([P, n]))\
                   .then_inc(E["e_wr"], 16)

        def moe_sync(sp):
            j0 = G_MOE % 2

            def group(q):
                g = G_MOE + 12 * q
                for s in range(12):
                    if s < 8:
                        rows = bass.ds(q * 4096 + (s // 2) * D, D)
                        cols = slice((s % 2) * P, (s % 2) * P + P)
                        load_slot(sp, g + s, (j0 + s) % 2,
                                  [(8 * i, 8, P, w[rows, cols].rearrange("(k p) n -> p k n", p=P))
                                   for i, w in enumerate((w_gate, w_up))])
                    else:
                        load_slot(sp, g + s, (j0 + s) % 2,
                                  pairs(w_down[bass.ds(q * D, D), :], (s - 8) * 2 * P))
                    if s == (2 if isinstance(q, int) else 0):
                        if isinstance(q, int):
                            sp.wait_ge(E["e_rows"], 2)
                            sp.dma_start(scratch_comb, comb_row[:, :]).then_inc(E["e_comb_in"], 16)
                            sp.wait_ge(E["e_comb_in"], 16)
                        else:
                            sp.wait_ge(E["e_up"], 8 * q)
                        sp.dma_start(comb_all[:, :, :],
                                     scratch_comb[bass.ds(4 * q, 4), :].rearrange("(o e) t -> o e t", o=1)
                                     .to_broadcast([P, 4, T])).then_inc(E["e_comb_in"], 16)
                    n = block_at(q, s)
                    if n is not None:
                        if isinstance(n, int) and n == 0:
                            sp.wait_ge(G["chunk_done"], 2 * G_PLE + 2)
                        elif not isinstance(n, int) or n >= 2:
                            sp.wait_ge(E["m2_sum"], 8 * n - 8 if isinstance(n, int) else 8 * n)
                            if isinstance(n, int):
                                sp.wait_ge(E["m2_ctx"], 8 * n - 8)
                        sp.dma_start(wm_raw[:, buffer_of(n), :, :], a["w_mod_2"][:, bass.ds(n * 2 * P, 2 * P)]
                                     .rearrange("(k p) n -> p k n", p=P)).then_inc(block_in(n)[0], 16)
            group(0)
            sp.dma_start(ctx_in[:, :, :], a["ctx_2"].rearrange("(i p) n -> p i n", p=P)).then_inc(L["ctx_in"], 16)
            with sp.Fori(1, 4) as q:
                group(q)

        def moe_tensor(pe):
            pe.wait_ge(E["e_wr_lo"], 1)
            pe.wait_ge(L["p_done"], 3)
            for k in range(KC):
                pe.wait_ge(G["h_lo_ready"], 8 * N_MOE + k + 1)
                to = psum[:, 6, :]
                pe.matmul(to, wr_hi[:, k, :], h_hi[:, k, :], start=(k == 0), stop=False)
                pe.matmul(to, wr_hi[:, k, :], h_lo[:, k, :], start=False, stop=False)
                done = pe.matmul(to, wr_lo[:, k, :], h_hi[:, k, :], start=False, stop=(k == KC - 1))
            done.then_inc(E["e_logits"], 1)
            j0 = G_MOE % 2

            def turn_logits():
                pe.wait_ge(E["e_rows"], 1)
                for i in range(NT):
                    done = pe.transpose(psum[:, 5, 32 * i:32 * i + ROUTE], rt_row[:, i * P:(i + 1) * P],
                                        ident[0:ROUTE, 0:ROUTE])
                done.then_inc(E["e_turned"], 1)

            def turn_comb():
                pe.wait_ge(E["e_comb"], 1)
                for i in range(NT):
                    done = pe.transpose(psum[0:EXPERTS, 4, i * P:(i + 1) * P], comb[:, i, :], ident)
                done.then_inc(E["e_turned"], 1)

            def sum_block(q, s):
                n = block_at(q, s)
                if n is None:
                    return
                pe.wait_ge(E["m2_sum"], 8 * n + 8)
                if has_ctx(n):
                    pe.wait_ge(E["m2_ctx"], 8 * n + 8)
                for v in range(2 if has_ctx(n) else 1):
                    for half in range(2):
                        done = pe.matmul(psum[:, 6, bass.ds(48 * v + 2 * n + half, 1)],
                                         wm_sum[:, buffer_of(n), v, half * P:(half + 1) * P], ones[:, 0:1],
                                         start=True, stop=True)
                done.then_inc(E["m2_used"], 1)

            def group(q):
                g, r = G_MOE + 12 * q, R_MOE + q
                for s in range(8):
                    if s >= 2:
                        pe.wait_ge(E["e_silu"], 8 * q + s - 1)
                        pe.wait_ge(E["e_up"], 8 * q + s - 1)
                    elif not isinstance(q, int):
                        pe.wait_ge(G["x_ready"], 8 * r - 2 + 2 * s)
                    if isinstance(q, int) and s < 2:
                        pe.wait_ge(L["p_done"], 8)
                        pe.wait_ge(G["lo_ready"], g + s + 1)
                        j = (j0 + s) % 2
                        half_slot(pe, j, 0, of_halves, 2 * j, between=turn_comb if s else turn_logits)
                        half_slot(pe, j, 1, of_halves, 2 * j + 1)
                    else:
                        whole_slot(pe, g + s, (j0 + s) % 2, of_halves, h_hi, h_lo)
                    sum_block(q, s - 1)
                for s in range(4):
                    if s >= 2:
                        pe.wait_ge(G["x_ready"], 8 * r + 2 * s - 2)
                    else:
                        pe.wait_ge(E["e_silu"], 8 * q + 7 + s)
                        pe.wait_ge(E["e_up"], 8 * q + 7 + s)
                    if s < 3:
                        whole_slot(pe, g + 8 + s, (j0 + s) % 2, of_pairs, d_hi, d_lo, KC,
                                   E["e_lo"] if s == 0 else None, 8 * q)
                    else:
                        last_slot(pe, g + 8 + s, (j0 + s) % 2, d_hi, d_lo)
                    sum_block(q, 7 + s)
            group(0)
            with pe.Fori(1, 4) as q:
                group(q)

        def moe_scalar(act):
            j0 = G_MOE % 2
            split_hi(act, G_MOE + 1, (j0 + 1) % 2)
            for n in range(2):
                act.wait_ge(E["e_shift"], n + 1)
                act.activation(r4[:, n, :, :], r4[:, n, :, :], ACT.Exp).then_inc(E["e_exp"], 1)
            for v in range(2):
                act.activation(silu_c[:, :, v:v + 1], vec[:, V_C + 8 * v:V_C + 8 * v + 8]
                               .rearrange("p (k o) -> p k o", o=1), ACT.Silu).then_inc(E["e_silu_c"], 1)
            split_hi(act, G_MOE + 2, j0)

            def group(q):
                g, r = G_MOE + 12 * q, R_MOE + q
                for s in range(8):
                    if s >= 2 or not isinstance(q, int):
                        split_hi(act, g + s + 1, (j0 + s + 1) % 2)
                    act.wait_ge(G["chunk_done"], 2 * (g + s) + 1)
                    act.activation(act_u[:, s % 2, :], psum[:, 2 * ((j0 + s) % 2), :], ACT.Silu)\
                       .then_inc(E["e_silu"], 1)
                    act.wait_ge(E["e_hid"], 8 * q + s + 1)
                    act.activation(d_hi[:, s, :], pre[:, s % 2, :], ACT.Copy).then_inc(E["e_hi"], 1)
                add_scalar(act, g + 8, j0, r)
            group(0)
            with act.Fori(1, 4) as q:
                group(q)

        def accumulate(dve, n):
            if n is None:
                return
            dve.wait_ge(*block_in(n))
            if isinstance(n, int) and n == 0:
                dve.wait_ge(E["e_silu_c"], 2)
            elif not isinstance(n, int) or n >= 2:
                dve.wait_ge(E["m2_used"], n - 1 if isinstance(n, int) else n)
            for k in range(KC):
                for v in ((1, 0) if has_ctx(n) else (0,)):
                    count, total = E[("m2_sum", "m2_ctx")[v]], wm_sum[:, buffer_of(n), v, :]
                    w, c = wm_raw[:, buffer_of(n), k, :], silu_c[:, k, v:v + 1]
                    if k == 0:
                        ins = dve.tensor_scalar(total, w, c, None, ALU.mult)
                    else:
                        dve.wait_ge(count, 8 * n + k)
                        ins = dve.scalar_tensor_tensor(out=total, in0=w, scalar=c, in1=total, op0=ALU.mult,
                                                       op1=ALU.add)
                    ins.then_inc(count, 1)

        def moe_vector(dve):
            j0 = G_MOE % 2
            dve.wait_ge(E["e_logits"], 1)
            dve.tensor_copy(rt_row[:, :], psum[0:ROUTE, 6, :]).then_inc(E["e_rows"], 1)
            split_lo(dve, G_MOE + 1, (j0 + 1) % 2)
            route(dve)
            dve.wait_ge(E["e_turned"], 2)
            dve.tensor_copy(comb_row[:, :], psum[0:EXPERTS, 4, :]).then_inc(E["e_rows"], 1)
            split_lo(dve, G_MOE + 2, j0)

            def group(q):
                g, r = G_MOE + 12 * q, R_MOE + q
                for s in range(8):
                    if not isinstance(q, int):
                        if s == 0:
                            dve.wait_ge(G["lo_ready"], g + 1)
                        split_lo(dve, g + s + 1, (j0 + s + 1) % 2)
                    accumulate(dve, block_at(q, s))
                    if s == 0:
                        dve.wait_ge(E["e_comb_in"], 16 * q + 32)
                    dve.wait_ge(G["chunk_done"], 2 * (g + s) + 2)
                    bank = 2 * ((j0 + s) % 2) + 1
                    dve.tensor_tensor(pre[:, s % 2, :], comb_all[:, s // 2, :], psum[:, bank, :],
                                      ALU.mult).then_inc(E["e_up"], 1)
                    dve.wait_ge(E["e_up"], 8 * q + s + 1)
                    dve.wait_ge(E["e_silu"], 8 * q + s + 1)
                    dve.tensor_tensor(pre[:, s % 2, :], pre[:, s % 2, :], act_u[:, s % 2, :], ALU.mult)\
                       .then_inc(E["e_hid"], 1)
                    dve.wait_ge(E["e_hi"], 8 * q + s + 1)
                    dve.tensor_tensor(d_lo[:, s, :], pre[:, s % 2, :], d_hi[:, s, :].bitcast(F32), ALU.subtract)\
                       .then_inc(E["e_lo"], 1)

                add_vector(dve, g + 8, j0, r, N_MOE + 1, tiles=(0 if isinstance(q, int) else 16,) * 4,
                           between={s: lambda s=s: accumulate(dve, block_at(q, 8 + s)) for s in range(4)})
            group(0)
            with dve.Fori(1, 4) as q:
                group(q)

        def route(dve):
            n = [0]

            def step(ins):
                n[0] += 1
                ins.then_inc(E["e_chain"], 1)
                dve.wait_ge(E["e_chain"], n[0])

            def wide(v):
                return v.rearrange("p (i o) -> p i o", o=1).to_broadcast([P, NT, 4])

            iota = iota4[:, :].rearrange("p (o n) -> p o n", o=1).to_broadcast([P, NT, 4])
            dve.wait_ge(E["e_turned"], 1)
            dve.wait_ge(E["e_iota"], 5)
            step(dve.tensor_tensor(rt[:, :, :], psum[:, 5, 0:P].rearrange("p (i n) -> p i n", n=32)[:, :, 0:20],
                                   b_route[:, :].rearrange("p (o n) -> p o n", o=1).to_broadcast([P, NT, 20]), ALU.add))

            def first_of(values, peak, mask, at, tmp):
                step(dve.tensor_reduce(peak, values, AX.X, ALU.max))
                step(dve.tensor_tensor(tmp, values, wide(peak), ALU.is_lt))
                step(dve.scalar_tensor_tensor(out=tmp, in0=tmp, scalar=64.0, in1=iota, op0=ALU.mult, op1=ALU.add))
                step(dve.tensor_reduce(at, tmp, AX.X, ALU.min))
                step(dve.tensor_tensor(mask, iota, wide(at), ALU.is_equal))

            g_exp, e_exp, g_mask, mask1, mask2, tmp, e_in = (r4[:, i, :, :] for i in range(7))
            g_max, at, g_sum, e_max, top, e_sum = (r1[:, i, :] for i in range(6))
            first_of(rt[:, :, 0:GROUPS], g_max, g_mask, at, tmp)
            dve.tensor_tensor(g_exp, rt[:, :, 0:GROUPS], wide(g_max), ALU.subtract).then_inc(E["e_shift"], 1)
            for e in range(PER_GROUP):
                of_e = rt[:, :, GROUPS:20].rearrange("p i (g e) -> p i g e", g=GROUPS)[:, :, :, e]
                step(dve.tensor_tensor(tmp, of_e, g_mask, ALU.mult))
                step(dve.tensor_reduce(e_in[:, :, e], tmp, AX.X, ALU.add))
            step(dve.tensor_reduce(e_max, e_in, AX.X, ALU.max))
            dve.tensor_tensor(e_exp, e_in, wide(e_max), ALU.subtract).then_inc(E["e_shift"], 1)
            dve.wait_ge(E["e_exp"], 2)
            step(dve.tensor_reduce(g_sum, g_exp, AX.X, ALU.add))
            first_of(e_exp, top, mask1, at, tmp)
            step(dve.scalar_tensor_tensor(out=e_in, in0=mask1, scalar=-2.0, in1=e_exp, op0=ALU.mult, op1=ALU.add))
            first_of(e_in, top, mask2, at, tmp)
            step(dve.tensor_tensor(mask1, mask1, mask2, ALU.add))
            step(dve.tensor_tensor(e_exp, e_exp, mask1, ALU.mult))
            step(dve.tensor_reduce(e_sum, e_exp, AX.X, ALU.add))
            step(dve.tensor_tensor(e_sum, e_sum, g_sum, ALU.mult))
            step(dve.reciprocal(e_sum, e_sum))
            step(dve.tensor_tensor(e_exp, e_exp, wide(e_sum), ALU.mult))
            for q in range(GROUPS):
                done = dve.tensor_tensor(comb[:, :, 4 * q:4 * q + 4], e_exp, wide(g_mask[:, :, q]), ALU.mult)
            done.then_inc(E["e_comb"], 1)

        def moe_gpsimd(pool):
            pool.wait_ge(MG["g_sum"], 8)
            pool.memset(wr_raw[:, :, ROUTE:P], 0.0).then_inc(E["e_iota"], 1)
            pool.wait_ge(G["chunk_done"], 2 * (G_WO + 3) + 2)
            for i in range(4):
                pool.memset(iota4[:, i:i + 1], float(i)).then_inc(E["e_iota"], 1)
            for g in range(G_MOE + 3, G_MOE + 13):
                pool.wait_ge(G["lo_ready"], g)
                split_lo(pool, g, g % 2)

        def ple_sync(sp):
            for s in range(4):
                load_slot(sp, G_PG + s, (G_PG + s) % 2, pairs(a["w_pg"], s * 2 * P))

        def ple_tensor(pe):
            def turn_context(n):
                for k in range(2):
                    for i in range(2):
                        done = pe.transpose(psum[:, 4 + n % 2, (2 * k + i) * P:(2 * k + i + 1) * P],
                                            ctx_in[:, i, (2 * n + k) * P:(2 * n + k + 1) * P], ident)
                done.then_inc(L["turned"], 1)
            pe.wait_ge(L["ctx_in"], 16)
            for n in range(2):
                turn_context(n)
            norm_mean(pe, N_PLE)
            keep_warm(pe, 0, 6)
            pe.wait_ge(L["ctx_copied"], 2)
            for n in range(2, 4):
                turn_context(n)
            for s in range(4):
                if s == 1:
                    pe.wait_ge(L["ctx_sq"], 4)
                    pe.wait_ge(L["gains"], 2)
                    for k in range(KC):
                        done = pe.matmul(psum[:, 6, 0:CTX], ones[:, :], ctx_sq[:, k, :], start=(k == 0),
                                         stop=(k == KC - 1))
                    done.then_inc(L["ctx_mean"], 1)
                if s >= 2:
                    pe.wait_ge(L["pg_sig"], 2 * s - 2)
                else:
                    pe.wait_ge(G["x_ready"], 8 * R_PG)
                if s < 3:
                    whole_slot(pe, G_PG + s, (G_PG + s) % 2, of_pairs, h_hi, h_lo, KC,
                               G["h_lo_ready"] if s == 0 else None, 8 * N_PLE)
                else:
                    last_slot(pe, G_PG + s, (G_PG + s) % 2, h_hi, h_lo)

        def ple_scalar(act):
            def context(c):
                n = 2 * (c // 4) + c % 2
                if c % 4 < 2:
                    act.wait_ge(L["turned"], n + 2)
                    act.activation(ctx_x[:, 2 * n:2 * n + 2, :],
                                   psum[:, 4 + n % 2, :].rearrange("p (k t) -> p k t", t=CTX), ACT.Copy)\
                       .then_inc(L["ctx_copied"], 1)
                else:
                    act.wait_ge(L["ctx_copied"], n + 1)
                    act.activation(ctx_sq[:, 2 * n:2 * n + 2, :], ctx_x[:, 2 * n:2 * n + 2, :], ACT.Square)\
                       .then_inc(L["ctx_sq"], 1)
            norm_rstd(act, N_PLE)
            norm_hi(act, N_PLE, between=context)
            for s in range(4):
                split_hi(act, G_PG + s + 1, (G_PG + s + 1) % 2)
                if s == 1:
                    context_scalar(act)
                for i in range(2):
                    c = 2 * s + i
                    act.wait_ge(G["chunk_done"], 2 * (G_PG + s) + i + 1)
                    if c >= 2:
                        act.wait_ge(G["x_ready"], 8 * R_PG + c - 1)
                    act.activation(sig[:, i, :], psum[:, 2 * ((G_PG + s) % 2) + i, :], ACT.Sigmoid)\
                       .then_inc(L["pg_sig"], 1)
                    if c == 6:
                        square(act, R_PG, 6)
                for i in range(s // 3, 2):
                    square(act, R_PG, 2 * s + i)

        def ple_vector(dve):
            norm_dve(dve, N_PLE, lambda c: vec[:, V_PLE_G + c:V_PLE_G + c + 1])
            dve.wait_ge(E["m2_used"], 24)
            bias = vec[:, V_BMOD:V_BMOD + 48]
            dve.tensor_tensor(mod[:, :, 0], psum[:, 6, 0:48], bias, ALU.add).then_inc(L["gains"], 1)
            dve.tensor_tensor(mod[:, 0:16, 1], psum[:, 6, 48:64], bias[:, 0:16], ALU.add).then_inc(L["gains"], 1)
            dve.wait_ge(L["gains"], 2)
            for n, (v, scale, col) in enumerate(((0, 8, V_N1), (1, 8, V_N1), (0, 32, V_N2))):
                dve.scalar_tensor_tensor(out=gain[:, n, :], in0=mod[:, scale:scale + 8, v], scalar=1.0,
                                         in1=vec[:, col:col + 8], op0=ALU.add, op1=ALU.mult).then_inc(L["gains"], 1)
            for s in range(4):
                split_lo(dve, G_PG + s + 1, (G_PG + s + 1) % 2)
                if s == 1:
                    dve.wait_ge(L["gains"], 5)
                    context_vector(dve)
                for i in range(2):
                    c = 2 * s + i
                    if c == 7:
                        add_square(dve, R_PG, 6, N_PLE + 1)
                    dve.wait_ge(L["pg_sig"], c + 1)
                    dve.wait_ge(L["p_done"], c + 1)
                    dve.tensor_tensor(sig[:, i, :], sig[:, i, :], pl[:, c, :], ALU.mult).then_inc(L["pg_gated"], 1)
                    dve.wait_ge(L["pg_gated"], c + 1)
                    dve.tensor_tensor(x[:, c, :], x[:, c, :], sig[:, i, :], ALU.add).then_inc(G["x_ready"], 1)
                for i in range(s // 3, 2):
                    add_square(dve, R_PG, 2 * s + i, N_PLE + 1)

        def context_scalar(act):
            act.wait_ge(L["ctx_mean"], 1)
            act.activation(ctx_r[:, :], psum[:, 6, 0:CTX], ACT.Ln, bias=eps[:, 0:1], scale=1.0 / D)\
               .then_inc(L["ctx_rstd"], 1)
            act.wait_ge(L["ctx_rstd"], 1)
            act.activation(ctx_r[:, :], ctx_r[:, :], ACT.Exp, scale=-0.5).then_inc(L["ctx_rstd"], 1)
            for c in range(KC):
                act.wait_ge(L["ctx_pre"], c + 1)
                act.activation(hc_hi[:, c, :], ctx_pre[:, c % 2, :], ACT.Identity, bias=mod[:, c, 1:2])\
                   .then_inc(L["ctx_hi"], 1)

        def context_vector(dve):
            def make(c):
                if c >= 2:
                    dve.wait_ge(L["ctx_lo"], c - 1)
                dve.scalar_tensor_tensor(out=ctx_pre[:, c % 2, :], in0=ctx_x[:, c, :], scalar=gain[:, 1, c:c + 1],
                                         in1=ctx_r[:, :], op0=ALU.mult, op1=ALU.mult).then_inc(L["ctx_pre"], 1)
            dve.wait_ge(L["ctx_rstd"], 2)
            make(0)
            for c in range(KC):
                if c + 1 < KC:
                    make(c + 1)
                dve.wait_ge(L["ctx_hi"], c + 1)
                dve.scalar_tensor_tensor(out=hc_lo[:, c, :], in0=ctx_pre[:, c % 2, :], scalar=mod[:, c, 1:2],
                                         in1=hc_hi[:, c, :].bitcast(F32), op0=ALU.add, op1=ALU.subtract)\
                   .then_inc(L["ctx_lo"], 1)

        H = semaphores("t_const", "t_dec", "t_sel", "t_tab", "t_raw", "t_turn", "t_rot", "t_qk",
                       "t_turned", "t_vtok", "t_decayed", "t_kv", "t_state", "t_scores", "t_dm",
                       "t_pv", "t_o", "t_mean", "t_cen", "t_sq", "t_var", "t_ln", "t_rstd", "t_yn", "t_y", "t_silu",
                       "t_gate", "x_out")
        C, SA, SB, O, X0, X1 = 2, 3, 4, 5, 6, 7

        def ret_pieces(m, s):
            w = a["w_in_2"]
            if s == 0:
                return halves(w, RK0 + m * P, m * P)
            if s == 3:
                return pairs(a["w_branch_gate_2"], m * P * 2)
            return pairs(w, m * 2 * P + (RV0, RG0)[s - 1])

        def ret_sync(sp):
            def pair(m):
                for s in range(4):
                    load_slot(sp, G_RET + 4 * m + s, (G_RET + s) % 2, ret_pieces(m, s))
                    if isinstance(m, int) and s == 1:
                        sp.wait_ge(G["x_ready"], 8 * R_PG + 8)
                        sp.wait_ge(L["ctx_lo"], 8)
                        sp.dma_start(dist[:, :], const["dist"]).then_inc(H["t_const"], 16)
                        sp.dma_start(rope[:, :, :], const["rope"].rearrange("p (a t) -> p a t", a=2))\
                          .then_inc(H["t_const"], 16)
                        for d, name in enumerate(("ret_decay_f_2", "ret_decay_b_2")):
                            sp.dma_start(decay[:, d, :], a[name].rearrange("(o h) -> o h", o=1)
                                         .to_broadcast([P, RET_HEADS])).then_inc(H["t_const"], 16)
                            with nc.allow_non_contiguous_dma(reason="every other one of eight numbers"):
                                for h in range(2):
                                    sp.dma_start(decay_row[64 * h:64 * h + 64, d, :],
                                                 a[name].rearrange("(o m h) -> o h m", o=1, h=2)[:, h, :]
                                                 .to_broadcast([64, 4])).then_inc(H["t_const"], 16)
                        sp.dma_start(scratch_x, x[:, :, :].rearrange("p k t -> p (k t)")).then_inc(H["x_out"], 16)
            pair(0)
            with sp.Fori(1, 4) as m:
                pair(m)

        def ret_scores(pe, m):
            pe.wait_ge(H["t_vtok"], 2 * m + 2)
            for h in range(2):
                r = slice(64 * h, 64 * h + 64)
                for i in range(NT):
                    t = slice(i * CHUNK, (i + 1) * CHUNK)
                    done = pe.matmul(psum[:, X0 + h, t], kr_t[r, t], qr_t[r, t], start=True, stop=True)
            done.then_inc(H["t_scores"], 1)

        def ret_turn_k(pe, m):
            pe.wait_ge(H["t_qk"], 2 * m + 2)
            pe.wait_ge(H["t_vtok"], 2 * m + 1)
            for b in range(6):
                done = pe.transpose(psum[:, SA + b // 4, (b % 4) * P:(b % 4 + 1) * P], kr_t[:, b * P:(b + 1) * P], ident)
            done.then_inc(H["t_turned"], 1)

        def ret_kv(pe, m):
            pe.wait_ge(H["t_decayed"], 6 * m + 6)
            for d in range(2):
                order = ((4, 5), (0,), (1,), (2,)) if d == 0 else ((4, 5), (3,), (2,), (1,))
                for n, blocks in enumerate(order):
                    for h in range(2):
                        for i, b in enumerate(blocks):
                            done = pe.matmul(psum[64 * h:64 * h + 64, SA + d, n * RET_V:(n + 1) * RET_V],
                                             k_dec[:, d, b, h, :], vr_tok[:, h, b * P:(b + 1) * P],
                                             start=(i == 0), stop=(i == len(blocks) - 1))
            done.then_inc(H["t_kv"], 1)

        def ret_pv(pe, m, h):
            pe.wait_ge(H["t_dm"], 2 * m + h + 1)
            pe.wait_ge(H["t_state"], 8 * m + 8)
            pe.wait_ge(H["t_decayed"], 6 * m + 6)
            pe.wait_ge(*((H["t_o"], 2 * m + 1) if h else (H["t_raw"], 4 * m + 4)))
            r = slice(64 * h, 64 * h + 64)
            for i in range(NT):
                t = slice(i * CHUNK, (i + 1) * CHUNK)
                pe.matmul(psum[:, O, t], vr_tok[:, h, t], weighted[:, h, t], start=True, stop=False)
                pe.matmul(psum[:, O, t], state[r, 0, i, :], q_dec[r, 0, t], start=False, stop=False)
                done = pe.matmul(psum[:, O, t], state[r, 1, NT - 1 - i, :], q_dec[r, 1, t], start=False, stop=True)
            done.then_inc(H["t_pv"], 1)

        def ret_mean(pe, m, h):
            pe.wait_ge(H["t_o"], 2 * m + h + 1)
            pe.matmul(psum[:, X0, :], ones[:, :], o_buf[:, :], start=True, stop=True).then_inc(H["t_mean"], 1)

        def ret_var(pe, m, h):
            pe.wait_ge(H["t_sq"], 2 * m + h + 1)
            pe.matmul(psum[:, (X1, C)[h], :], ones[:, :], o_buf[:, :], start=True, stop=True).then_inc(H["t_var"], 1)

        def ret_after_tensor(pe, p):
            return (lambda: ret_pv(pe, p, 0), lambda: ret_mean(pe, p, 0), lambda: ret_var(pe, p, 0),
                    lambda: ret_pv(pe, p, 1), lambda: ret_mean(pe, p, 1), lambda: ret_var(pe, p, 1))

        def ret_tensor(pe):
            def context(j, tile_of, half, first=False):
                for k in range(KC):
                    if first:
                        pe.wait_ge(L["ctx_lo"], k + 1)
                    product(pe, psum[:, C, 0:CTX], j, tile_of(half, k), hc_hi, hc_lo, k, k == KC - 1, CTX)

            def turn_v(m, h, banks):
                for b in range(6):
                    done = pe.transpose(psum[:, banks[b // 4], (b % 4) * P:(b % 4 + 1) * P],
                                        vr_raw[:, b * P:(b + 1) * P], ident)
                done.then_inc(H["t_turned"], 1)

            def pair(m, rest):
                g, j = G_RET + 4 * m, G_RET % 2
                first = rest[0] is nothing
                rest[0]()
                pe.wait_ge(G["lo_ready"], g + 1)
                if first:
                    pe.wait_ge(L["pg_sig"], 8)
                context(j, of_halves, 0, first)
                if first:
                    norm_mean(pe, N_RET)
                    keep_warm(pe, SB, 6)
                    pe.wait_ge(G["x_ready"], 8 * R_PG + 8)
                    assert j == 0
                    whole_slot(pe, g, j, of_halves, h_hi, h_lo, KC, G["h_lo_ready"], 8 * N_RET)
                else:
                    pe.wait_ge(H["t_gate"], 2 * m - 1)
                    half_slot(pe, j, 0, of_halves, 0)
                rest[1]()
                if not first:
                    pe.wait_ge(H["t_gate"], 2 * m)
                    half_slot(pe, j, 1, of_halves, 1)
                rest[2]()
                pe.wait_ge(G["lo_ready"], g + 2)
                pe.wait_ge(H["t_raw"], 4 * m + 1)
                context(1 - j, of_pairs, 0)
                half_slot(pe, 1 - j, 0, of_pairs, 0)
                rest[3]()
                pe.wait_ge(H["t_raw"], 4 * m + 2)
                if not first:
                    pe.wait_ge(H["t_state"], 8 * m)
                pe.matmul(psum[:, SA, :], turn, kr_raw[:, 0:T], start=True, stop=True)
                pe.matmul(psum[:, SB, :], turn, qr_raw[:, :], start=True, stop=True).then_inc(H["t_turn"], 1)
                pe.wait_ge(H["t_raw"], 4 * m + 3)
                context(1 - j, of_pairs, 1)
                half_slot(pe, 1 - j, 1, of_pairs, 1)
                rest[4]()
                pe.wait_ge(H["t_qk"], 2 * m + 2)
                turn_v(m, 0, (SA, SB))
                pe.wait_ge(G["lo_ready"], g + 3)
                half_slot(pe, j, 0, of_pairs, 0)
                pe.wait_ge(H["t_raw"], 4 * m + 4)
                rest[5]()
                if not first:
                    pe.wait_ge(H["t_cen"], 2 * m)
                turn_v(m, 1, (X0, X1))
                half_slot(pe, j, 1, of_pairs, 1)
                ret_turn_k(pe, m)
                ret_scores(pe, m)
                pe.wait_ge(G["lo_ready"], g + 4)
                pe.wait_ge(H["t_silu"], 2 * m + 1)
                half_slot(pe, 1 - j, 0, of_pairs, 0)
                ret_kv(pe, m)
                pe.wait_ge(H["t_silu"], 2 * m + 2)
                half_slot(pe, 1 - j, 1, of_pairs, 1)

            pair(0, (nothing,) * 6)
            with pe.Fori(1, 4) as m:
                pair(m, ret_after_tensor(pe, m - 1))

        def ret_gate(act, m, i):
            act.wait_ge(G["chunk_done"], 2 * (G_RET + 4 * m + 3) + i + 1)
            act.activation(gr[:, bass.ds(2 * m + i, 1), :], psum[:, i:i + 1, :], ACT.Sigmoid,
                           bias=vec[:, bass.ds(V_BG + 2 * m + i, 1)]).then_inc(H["t_gate"], 1)

        def ret_copy_o(act, m, h):
            act.wait_ge(H["t_pv"], 2 * m + h + 1)
            act.activation(o_buf[:, :], psum[:, O, :], ACT.Copy).then_inc(H["t_o"], 1)

        def ret_square(act, m, h):
            act.wait_ge(H["t_cen"], 2 * m + h + 1)
            act.activation(o_buf[:, :], cen[:, :], ACT.Square).then_inc(H["t_sq"], 1)

        def ret_rstd(act, m, h):
            act.wait_ge(H["t_var"], 2 * m + h + 1)
            act.activation(rstd[:, :], psum[:, (X1, C)[h], :], ACT.Ln, bias=eps[:, 0:1], scale=1.0 / RET_V)\
               .then_inc(H["t_ln"], 1)
            act.wait_ge(H["t_ln"], 2 * m + h + 1)
            act.activation(rstd[:, :], rstd[:, :], ACT.Exp, scale=-0.5).then_inc(H["t_rstd"], 1)

        def ret_after_scalar(act, p):
            return (lambda: ret_copy_o(act, p, 0), lambda: ret_square(act, p, 0), lambda: ret_rstd(act, p, 0),
                    lambda: ret_copy_o(act, p, 1), lambda: ret_square(act, p, 1), lambda: ret_rstd(act, p, 1))

        def ret_scalar(act):
            norm_rstd(act, N_RET)
            norm_hi(act, N_RET, lambda c: mod[:, c, 0:1])
            act.wait_ge(H["t_const"], 128)
            act.activation(decay[:, :, :], decay[:, :, :], ACT.Exp).then_inc(H["t_dec"], 1)
            act.activation(decay_row[:, :, :], decay_row[:, :, :], ACT.Exp).then_inc(H["t_dec"], 1)

            def tables():
                act.wait_ge(H["t_dec"], 4)
                act.wait_ge(H["x_out"], 16)
                away, to_key = dist[:, 0:CHUNK], 3 * CHUNK
                for h in range(RET_HEADS):
                    act.activation(near[:, h, :], away, ACT.Exp, scale=decay[:, 0, h:h + 1])
                    done = act.activation(near_b[:, h, :], away, ACT.Exp, scale=decay_b[:, h:h + 1])
                done.then_inc(H["t_tab"], 1)
                for d in range(2):
                    for p in range(4):
                        act.activation(q_reach[:, d, p, :], dist[:, (1 + d) * CHUNK:(2 + d) * CHUNK], ACT.Exp,
                                       scale=decay_row[:, d, p:p + 1])
                    for n, col in enumerate(((0, 2, 0), (1, 1, 3))[d]):
                        act.activation(k_reach[:, d, n, :], decay[:, d, :], ACT.Exp,
                                       scale=dist[:, to_key + col:to_key + col + 1])
                done = act.activation(step[:, :, :], decay_row[:, :, :], ACT.Exp, scale=dist[:, to_key + 4:to_key + 5])
                done.then_inc(H["t_tab"], 1)

            def copy_v(m, h):
                g = G_RET + 4 * m + 1
                act.wait_ge(G["chunk_done"], 2 * g + h + 1)
                if h or not isinstance(m, int):
                    act.wait_ge(H["t_turned"], 3 * m + h)
                act.activation(vr_raw[:, 0:T], psum[:, h, :], ACT.Copy)
                act.activation(vr_raw[:, T:T + CTX], psum[:, C, 0:CTX], ACT.Copy).then_inc(H["t_raw"], 1)

            def silu_g(m, i):
                act.wait_ge(G["chunk_done"], 2 * (G_RET + 4 * m + 2) + i + 1)
                if not isinstance(m, int):
                    act.wait_ge(H["t_y"], 2 * m + i)
                act.activation(sg[:, i, :], psum[:, i, :], ACT.Silu).then_inc(H["t_silu"], 1)

            def pair(m, rest):
                g, j = G_RET + 4 * m, G_RET % 2
                if rest[0] is not nothing:
                    ret_gate(act, m - 1, 1)
                split_hi(act, g + 1, 1 - j)
                rest[0]()
                act.wait_ge(G["chunk_done"], 2 * g + 1)
                act.activation(kr_raw[:, 0:T], psum[:, 0, :], ACT.Copy)
                act.activation(kr_raw[:, T:T + CTX], psum[:, C, 0:CTX], ACT.Copy).then_inc(H["t_raw"], 1)
                rest[1]()
                act.wait_ge(G["chunk_done"], 2 * g + 2)
                act.activation(qr_raw[:, :], psum[:, 1, :], ACT.Copy).then_inc(H["t_raw"], 1)
                split_hi(act, g + 2, j)
                rest[2]()
                copy_v(m, 0)
                rest[3]()
                if rest[0] is nothing:
                    tables()
                copy_v(m, 1)
                rest[4]()
                split_hi(act, g + 3, 1 - j)
                rest[5]()
                silu_g(m, 0)
                split_hi(act, g + 4, j)
                silu_g(m, 1)
                ret_gate(act, m, 0)

            pair(0, (nothing,) * 6)
            with act.Fori(1, 4) as m:
                pair(m, ret_after_scalar(act, m - 1))

        def ret_weigh(dve, m, h):
            dve.wait_ge(H["t_scores"], m + 1)
            if not isinstance(m, int):
                dve.wait_ge(H["t_pv"], 2 * m)
            dve.tensor_tensor(weighted[:, h, :].rearrange("p (i n) -> p i n", n=CHUNK),
                              near[:, bass.ds(2 * m + h, 1), :].to_broadcast([P, NT, CHUNK]),
                              psum[:, X0 + h, :].rearrange("p (i n) -> p i n", n=CHUNK), ALU.mult)\
               .then_inc(H["t_dm"], 1)

        def ret_weigh_k(dve, m):
            dve.wait_ge(H["t_turned"], 3 * m + 3)
            if not isinstance(m, int):
                dve.wait_ge(H["t_kv"], m)
            for d in range(2):
                for b, n, bank in ((0, 4, SA), (4, 2, SB)):
                    reach = k_reach[:, d, 0:1, bass.ds(2 * m, 2)] if n == 4 else k_reach[:, d, 1:3, bass.ds(2 * m, 2)]
                    dve.tensor_tensor(k_dec[:, d, b:b + n, :, :],
                                      psum[:, bank, 0:n * P].rearrange("p (b h f) -> p b h f", b=n, h=2),
                                      reach.rearrange("p b (h o) -> p b h o", o=1).to_broadcast([P, n, 2, HEAD_DIM]),
                                      ALU.mult).then_inc(H["t_decayed"], 1)

        def ret_weigh_q(dve, m):
            if not isinstance(m, int):
                dve.wait_ge(H["t_pv"], 2 * m)
            for d in range(2):
                dve.tensor_tensor(q_dec[:, d, :].rearrange("p (i n) -> p i n", n=CHUNK),
                                  q_reach[:, d, bass.ds(m, 1), :].to_broadcast([P, NT, CHUNK]),
                                  qr_t[:, :].rearrange("p (i n) -> p i n", n=CHUNK), ALU.mult).then_inc(H["t_decayed"], 1)

        def ret_states(dve, m):
            dve.wait_ge(H["t_kv"], m + 1)
            if not isinstance(m, int):
                dve.wait_ge(H["t_pv"], 2 * m)
            for n in range(NT):
                for d in range(2):
                    block = psum[:, SA + d, n * RET_V:(n + 1) * RET_V]
                    if n == 0:
                        ins = dve.tensor_copy(state[:, d, 0, :], block)
                    else:
                        dve.wait_ge(H["t_state"], 8 * m + 2 * n + d - 1)
                        ins = dve.scalar_tensor_tensor(out=state[:, d, n, :], in0=state[:, d, n - 1, :],
                                                       scalar=step[:, d, bass.ds(m, 1)], in1=block, op0=ALU.mult,
                                                       op1=ALU.add)
                    ins.then_inc(H["t_state"], 1)

        def ret_center(dve, m, h):
            dve.wait_ge(H["t_mean"], 2 * m + h + 1)
            dve.wait_ge(H["t_y"], 2 * m + h + 1)
            dve.scalar_tensor_tensor(out=cen[:, :], in0=psum[:, X0, :], scalar=-1.0 / RET_V, in1=o_buf[:, :],
                                     op0=ALU.mult, op1=ALU.add).then_inc(H["t_cen"], 1)

        def ret_out(dve, m, h):
            dve.wait_ge(H["t_rstd"], 2 * m + h + 1)
            dve.wait_ge(H["t_silu"], 2 * m + h + 1)
            dve.tensor_tensor(cen[:, :], cen[:, :], rstd[:, :], ALU.mult).then_inc(H["t_yn"], 1)
            dve.wait_ge(H["t_yn"], 2 * m + h + 1)
            dve.tensor_tensor(yr[:, bass.ds(2 * m + h, 1), :], cen[:, :].rearrange("p (o t) -> p o t", o=1),
                              sg[:, h:h + 1, :], ALU.mult).then_inc(H["t_y"], 1)

        def ret_after_vector(dve, p):
            return (nothing, lambda: ret_center(dve, p, 0), lambda: ret_out(dve, p, 0), nothing,
                    lambda: ret_center(dve, p, 1), lambda: ret_out(dve, p, 1))

        def ret_vector(dve):
            norm_dve(dve, N_RET, lambda c: gain[:, 0, c:c + 1], lambda c: mod[:, c, 0:1])
            dve.wait_ge(H["t_dec"], 2)
            dve.tensor_copy(decay_b[:, :], decay[:, 1, :])
            dve.tensor_scalar(decay_row[:, :, :], decay_row[:, :, :], -1.0, None, ALU.mult).then_inc(H["t_dec"], 1)
            dve.wait_ge(H["t_dec"], 3)
            dve.tensor_scalar(decay[:, :, :], decay[:, :, :], -1.0, None, ALU.mult).then_inc(H["t_dec"], 1)
            cos, sin = rope[:, 0, :], rope[:, 1, :]

            def rotate(m, i):
                raw_t, bank, out, scale = ((kr_raw, SA, kr_t, 1.0), (qr_raw, SB, qr_t, HEAD_DIM ** -0.5))[i]
                tmp = pre[:, i, :]
                dve.scalar_tensor_tensor(out=tmp, in0=psum[:, bank, :], scalar=scale, in1=sin, op0=ALU.mult,
                                         op1=ALU.mult).then_inc(H["t_rot"], 1)
                dve.scalar_tensor_tensor(out=out[:, 0:T], in0=raw_t[:, 0:T], scalar=scale, in1=cos, op0=ALU.mult,
                                         op1=ALU.mult).then_inc(H["t_rot"], 1)
                dve.wait_ge(H["t_rot"], 4 * m + 2 * i + 2)
                dve.tensor_tensor(out[:, 0:T], out[:, 0:T], tmp, ALU.add).then_inc(H["t_qk"], 1)

            def pair(m, rest):
                g, j = G_RET + 4 * m, G_RET % 2
                rest[0]()
                split_lo(dve, g + 1, 1 - j)
                rest[1]()
                split_lo(dve, g + 2, j)
                rest[2]()
                dve.wait_ge(H["t_turn"], m + 1)
                if rest[0] is nothing:
                    dve.wait_ge(H["t_const"], 128)
                dve.tensor_copy(kr_t[:, T:T + CTX], kr_raw[:, T:T + CTX])
                for i in range(2):
                    rotate(m, i)
                rest[4]()
                split_lo(dve, g + 3, 1 - j)
                for h, banks in enumerate(((SA, SB), (X0, X1))):
                    dve.wait_ge(H["t_turned"], 3 * m + h + 1)
                    dve.tensor_copy(vr_tok[:, h, 0:T], psum[:, banks[0], :])
                    dve.tensor_copy(vr_tok[:, h, T:T + CTX], psum[:, banks[1], 0:CTX]).then_inc(H["t_vtok"], 1)
                rest[5]()
                if rest[0] is nothing:
                    dve.wait_ge(H["t_tab"], 3)
                ret_weigh_q(dve, m)
                ret_weigh_k(dve, m)
                split_lo(dve, g + 4, j)
                for h in range(2):
                    ret_weigh(dve, m, h)
                ret_states(dve, m)

            pair(0, (nothing,) * 6)
            with dve.Fori(1, 4) as m:
                pair(m, ret_after_vector(dve, m - 1))

        def ret_gpsimd(pool):
            pool.wait_ge(H["t_tab"], 1)
            for n, (table, sign) in enumerate(((near, 1), (near_b, -1))):
                pool.affine_select(out=table[:, :, :], in_=table[:, :, :], compare_op=ALU.is_ge, fill=0.0, base=0,
                                   pattern=[[0, RET_HEADS], [sign, CHUNK]], channel_multiplier=-sign)\
                    .then_inc(H["t_sel"], 1)
            pool.wait_ge(H["t_sel"], 2)
            pool.tensor_tensor(near[:, :, :], near[:, :, :], near_b[:, :, :], ALU.add).then_inc(H["t_tab"], 1)

        Z = semaphores("z_const", "z_f", "z_gate", "z_d", "z_copied", "z_l", "z_hi", "z_lo", "z_yhi", "z_ylo", "z_ret",
                       "z_bank", "z_four", "z_sum", "z_mhi", "z_mlo")

        def four_sync(sp):
            for s in range(2):
                load_slot(sp, G_FOUR + s, (G_FOUR + s) % 2, pairs(a["w_in_2"], RF0 + s * 2 * P))
            sp.wait_ge(G["chunk_done"], 2 * G_FOUR)
            sp.wait_ge(H["t_decayed"], 24)
            sp.wait_ge(H["t_vtok"], 8)
            sp.dma_start(dft_d[:, :], const["dft_d"]).then_inc(Z["z_const"], 16)
            sp.dma_start(dft_l[:, :, :, :], const["dft_l"].rearrange("a (i p) t -> p a i t", p=P))\
              .then_inc(Z["z_const"], 16)
            for s in range(4):
                load_slot(sp, G_GF + s, (G_GF + s) % 2, pairs(a["w_branch_gate_2"], D + s * 2 * P))
            for s in range(4):
                load_slot(sp, G_RO + s, (G_RO + s) % 2, pairs(a["w_ret_out_2"], s * 2 * P))
            sp.wait_ge(Z["z_l"], 4)
            sp.dma_start(x[:, :, :].rearrange("p k t -> p (k t)"), scratch_x).then_inc(H["x_out"], 16)
            for s in range(2):
                load_slot(sp, G_FO + s, (G_FO + s) % 2,
                          [(0, 16, T, a["w_four_out_2"][:, s * T:(s + 1) * T].rearrange("(k p) n -> p k n", p=P))])

        def four_tensor(pe):
            rest = ret_after_tensor(pe, 3)

            def over_features(g):
                if g == 0:
                    pe.wait_ge(Z["z_const"], 32)
                    pe.wait_ge(Z["z_f"], 4)
                    pe.wait_ge(H["t_state"], 32)
                else:
                    pe.wait_ge(Z["z_copied"], g)
                for i in range(NT):
                    done = pe.matmul(psum[:, SA + i // 2, (i % 2) * 256:(i % 2) * 256 + 256],
                                     f_t[:, g, i * P:(i + 1) * P], dft_d[:, :], start=True, stop=True)
                done.then_inc(Z["z_d"], 1)

            def over_tokens(g):
                pe.wait_ge(Z["z_copied"], g + 1)
                if g == 0:
                    pe.wait_ge(H["t_y"], 9)
                if g >= 2:
                    pe.wait_ge(Z["z_lo"], g - 1)
                for n in range(8):
                    i, part = n // 2, n % 2
                    done = pe.matmul(psum[:, 5 + g % 2, :], fd[:, g, i, part * P:(part + 1) * P],
                                     dft_l[:, part, i, :], start=(n == 0), stop=(n == 7))
                done.then_inc(Z["z_l"], 1)

            for t in range(12):
                s, half = G_FOUR + t // 2, t % 2
                if t < 6:
                    rest[t]()
                if 5 <= t < 9:
                    over_features(t - 5)
                if 7 <= t < 11:
                    over_tokens(t - 7)
                if half == 0:
                    pe.wait_ge(G["lo_ready"], s + 1)
                if t < 2:
                    pe.wait_ge(H["t_gate"], 7 + t)
                elif t < 6:
                    pe.wait_ge(Z["z_f"], t - 1)
                else:
                    pe.wait_ge(Z["z_gate"], t - 5)
                half_slot(pe, s % 2, half, of_pairs, half)
            for s in range(4):
                if s == 0:
                    pe.wait_ge(Z["z_gate"], 8)
                if s >= 2:
                    pe.wait_ge(Z["z_ret"], 2 * s - 2)
                whole_slot(pe, G_RO + s, (G_RO + s) % 2, of_pairs, yr_hi, yr_lo, KC, Z["z_ylo"] if s == 0 else None, 0)
            pe.wait_ge(Z["z_lo"], 4)
            for c in range(KC):
                s = c // 4
                if c % 4 == 0:
                    pe.wait_ge(G["lo_ready"], G_FO + s + 1)
                if c >= 4:
                    pe.wait_ge(Z["z_four"], c - 3)
                for k in range(4):
                    done = product(pe, psum[:, 4 + c % 4, :], (G_FO + s) % 2, 4 * k + c % 4, z_hi, z_lo, k, k == 3)
                done.then_inc(G["chunk_done"] if c % 2 else Z["z_bank"], 1)

        def four_scalar(act):
            rest = ret_after_scalar(act, 3)
            ret_gate(act, 3, 1)
            for t in range(12):
                if t % 2 == 0:
                    split_hi(act, G_FOUR + t // 2 + 1, (G_FOUR + t // 2 + 1) % 2)
                if 1 <= t <= 4:
                    act.wait_ge(G["chunk_done"], 2 * G_FOUR + t)
                    act.activation(f_t[:, t - 1, :], psum[:, (t - 1) % 2, :], ACT.Copy).then_inc(Z["z_f"], 1)
                if t < 6:
                    rest[t]()
                if 5 <= t < 9:
                    act.wait_ge(Z["z_d"], t - 4)
                    act.activation(fd[:, t - 5, :, :], psum[:, SA:SA + 2, :].rearrange("p b (i n) -> p (b i) n", n=256),
                                   ACT.Copy).then_inc(Z["z_copied"], 1)
                if t >= 5:
                    four_gate(act, t - 5)
                if 7 <= t < 11:
                    g = t - 7
                    act.wait_ge(Z["z_l"], g + 1)
                    act.activation(z_hi[:, g, :], psum[:, 5 + g % 2, :], ACT.Copy).then_inc(Z["z_hi"], 1)
            four_gate(act, 7)
            for c in range(KC):
                act.activation(yr_hi[:, c, :], yr[:, c, :], ACT.Copy).then_inc(Z["z_yhi"], 1)
            for s in range(4):
                split_hi(act, G_RO + s + 1, (G_RO + s + 1) % 2)
            for c in range(KC):
                if c % 4 == 0:
                    split_hi(act, G_FO + c // 4 + 1, (G_FO + c // 4 + 1) % 2)
                act.wait_ge(Z["z_sum"], c + 1)
                act.activation(h_hi[:, c, :], pre[:, c % 2, :], ACT.Copy).then_inc(Z["z_mhi"], 1)

        def four_gate(act, c):
            act.wait_ge(G["chunk_done"], 2 * G_GF + c + 1)
            act.activation(gf[:, c, :], psum[:, c % 2, :], ACT.Sigmoid, bias=vec[:, V_BG + 8 + c:V_BG + 9 + c])\
               .then_inc(Z["z_gate"], 1)

        def four_vector(dve):
            rest = ret_after_vector(dve, 3)
            for t in range(12):
                if t % 2 == 0:
                    split_lo(dve, G_FOUR + t // 2 + 1, (G_FOUR + t // 2 + 1) % 2)
                if t < 6:
                    rest[t]()
                if 7 <= t < 11:
                    g = t - 7
                    dve.wait_ge(Z["z_hi"], g + 1)
                    dve.tensor_tensor(z_lo[:, g, :], psum[:, 5 + g % 2, :], z_hi[:, g, :].bitcast(F32), ALU.subtract)\
                       .then_inc(Z["z_lo"], 1)
            for c in range(KC):
                dve.wait_ge(Z["z_yhi"], c + 1)
                dve.tensor_tensor(yr_lo[:, c, :], yr[:, c, :], yr_hi[:, c, :].bitcast(F32), ALU.subtract)\
                   .then_inc(Z["z_ylo"], 1)
            for c in range(KC):
                s = G_RO + c // 2
                if c % 2 == 0:
                    split_lo(dve, s + 1, (s + 1) % 2)
                dve.wait_ge(G["chunk_done"], 2 * s + c % 2 + 1)
                dve.tensor_tensor(gr[:, c, :], gr[:, c, :], psum[:, 2 * (s % 2) + c % 2, :], ALU.mult)\
                   .then_inc(Z["z_ret"], 1)
            for c in range(KC):
                s = G_FO + c // 4
                if c % 4 == 0:
                    split_lo(dve, s + 1, (s + 1) % 2)
                if c % 2:
                    dve.wait_ge(G["chunk_done"], 2 * s + (c % 4) // 2 + 1)
                else:
                    dve.wait_ge(Z["z_bank"], c // 2 + 1)
                dve.wait_ge(Z["z_ret"], c + 1)
                dve.tensor_tensor(pre[:, c % 2, :], gf[:, c, :], psum[:, 4 + c % 4, :], ALU.mult).then_inc(Z["z_four"], 1)
                dve.wait_ge(Z["z_four"], c + 1)
                dve.tensor_tensor(pre[:, c % 2, :], pre[:, c % 2, :], gr[:, c, :], ALU.add).then_inc(Z["z_sum"], 1)
                dve.wait_ge(Z["z_mhi"], c + 1)
                dve.tensor_tensor(h_lo[:, c, :], pre[:, c % 2, :], h_hi[:, c, :].bitcast(F32), ALU.subtract)\
                   .then_inc(Z["z_mlo"], 1)

        def wout_sync(sp):
            for s in range(4):
                load_slot(sp, G_WOUT + s, (G_WOUT + s) % 2, pairs(a["w_out_2"], s * 2 * P))

        def wout_tensor(pe):
            add_tensor(pe, G_WOUT, G_WOUT % 2, R_WOUT, h_hi, h_lo, KC, Z["z_mlo"], 0, lambda s: None)

        def wout_scalar(act):
            add_scalar(act, G_WOUT, G_WOUT % 2, R_WOUT)

        def wout_vector(dve):
            dve.wait_ge(H["x_out"], 32)
            add_vector(dve, G_WOUT, G_WOUT % 2, R_WOUT, N_RET + 1, lambda c: mod[:, 16 + c, 0:1])

        V = semaphores("v_mid", "v_left", "v_conv", "v_gelu", "v_hid", "v_hi", "v_lo")

        def ffn_rounds(eng, body):
            with eng.Fori(0, 2) as q:
                body(q, 8)
            body(2, 6)

        def ffn_sync(sp):
            def body(q, n):
                g = G_FFN + 12 * q
                for s in range(n):
                    col = q * D + s * P
                    load_slot(sp, g + s, (G_FFN + s) % 2, halves(a["w_up_2"], col, col + FFN))
                for s in range(4):
                    load_slot(sp, g + n + s, (G_FFN + s) % 2,
                              pairs(a["w_down_2"][bass.ds(q * D, n * P), :], s * 2 * P))
            ffn_rounds(sp, body)

        def ffn_tensor(pe):
            keep_warm(pe, 6, 3)
            norm_mean(pe, N_FFN)
            keep_warm(pe, 6, 6)

            def body(q, n):
                g, r, j0 = G_FFN + 12 * q, R_FFN + q, G_FFN % 2
                for s in range(n):
                    if s < 2:
                        pe.wait_ge(G["x_ready"], 8 * r - 2 + 2 * s)
                    else:
                        pe.wait_ge(V["v_conv"], 2 * (8 * q + s) - 2)
                    whole_slot(pe, g + s, (j0 + s) % 2, of_halves, h_hi, h_lo, KC,
                               G["h_lo_ready"] if s == 0 else None, 8 * N_FFN)
                add_tensor(pe, g + n, j0, r, d2_hi, d2_lo, n, V["v_lo"], 8 * q,
                           lambda s: pe.wait_ge(V["v_conv"], 2 * (8 * q + n - 1 + s)))
            ffn_rounds(pe, body)

        def ffn_scalar(act):
            norm_rstd(act, N_FFN)
            norm_hi(act, N_FFN, lambda c: mod[:, 24 + c, 0:1])

            def body(q, n):
                g, r, j0 = G_FFN + 12 * q, R_FFN + q, G_FFN % 2
                for s in range(n):
                    at = 8 * q + s
                    split_hi(act, g + s + 1, (j0 + s + 1) % 2, 16 if s + 1 < n else 2 * n)
                    for half in range(2):
                        act.wait_ge(G["chunk_done"], 2 * (g + s) + half + 1)
                        col = at + half * FC
                        act.activation(cv[:, s % 2, half, :], psum[:, 2 * ((j0 + s) % 2) + half, :], ACT.Identity,
                                       bias=vec[:, bass.ds(V_CONVB + col, 1)],
                                       scale=vec[:, bass.ds(V_CONV2 + 2 * FC + col, 1)]).then_inc(V["v_mid"], 1)
                    act.wait_ge(V["v_conv"], 2 * at + 1)
                    act.activation(cv[:, s % 2, 0, :], cv[:, s % 2, 0, :], ACT.Gelu_apprx_tanh).then_inc(V["v_gelu"], 1)
                    act.wait_ge(V["v_hid"], at + 1)
                    act.activation(d2_hi[:, s, :], pre[:, s % 2, :], ACT.Copy).then_inc(V["v_hi"], 1)
                add_scalar(act, g + n, j0, r, (2 * n,) * 3 + (16 if n == 8 else 0,))
            ffn_rounds(act, body)

        def ffn_vector(dve):
            norm_dve(dve, N_FFN, lambda c: gain[:, 2, c:c + 1], lambda c: mod[:, 24 + c, 0:1])

            def body(q, n):
                g, r, j0 = G_FFN + 12 * q, R_FFN + q, G_FFN % 2
                for s in range(n):
                    at = 8 * q + s
                    split_lo(dve, g + s + 1, (j0 + s + 1) % 2, 16 if s + 1 < n else 2 * n)
                    for half in range(2):
                        col = at + half * FC
                        buf, bank = cv[:, s % 2, half, :], psum[:, 2 * ((j0 + s) % 2) + half, :]
                        dve.wait_ge(V["v_mid"], 2 * at + half + 1)
                        dve.scalar_tensor_tensor(out=buf[:, 1:T], in0=bank[:, 0:T - 1],
                                                 scalar=vec[:, bass.ds(V_CONV2 + col, 1)], in1=buf[:, 1:T],
                                                 op0=ALU.mult, op1=ALU.add).then_inc(V["v_left"], 1)
                        dve.wait_ge(V["v_left"], 2 * at + half + 1)
                        dve.scalar_tensor_tensor(out=buf[:, 0:T - 1], in0=bank[:, 1:T],
                                                 scalar=vec[:, bass.ds(V_CONV2 + 4 * FC + col, 1)],
                                                 in1=buf[:, 0:T - 1], op0=ALU.mult, op1=ALU.add)\
                           .then_inc(V["v_conv"], 1)
                    dve.wait_ge(V["v_gelu"], at + 1)
                    dve.wait_ge(V["v_conv"], 2 * at + 2)
                    dve.tensor_tensor(pre[:, s % 2, :], cv[:, s % 2, 0, :], cv[:, s % 2, 1, :], ALU.mult)\
                       .then_inc(V["v_hid"], 1)
                    dve.wait_ge(V["v_hi"], at + 1)
                    dve.tensor_tensor(d2_lo[:, s, :], pre[:, s % 2, :], d2_hi[:, s, :].bitcast(F32), ALU.subtract)\
                       .then_inc(V["v_lo"], 1)
                add_vector(dve, g + n, j0, r, N_FFN + 1, lambda c: mod[:, 40 + c, 0:1],
                           (2 * n,) * 3 + (16 if n == 8 else 0,))
            ffn_rounds(dve, body)

        OUT = semaphores("o_turned", "o_copied", "o_out")

        def by_token(c):
            pair = raw[c // 4][:, 8 * (c // 2 % 2):8 * (c // 2 % 2) + 8, :]
            return pair.rearrange("p (i a) n -> p i a n", a=2)[:, :, c % 2, :]

        def out_tensor(pe):
            keep_warm(pe, 6, 3)
            norm_mean(pe, N_OUT)
            keep_warm(pe, 6, 4)
            for c in range(KC):
                pe.wait_ge(G["pre_ready"], 8 * N_OUT + c + 1)
                if c >= 4:
                    pe.wait_ge(OUT["o_copied"], c - 3)
                for i in range(NT):
                    done = pe.transpose(psum[:, c % 4, i * P:(i + 1) * P], pre[:, c % 2, i * P:(i + 1) * P], ident)
                done.then_inc(OUT["o_turned"], 1)

        def out_scalar(act):
            norm_rstd(act, N_OUT)
            act.wait_ge(G["lo_ready"], G_END)
            for c in range(KC):
                act.wait_ge(OUT["o_turned"], c + 1)
                act.activation(by_token(c), psum[:, c % 4, :].rearrange("p (i n) -> p i n", n=P), ACT.Copy)\
                   .then_inc(OUT["o_copied"], 1)

        def out_vector(dve):
            dve.wait_ge(G["rstd_ready"], N_OUT + 1)
            for c in range(KC):
                if c >= 2:
                    dve.wait_ge(OUT["o_turned"], c - 1)
                dve.scalar_tensor_tensor(out=pre[:, c % 2, :], in0=x[:, c, :], scalar=vec[:, V_FIN + c:V_FIN + c + 1],
                                         in1=rstd[:, :], op0=ALU.mult, op1=ALU.mult).then_inc(G["pre_ready"], 1)

        def out_sync(sp):
            for b in range(KC // 2):
                sp.wait_ge(OUT["o_copied"], 2 * b + 2)
                sp.dma_start(out[:, b * 2 * P:(b + 1) * 2 * P].rearrange("(i p) n -> p i n", p=P),
                             raw[b // 2][:, 8 * (b % 2):8 * (b % 2) + 8, :].rearrange("p (i a) n -> p i (a n)", a=2))\
                  .then_inc(OUT["o_out"], 16)
            sp.wait_ge(OUT["o_out"], 16 * KC // 2)

        block = root.enter_context(nc.Block())

        @block.sync
        def _(sp):
            for stage in (start_sync, mix_sync, merge_sync, wo_sync, embed_sync, moe_sync, ple_sync, ret_sync, four_sync,
                          wout_sync, ffn_sync, out_sync):
                stage(sp)

        @block.scalar
        def _(act):
            for stage in (start_scalar, forget_scalar):
                stage(act)
            rest = mix_scalar(act)
            merge_scalar(act, rest)
            for stage in (wo_scalar, embed_scalar, moe_scalar, ple_scalar, ret_scalar, four_scalar, wout_scalar, ffn_scalar,
                          out_scalar):
                stage(act)

        @block.tensor
        def _(pe):
            for stage in (start_tensor,):
                stage(pe)
            rest = mix_tensor(pe)
            merge_tensor(pe, rest)
            for stage in (wo_tensor, embed_tensor, moe_tensor, ple_tensor, ret_tensor, four_tensor, wout_tensor, ffn_tensor,
                          out_tensor):
                stage(pe)

        @block.vector
        def _(dve):
            for stage in (start_vector,):
                stage(dve)
            rest = mix_vector(dve)
            merge_vector(dve, rest)
            for stage in (wo_vector, embed_vector, moe_vector, ple_vector, ret_vector, four_vector, wout_vector, ffn_vector,
                          out_vector):
                stage(dve)

        @block.gpsimd
        def _(pool):
            for stage in (start_gpsimd, mix_gpsimd, moe_gpsimd, ret_gpsimd):
                stage(pool)


def kernel(**inputs):
    import concourse.bacc as bacc
    from concourse.bass_utils import run_bass_kernel_spmd

    nc = bacc.Bacc("TRN2", target_bir_lowering=False, num_devices=1)
    arrays, a, const = {}, {}, {}
    for name, value in inputs.items():
        value = np.ascontiguousarray(value)
        while value.ndim > 1 and value.shape[0] == 1:
            value = value[0]
        if name in ("conv_w", "conv_w_2"):
            value = value.reshape(-1)
        arrays[f"in_{name}"] = value
        a[name] = nc.dram_tensor(f"in_{name}", value.shape, F32, kind="ExternalInput").ap()
    for name, value in shape_constants().items():
        arrays[f"const_{name}"] = value
        const[name] = nc.dram_tensor(f"const_{name}", value.shape, F32, kind="ExternalInput").ap()
    out = nc.dram_tensor("out", (T, D), F32, kind="ExternalOutput").ap()
    build(nc, a, const, out)
    result = run_bass_kernel_spmd(nc, [arrays], core_ids=[0])
    return result.results[0]["out"].reshape(1, T, D)
```
